# Optimizing a Trainium2 kernel written in Bass

```python
import math
import jax, jax.numpy as jnp
from jax import lax
import numpy as np

D_MODEL = 1024
BATCH = 1
SEQ = 512
DEPTH = 2

N_EVEN = (DEPTH + 1) // 2
N_ODD = DEPTH // 2
EPS = 1e-6
NEG_INF = -1e30

A_GROUPS = 4
A_GROUP_DIM = 128
A_CHUNK = 128
A_WIDTH = A_GROUPS * A_GROUP_DIM

B_HEADS = 8
B_KV_HEADS = 2
B_HEAD_DIM = 64
B_WIDTH = B_HEADS * B_HEAD_DIM
B_KV_WIDTH = B_KV_HEADS * B_HEAD_DIM
CMP_BLOCK = 32
CMP_STRIDE = 16
CMP_HIDDEN = 128
SLC_BLOCK = 64
SLC_TOPK = 16
WINDOW = 512
Q_BLOCK = 128
N_BRANCH = 3

MIX_WIDTH = A_WIDTH + B_WIDTH
EVEN_IN = 2 * A_WIDTH + B_WIDTH + 6 * B_KV_WIDTH + N_BRANCH * B_HEADS
EVEN_SPLITS = [int(c) for c in np.cumsum([A_WIDTH, A_WIDTH, B_WIDTH] + [B_KV_WIDTH] * 6)]

C_HEADS = 8
C_HEAD_DIM = 128
C_WIDTH = C_HEADS * C_HEAD_DIM
C_CHUNK = 64
ODD_IN = 4 * C_WIDTH

P_HEADS = 8
P_QDIM = 256
P_NKEYS = 128
P_TOPK = 16
P_EXPERTS = P_NKEYS * P_NKEYS
P_TOK_BLOCK = 128

kernel_name = "hybrid_gmlp_nsa_hgrn2_peer"

def rmsnorm(x, w):
    xf = x.astype(jnp.float32)
    y = xf * lax.rsqrt(jnp.mean(xf * xf, axis=-1, keepdims=True) + EPS)
    return (y * w.astype(jnp.float32)).astype(x.dtype)

def layernorm(x, w):
    xf = x.astype(jnp.float32)
    mu = jnp.mean(xf, axis=-1, keepdims=True)
    var = jnp.mean(jnp.square(xf - mu), axis=-1, keepdims=True)
    return ((xf - mu) * lax.rsqrt(var + EPS) * w.astype(jnp.float32)).astype(x.dtype)

def alibi_slopes(n_heads):
    return (2.0 ** (-8.0 * np.arange(1, n_heads + 1) / n_heads)).astype(np.float32)

def masked_softmax(scores, bias, valid):
    s = jnp.where(valid, scores.astype(jnp.float32) + bias, NEG_INF)
    m = jnp.max(s, axis=-1, keepdims=True)
    e = jnp.where(valid, jnp.exp(s - m), 0.0)
    return e / jnp.maximum(jnp.sum(e, axis=-1, keepdims=True), 1e-30)

def chunked_gmlp(u, v, ln_w, w_s, b_s):
    B_, S_, _ = u.shape
    nc = S_ // A_CHUNK
    vc = v.reshape(B_, nc, A_CHUNK, A_GROUPS, A_GROUP_DIM)
    vc = layernorm(vc, ln_w.reshape(A_GROUPS, A_GROUP_DIM))
    causal = jnp.tril(jnp.ones((A_CHUNK, A_CHUNK), dtype=bool))
    ws = jnp.where(causal[None], w_s, 0.0).astype(v.dtype)
    mixed = jnp.einsum('gts,bnsgd->bntgd', ws, vc) + b_s.T.astype(v.dtype)[:, :, None]
    return u * mixed.reshape(B_, S_, A_WIDTH)

def compress(kv, idx, pos, w1, w2):
    B_, _, G, Dh = kv.shape
    blk = kv[:, idx] + pos[:, None, :].astype(kv.dtype)
    blk = blk.transpose(0, 1, 3, 2, 4).reshape(B_, idx.shape[0], G, CMP_BLOCK * Dh)
    return jax.nn.gelu(blk @ w1) @ w2

def nsa(q, k_c, v_c, k_s, v_s, k_w, v_w, gates, cmp_pos, ck_w1, ck_w2, cv_w1, cv_w2):
    B_, S_ = q.shape[0], q.shape[1]
    G, R, Dh = B_KV_HEADS, B_HEADS // B_KV_HEADS, B_HEAD_DIM
    dt = q.dtype
    scale = Dh ** -0.5
    slopes = jnp.asarray(alibi_slopes(B_HEADS)).reshape(G, R)[:, :, None, None]

    n_cmp = (S_ - CMP_BLOCK) // CMP_STRIDE + 1
    cmp_idx = np.arange(n_cmp)[:, None] * CMP_STRIDE + np.arange(CMP_BLOCK)[None, :]
    k_cmp = compress(k_c, cmp_idx, cmp_pos, ck_w1, ck_w2)
    v_cmp = compress(v_c, cmp_idx, cmp_pos, cv_w1, cv_w2)
    cmp_end = jnp.asarray(cmp_idx[:, -1].astype(np.int32))

    n_slc = S_ // SLC_BLOCK
    topk = min(SLC_TOPK, n_slc)
    ci = np.arange(n_cmp)[:, None] * CMP_STRIDE
    sj = np.arange(n_slc)[None, :] * SLC_BLOCK
    overlap = jnp.asarray(((ci < sj + SLC_BLOCK) & (ci + CMP_BLOCK > sj)).astype(np.float32))
    ks_blocks = k_s.transpose(0, 2, 1, 3).reshape(B_, G, n_slc, SLC_BLOCK, Dh)
    vs_blocks = v_s.transpose(0, 2, 1, 3).reshape(B_, G, n_slc, SLC_BLOCK, Dh)
    bi = jnp.arange(B_)[:, None, None, None]
    gi = jnp.arange(G)[None, :, None, None]
    j_blk = jnp.arange(n_slc)

    k_w_pad = jnp.pad(k_w, ((0, 0), (WINDOW, 0), (0, 0), (0, 0)))
    v_w_pad = jnp.pad(v_w, ((0, 0), (WINDOW, 0), (0, 0), (0, 0)))
    gate = jax.nn.sigmoid(gates.astype(jnp.float32)).astype(dt)

    def one_block(qb):
        t0 = qb * Q_BLOCK
        t = t0 + jnp.arange(Q_BLOCK)
        qg = lax.dynamic_slice_in_dim(q, t0, Q_BLOCK, 1).reshape(B_, Q_BLOCK, G, R, Dh) * scale

        sc = jnp.einsum('btgrd,bngd->bgrtn', qg, k_cmp)
        dist_c = t[:, None] - cmp_end[None, :]
        p_cmp = masked_softmax(sc, -slopes * dist_c, dist_c >= 0)
        o_cmp = jnp.einsum('bgrtn,bngd->btgrd', p_cmp.astype(dt), v_cmp)

        imp = jnp.einsum('bgrtn,nj->bgtj', p_cmp, overlap)
        jcur = t // SLC_BLOCK
        forced = (j_blk[None, :] == 0) | (j_blk[None, :] == jcur[:, None]) | (j_blk[None, :] == jcur[:, None] - 1)
        causal_blk = j_blk[None, :] * SLC_BLOCK <= t[:, None]
        imp = jnp.where(forced, 1e9, jnp.where(causal_blk, imp, NEG_INF))
        _, sel = lax.top_k(imp, topk)
        ks = ks_blocks[bi, gi, sel].reshape(B_, G, Q_BLOCK, topk * SLC_BLOCK, Dh)
        vs = vs_blocks[bi, gi, sel].reshape(B_, G, Q_BLOCK, topk * SLC_BLOCK, Dh)
        kpos = (sel[..., None] * SLC_BLOCK + jnp.arange(SLC_BLOCK)).reshape(B_, G, Q_BLOCK, topk * SLC_BLOCK)
        dist_s = (t[None, None, :, None] - kpos)[:, :, None]
        ss = jnp.einsum('btgrd,bgtkd->bgrtk', qg, ks)
        p_s = masked_softmax(ss, -slopes * dist_s, dist_s >= 0)
        o_slc = jnp.einsum('bgrtk,bgtkd->btgrd', p_s.astype(dt), vs)

        kw = lax.dynamic_slice_in_dim(k_w_pad, t0, Q_BLOCK + WINDOW, 1)
        vw = lax.dynamic_slice_in_dim(v_w_pad, t0, Q_BLOCK + WINDOW, 1)
        kpos_w = t0 - WINDOW + jnp.arange(Q_BLOCK + WINDOW)
        dist_w = t[:, None] - kpos_w[None, :]
        valid_w = (dist_w >= 0) & (dist_w < WINDOW) & (kpos_w[None, :] >= 0)
        sw = jnp.einsum('btgrd,blgd->bgrtl', qg, kw)
        p_w = masked_softmax(sw, -slopes * dist_w, valid_w)
        o_win = jnp.einsum('bgrtl,blgd->btgrd', p_w.astype(dt), vw)

        gb = lax.dynamic_slice_in_dim(gate, t0, Q_BLOCK, 1).reshape(B_, Q_BLOCK, G, R, N_BRANCH)
        o = gb[..., 0:1] * o_cmp + gb[..., 1:2] * o_slc + gb[..., 2:3] * o_win
        return o.reshape(B_, Q_BLOCK, B_WIDTH)

    out = lax.map(one_block, jnp.arange(S_ // Q_BLOCK))
    return out.transpose(1, 0, 2, 3).reshape(B_, S_, B_WIDTH)

def even_mixer(h, w_in, a_ln_w, a_ws, a_bs, cmp_pos, ck_w1, ck_w2, cv_w1, cv_w2, w_out):
    B_, S_, _ = h.shape
    u, v, q, kc, vc, ks, vs, kw, vw, gt = jnp.split(h @ w_in, EVEN_SPLITS, axis=-1)
    a = chunked_gmlp(jax.nn.gelu(u), jax.nn.gelu(v), a_ln_w, a_ws, a_bs)
    kvh = lambda z: z.reshape(B_, S_, B_KV_HEADS, B_HEAD_DIM)
    b = nsa(q.reshape(B_, S_, B_HEADS, B_HEAD_DIM), kvh(kc), kvh(vc), kvh(ks), kvh(vs), kvh(kw), kvh(vw),
            gt.reshape(B_, S_, B_HEADS, N_BRANCH), cmp_pos, ck_w1, ck_w2, cv_w1, cv_w2)
    return jnp.concatenate([a, b], axis=-1) @ w_out

def hgrn2_recurrence(q, f_logits, i, lb):
    B_, S_, _ = q.shape
    nc = S_ // C_CHUNK
    fg = lb + (1.0 - lb) * jax.nn.sigmoid(f_logits.astype(jnp.float32))
    log_f = jnp.log(fg)
    k = 1.0 - fg

    def to_chunks(z):
        return z.astype(jnp.float32).reshape(B_, nc, C_CHUNK, C_HEADS, C_HEAD_DIM).transpose(1, 0, 3, 2, 4)

    causal = jnp.tril(jnp.ones((C_CHUNK, C_CHUNK), dtype=bool))[:, :, None]

    def step(state, inp):
        qc, kc, vc, gc = inp
        b = jnp.cumsum(gc, axis=2)
        o_inter = jnp.einsum('bhtk,bhkv->bhtv', qc * jnp.exp(b), state)
        diff = b[:, :, :, None, :] - b[:, :, None, :, :]
        decay = jnp.exp(jnp.where(causal, diff, NEG_INF))
        attn = jnp.einsum('bhtk,bhsk,bhtsk->bhts', qc, kc, decay)
        o_intra = jnp.einsum('bhts,bhsv->bhtv', attn, vc)
        b_last = b[:, :, -1:, :]
        state = jnp.exp(b_last[:, :, 0, :])[..., None] * state + \
            jnp.einsum('bhsk,bhsv->bhkv', kc * jnp.exp(b_last - b), vc)
        return state, o_inter + o_intra

    s0 = jnp.zeros((B_, C_HEADS, C_HEAD_DIM, C_HEAD_DIM), jnp.float32)
    _, o = lax.scan(step, s0, (to_chunks(q), to_chunks(k), to_chunks(i), to_chunks(log_f)))
    return o.transpose(1, 0, 3, 2, 4).reshape(B_, S_, C_HEADS, C_HEAD_DIM).astype(q.dtype)

def odd_mixer(h, w_in, lb, norm_w, w_out):
    B_, S_, _ = h.shape
    q, f, i, g = jnp.split(h @ w_in, 4, axis=-1)
    o = hgrn2_recurrence(jax.nn.silu(q), f, i, lb)
    o = rmsnorm(o, norm_w.reshape(C_HEADS, C_HEAD_DIM)) * jax.nn.silu(g).reshape(B_, S_, C_HEADS, C_HEAD_DIM)
    return o.reshape(B_, S_, C_WIDTH) @ w_out

def peer(x, w_q, sub_keys, u_tab, v_tab):
    B_, S_, D = x.shape
    xt = x.reshape(-1, P_TOK_BLOCK, D)

    def block(xb):
        qh = (xb @ w_q).reshape(P_TOK_BLOCK, P_HEADS, 2, P_QDIM // 2)
        s = jnp.einsum('thpd,hpnd->thpn', qh, sub_keys).astype(jnp.float32)
        s_top, i_top = lax.top_k(s, P_TOPK)
        cand = (s_top[:, :, 0, :, None] + s_top[:, :, 1, None, :]).reshape(P_TOK_BLOCK, P_HEADS, P_TOPK * P_TOPK)
        cand_idx = (i_top[:, :, 0, :, None] * P_NKEYS + i_top[:, :, 1, None, :]).reshape(P_TOK_BLOCK, P_HEADS, P_TOPK * P_TOPK)
        best, pos = lax.top_k(cand, P_TOPK)
        experts = jnp.take_along_axis(cand_idx, pos, axis=-1)
        gate = jax.nn.softmax(best, axis=-1).astype(xb.dtype)
        u = u_tab[experts]
        v = v_tab[experts]
        act = jax.nn.gelu(jnp.einsum('td,thkd->thk', xb, u))
        return jnp.einsum('thk,thkd->td', gate * act, v)

    return lax.map(block, xt).reshape(B_, S_, D)

def setup_inputs(seed: int = 0) -> dict:
    key = jax.random.key(seed)
    ks = jax.random.split(key, 24)
    nrm = lambda k, shape, sc: jax.random.normal(k, shape, jnp.float32) * sc
    gain = lambda k, shape: 1.0 + 0.02 * jax.random.normal(k, shape, jnp.float32)
    return {
        "x": nrm(ks[0], (BATCH, SEQ, D_MODEL), 1.0),
        "norm_mix": gain(ks[1], (DEPTH, D_MODEL)),
        "norm_ffn": gain(ks[2], (DEPTH, D_MODEL)),
        "final_norm": gain(ks[3], (D_MODEL,)),
        "even_w_in": nrm(ks[4], (N_EVEN, D_MODEL, EVEN_IN), D_MODEL ** -0.5),
        "gmlp_ln_w": gain(ks[5], (N_EVEN, A_WIDTH)),
        "gmlp_w_s": nrm(ks[6], (N_EVEN, A_GROUPS, A_CHUNK, A_CHUNK), A_CHUNK ** -0.5),
        "gmlp_b_s": gain(ks[7], (N_EVEN, A_GROUPS, A_CHUNK)),
        "nsa_cmp_pos": nrm(ks[8], (N_EVEN, CMP_BLOCK, B_HEAD_DIM), 0.1),
        "nsa_ck_w1": nrm(ks[9], (N_EVEN, CMP_BLOCK * B_HEAD_DIM, CMP_HIDDEN), (CMP_BLOCK * B_HEAD_DIM) ** -0.5),
        "nsa_ck_w2": nrm(ks[10], (N_EVEN, CMP_HIDDEN, B_HEAD_DIM), CMP_HIDDEN ** -0.5),
        "nsa_cv_w1": nrm(ks[11], (N_EVEN, CMP_BLOCK * B_HEAD_DIM, CMP_HIDDEN), (CMP_BLOCK * B_HEAD_DIM) ** -0.5),
        "nsa_cv_w2": nrm(ks[12], (N_EVEN, CMP_HIDDEN, B_HEAD_DIM), CMP_HIDDEN ** -0.5),
        "even_w_out": nrm(ks[13], (N_EVEN, MIX_WIDTH, D_MODEL), MIX_WIDTH ** -0.5),
        "odd_w_in": nrm(ks[14], (N_ODD, D_MODEL, ODD_IN), D_MODEL ** -0.5),
        "hgrn_lower_bounds": nrm(ks[15], (DEPTH, C_WIDTH), 0.1),
        "hgrn_norm_w": gain(ks[16], (N_ODD, C_WIDTH)),
        "odd_w_out": nrm(ks[17], (N_ODD, C_WIDTH, D_MODEL), C_WIDTH ** -0.5),
        "peer_w_q": nrm(ks[18], (DEPTH, D_MODEL, P_HEADS * P_QDIM), D_MODEL ** -0.5),
        "peer_keys": nrm(ks[19], (DEPTH, P_HEADS, 2, P_NKEYS, P_QDIM // 2), (P_QDIM // 2) ** -0.5),
        "peer_u": nrm(ks[20], (DEPTH, P_EXPERTS, D_MODEL), D_MODEL ** -0.5),
        "peer_v": nrm(ks[21], (DEPTH, P_EXPERTS, D_MODEL), P_HEADS ** -0.5),
    }

def reference(x, norm_mix, norm_ffn, final_norm, even_w_in, gmlp_ln_w, gmlp_w_s, gmlp_b_s,
              nsa_cmp_pos, nsa_ck_w1, nsa_ck_w2, nsa_cv_w1, nsa_cv_w2, even_w_out,
              odd_w_in, hgrn_lower_bounds, hgrn_norm_w, odd_w_out,
              peer_w_q, peer_keys, peer_u, peer_v):
    p_lb = jax.nn.softmax(hgrn_lower_bounds.astype(jnp.float32), axis=0)
    lbs = jnp.cumsum(p_lb, axis=0) - p_lb[0:1]
    for layer in range(DEPTH):
        h = rmsnorm(x, norm_mix[layer])
        if layer % 2 == 0:
            e = layer // 2
            x = x + even_mixer(h, even_w_in[e], gmlp_ln_w[e], gmlp_w_s[e], gmlp_b_s[e],
                               nsa_cmp_pos[e], nsa_ck_w1[e], nsa_ck_w2[e], nsa_cv_w1[e], nsa_cv_w2[e],
                               even_w_out[e])
        else:
            o = layer // 2
            x = x + odd_mixer(h, odd_w_in[o], lbs[layer], hgrn_norm_w[o], odd_w_out[o])
        x = x + peer(rmsnorm(x, norm_ffn[layer]), peer_w_q[layer], peer_keys[layer], peer_u[layer], peer_v[layer])
    return rmsnorm(x, final_norm)


_drawn_inputs = setup_inputs


def setup_inputs(seed=0):
    import zlib

    import numpy as np

    out = dict(_drawn_inputs(seed))
    spreads = {}
    factors = {'final_norm': 3.001, 'gmlp_ln_w': 2.728, 'hgrn_lower_bounds': 4.699, 'hgrn_norm_w': 3.397}
    for name, (base, spread) in spreads.items():
        noise = np.random.default_rng([zlib.crc32(name.encode()), seed]).standard_normal(out[name].shape)
        drawn = base * np.exp(spread * noise) if base else spread * noise
        out[name] = __import__('jax').numpy.asarray(drawn.astype(out[name].dtype))
    for name, factor in factors.items():
        out[name] = (out[name] * factor).astype(out[name].dtype)
    return out
```

```python
import concourse.bass as bass
from concourse import mybir
from contextlib import ExitStack

D_MODEL = 1024
SEQ = 512
DEPTH = 2
P = 128
TB = SEQ // P
KC = D_MODEL // P
EPS = 1e-6
NEG = -1e30
A_GROUPS = 4
B_HEADS = 8
HD = 64
CMP_BLOCK = 32
CMP_STRIDE = 16
N_CMP = (SEQ - CMP_BLOCK) // CMP_STRIDE + 1
W_EVEN = 2328
TM_UV = 1024
TM_ALL = 1304
C_HEADS = 8
LEVELS = 7
P_HEADS = 8
TOPK = 16
NKEYS = 128
ROW = 2 * D_MODEL
NBUF = 8
GRP = 4


class Event:

    def __init__(self, sem, prime=2):
        self.sem, self.prime = sem, prime

    def at(self, n):
        return n + self.prime + 1


class Chain:

    def __init__(self, eng, sem):
        self.eng, self.sem, self.n = eng, sem, 0

    def __call__(self, ins):
        self.n += 1
        ins.then_inc(self.sem, 1)
        self.eng.wait_ge(self.sem, self.n)

    def reset(self):
        self.eng.sem_clear(self.sem)
        self.n = 0


def build(nc, x, wcol_mix, w_ffn, w_fin, w_even, ln_w, ws_t, b_s, pos, ck1, ck2, cv1, cv2, w_out_e,
          w_odd, lbs, hg_w, w_out_o, w_q, keys, uv, out):
    fp32 = mybir.dt.float32
    u32 = mybir.dt.uint32
    i32 = mybir.dt.int32
    ALU = mybir.AluOpType
    ACT = mybir.ActivationFunctionType
    AXX = mybir.AxisListType.X
    ds = bass.ds

    with ExitStack() as ctx:
        def sb(name, shape, dt=fp32):
            return ctx.enter_context(nc.sbuf_tensor(name, shape, dt))

        def sem(name):
            return ctx.enter_context(nc.semaphore(name))

        events = []

        def event(name, prime=2):
            e = Event(sem(name), prime)
            events.append(e)
            return e

        RA = sb("region_a", [P, KC * W_EVEN])
        RG = sb("region_g", [P, NBUF * ROW])
        RH = sb("region_h", [P, KC * SEQ])
        RC = sb("region_c", [P, 5632])
        X = sb("x_res", [P, TB + 1, D_MODEL])
        ident_z = sb("ident_z", [P, 2 * P])
        ident = ident_z[:, 0:P]
        alibi = sb("alibi", [P, SEQ])
        level_mask = sb("level_mask", [P, LEVELS + 1, P], i32)
        iota16 = sb("iota16", [P, TOPK])
        scan_keep = alibi
        half = sb("half", [P, 8])
        wcol = sb("wcol", [P, DEPTH, KC])
        stat = sb("stat", [P, 8])
        rstd = sb("rstd", [P, 8])
        PS = ctx.enter_context(nc.psum_tensor("ps", [P, 8, 512], fp32))

        def carve(region, at, *shape):
            n = 1
            for s in shape:
                n *= s
            v = region[:, at:at + n]
            if len(shape) == 2:
                v = v.rearrange("p (a b) -> p a b", a=shape[0])
            if len(shape) == 3:
                v = v.rearrange("p (a b c) -> p a b c", a=shape[0], b=shape[1])
            return v

        def taker(region, start=0):
            at = [start]

            def take(*shape):
                n = 1
                for s in shape:
                    n *= s
                v = carve(region, at[0], *shape)
                at[0] += n
                assert at[0] <= region.shape[1], (at[0], region.shape)
                return v
            return take

        hT = carve(RH, 0, KC, SEQ)

        We = carve(RA, 0, KC, W_EVEN)
        tg = taker(RG)
        w_out_sb = tg(KC, D_MODEL)
        mixT = tg(KC, SEQ)
        qT = tg(4, SEQ)
        kcd = tg(2, SEQ)
        vcd = tg(2, SEQ)
        tc = taker(RC)
        xnS = tc(2, D_MODEL)
        kT = tc(2, SEQ)
        vsw = tc(TB, 2, P)
        gates = tc(TB, 24)
        gu = tc(SEQ)
        gv = tc(SEQ)
        kvc = X[:, TB, :].rearrange("p (a b) -> p a b", a=2)
        alibi_c = tc(TB, N_CMP)
        valid_c = tc(TB, N_CMP)
        bs_sb = sb("bs_sb", [P, A_GROUPS])
        mean = sb("mean", [P, 4])
        w2s = sb("w2s", [P, 2, HD])
        pos_sb = sb("pos_sb", [P, CMP_BLOCK // 2])
        posb = sb("posb", [P, 2])
        hid = sb("hid", [P, 2, 2 * N_CMP])
        kcmp = sb("kcmp", [P, N_CMP])
        vcmp = sb("vcmp", [N_CMP, 2 * HD])
        slope = sb("slope", [P, 2])
        gst = sb("gst", [P, TB, 2, 3])
        zc = sb("zc", [P, 2, N_CMP])
        pc = sb("pc", [P, 2, N_CMP])
        nmax = sb("nmax", [P, 2, 3])
        sums = sb("sums", [P, 2, 3])
        coef = sb("coef", [P, 3])
        pcT = sb("pcT", [N_CMP, 2, P])
        ws_sb = carve(RG, 8192 + 4 * SEQ, 4, P)
        lnw = carve(RG, 8192 + 5 * SEQ, SEQ)
        gsq = carve(RG, 8192 + 6 * SEQ, SEQ)
        gvn = carve(RG, 8192 + 7 * SEQ, SEQ)
        w1 = carve(RH, 0, 2, CMP_BLOCK // 2 * P)
        zs = carve(RH, 0, 2, 2 * SEQ)
        ps_ = carve(RH, 4 * SEQ, 2, 2 * SEQ)
        pTs = carve(RC, 0, 2, 2 * SEQ)
        qst = gu
        ot = gv

        slab = carve(RG, 0, 2, KC * 512)
        wo_odd = carve(RG, 0, KC, D_MODEL)
        og = taker(RG, 8192 + KC * SEQ)
        qs, kk, bb, fg, gs, iS, sigm, ob = (og(SEQ) for _ in range(8))
        oc2 = taker(RC)
        dE = oc2(2, SEQ)
        qE = oc2(2, SEQ)
        kE = oc2(2, SEQ)
        attn = oc2(SEQ)
        kdT = oc2(SEQ)
        qd = oc2(SEQ)
        kd = oc2(SEQ)
        eb = oc2(SEQ)
        Sst = sb("state", [P, TB - 1, P])
        hgw = X[:, TB, :]
        lb = sb("lb", [P, 2, 8])
        lbst = sb("lbst", [P, 2, 2])
        lbraw = sb("lbraw", [P, 2, 8])

        wq = carve(RA, 0, KC, 2 * D_MODEL)
        keysT = carve(RA, KC * 2 * D_MODEL, 2 * P_HEADS, NKEYS)
        gath = carve(RG, 0, NBUF, ROW)
        th = taker(RH)
        XN = th(D_MODEL)
        XN2 = th(D_MODEL)
        hTb = th(KC, P)
        wrow = th(D_MODEL)
        tp = taker(RC)
        diag = tp(NBUF, P)
        q_sb = tp(2, P)
        qT_sb = tp(2, P)
        s1 = tp(2, P)
        s2 = tp(2, P)
        cand = tp(2 * P)
        cand2 = tp(2 * P)
        oneh = tp(2, TOPK, TOPK)
        vtop = tp(2, TOPK)
        itop = tp(2, TOPK).bitcast(u32)
        itopf = tp(2, TOPK)
        best = tp(TOPK)
        bpos = tp(TOPK).bitcast(u32)
        bij = tp(2, TOPK).bitcast(u32)
        bijf = tp(2, TOPK)
        esel = tp(2, TOPK)
        experts = sb("experts", [P, 2 * TOPK], u32)
        gexp = tp(TOPK)
        gate = sb("gate", [P, 2, TOPK])
        gstat = sb("gstat", [P, 4])
        dots = tp(2 * TOPK)
        gact = tp(2 * TOPK)
        wts = tp(2 * TOPK)
        rsb = sb("rsb", [P, 1])
        wfin = wrow

        primed = sem("primed")
        consts = sem("consts")
        pool_chain, dve_chain, act_chain = sem("pool_chain"), sem("dve_chain"), sem("act_chain")
        half_set = sem("half_set")
        x_in, we_in, small_in, w1_in, wout_in = (sem(n) for n in ("x_in", "we_in", "small_in", "w1_in", "wout_in"))
        dup_in = sem("dup_in")
        wq_in, ffn_in, lb_in = sem("wq_in"), sem("ffn_in"), sem("lb_in")
        slab_in = [sem("slab_in0"), sem("slab_in1")]
        fin_in, stored = sem("fin_in"), [sem("stored0"), sem("stored1")]
        ss_ready, rs_ready = event("ss_ready"), event("rs_ready")
        xn_ready, xT_done, hT_ready = event("xn_ready"), event("xT_done"), event("hT_ready")
        fm_done, fm_out = event("fm_done"), event("fm_out")
        tm_done, uv_out, vsw_out = event("tm_done"), event("uv_out"), event("vsw_out")
        ln_ss, ln_rs, ln_done = event("ln_ss"), event("ln_rs"), event("ln_done")
        mix_done, a_ready, aT_done, aT_out = event("mix_done"), event("a_ready"), event("aT_done"), event("aT_out")
        posb_done, posb_out, hid_done, hid_out, cmp_done, cmp_out = (
            event(n) for n in ("posb_done", "posb_out", "hid_done", "hid_out", "cmp_done", "cmp_out"))
        q_staged, gate_sig = event("q_staged"), event("gate_sig")
        sc_done, z_ready, ec_ready, pc_ready, p_ready, pT_done, pT_out, pv_done, o_ready = (
            event(n) for n in ("sc_done", "z_ready", "ec_ready", "pc_ready", "p_ready", "pT_done", "pT_out",
                               "pv_done", "o_ready"))
        oT_done, oT_out = event("oT_done"), event("oT_out")
        wo_done, wo_out = event("wo_done"), event("wo_out")
        pr_done = event("pr_done")
        sig_ready, fg_ready, lf_ready, dd_ready, e_ready, qe_ready, ke_ready, lv_out = (
            event(n) for n in ("sig_ready", "fg_ready", "lf_ready", "dd_ready", "e_ready", "qe_ready",
                               "ke_ready", "lv_out"))
        lv_done = event("lv_done", 4)
        og_final = event("og_final")
        i_out, kds_ready, ebe_ready, kd_ready, kdT_done, kdT_out, kv_done, s_ready, oi_done, osq_ready = (
            event(n) for n in ("i_out", "kds_ready", "ebe_ready", "kd_ready", "kdT_done", "kdT_out", "kv_done",
                               "s_ready", "oi_done", "osq_ready"))
        oss_ready, ors_ready, og_ready, ogT_done, ogT_out = (
            event(n) for n in ("oss_ready", "ors_ready", "og_ready", "ogT_done", "ogT_out"))
        qk_ready = event("qk_ready")
        pxn_ready, pxT_done, pxT_out = event("pxn_ready"), event("pxT_done"), event("pxT_out")
        rq_done, rq_out, rqT_done, rqT_out, rs_done, rs_out = (
            event(n) for n in ("rq_done", "rq_out", "rqT_done", "rqT_out", "rs_done", "rs_out"))
        routed, gexp_in, gexp_out = event("routed"), event("gexp_in"), event("gexp_out")
        dots_ready, gelu_ready, w_ready, diag_ready = (
            event(n) for n in ("dots_ready", "gelu_ready", "w_ready", "diag_ready"))
        slot_done = event("slot_done", NBUF)
        acc_done, acc_out = event("acc_done"), event("acc_out")
        gathered = [sem(f"gathered{i}") for i in range(NBUF)]

        block = ctx.enter_context(nc.Block())

        def after(eng, ev, n):
            v = ev.at(n)
            if isinstance(v, int):
                eng.wait_ge(ev.sem, v)
            else:
                r = eng.to_reg(v)
                eng.wait_ge(primed, 1)
                eng.wait_ge(ev.sem, r)

        def reached(eng, s, v):
            if isinstance(v, int):
                eng.wait_ge(s, v)
            else:
                r = eng.to_reg(v)
                eng.wait_ge(primed, 1)
                eng.wait_ge(s, r)

        def bc(ap, n):
            shape = list(ap.shape)
            return ap.unsqueeze(len(shape)).broadcast_to(shape + [n])

        def bmid(ap, n):
            return ap.unsqueeze(1).broadcast_to([ap.shape[0], n, ap.shape[1]])

        def v3(ap, a):
            return ap.rearrange("p (a b) -> p a b", a=a)

        UNITS = 8

        def unit(i):
            return i // 2, i % 2

        LAYER_SLOTS = TB * P_HEADS * TOPK
        LAYER_UNITS = TB * P_HEADS

        @block.sync
        def _(sp):
            for e in events:
                sp.sem_inc(e.sem, e.prime)
            sp.sem_inc(primed, 1)
            sp.dma_start(X[:, 0:TB, :], x.rearrange("(b p) d -> p b d", p=P)).then_inc(x_in, 16)
            sp.dma_start(wcol[:], wcol_mix).then_inc(small_in, 16)
            sp.dma_start(bs_sb[:], b_s).then_inc(small_in, 16)
            sp.dma_start(lnw, ln_w.partition_broadcast(P)).then_inc(small_in, 16)
            sp.dma_start(ws_sb, ws_t).then_inc(small_in, 16)
            sp.dma_start(pos_sb[:], pos).then_inc(small_in, 16)
            sp.dma_start(w2s[:, 0, :], ck2).then_inc(small_in, 16)
            sp.dma_start(w2s[:, 1, :], cv2).then_inc(small_in, 16)
            sp.dma_start(lbraw[:], lbs).then_inc(small_in, 16)
            sp.dma_start(We[:, :, TM_ALL:W_EVEN], w_even[:, :, TM_ALL:W_EVEN]).then_inc(we_in, 16)
            sp.dma_start(We[:, :, 0:TM_ALL], w_even[:, :, 0:TM_ALL]).then_inc(we_in, 16)
            sp.dma_start(w_out_sb, w_out_e).then_inc(wout_in, 16)
            after(sp, fm_out, 7)
            for kv, dst in ((0, kcd), (1, vcd)):
                for g in range(2):
                    src = kvc[g * HD:(g + 1) * HD, kv, :]
                    sp.dma_start(dst[0:HD, g, :], src).then_inc(dup_in, 16)
                    sp.dma_start(dst[HD:P, g, 0:SEQ - 1], src[:, 1:SEQ]).then_inc(dup_in, 16)
            after(sp, tm_done, TB - 1)
            sp.dma_start(w1[:, 0, :], ck1).then_inc(w1_in, 16)
            sp.dma_start(w1[:, 1, :], cv1).then_inc(w1_in, 16)
            sp.dma_start(wq, w_q[0]).then_inc(wq_in, 16)
            sp.dma_start(keysT, keys[0]).then_inc(wq_in, 16)
            after(sp, wo_out, TB - 1)
            sp.dma_start(wrow, w_ffn[0:1, :].partition_broadcast(P)).then_inc(ffn_in, 16)
            after(sp, acc_out, TB - 1)
            sp.dma_start(hgw, hg_w.partition_broadcast(P)).then_inc(lb_in, 16)
            sp.dma_start(slab[:, 0, :], w_odd[0]).then_inc(slab_in[0], 16)
            sp.dma_start(slab[:, 1, :], w_odd[1]).then_inc(slab_in[1], 16)
            sp.dma_start(wq, w_q[1]).then_inc(wq_in, 16)
            sp.dma_start(keysT, keys[1]).then_inc(wq_in, 16)
            with sp.Fori(0, C_HEADS // 2 - 1) as hp:
                for e in range(2):
                    after(sp, pr_done, hp * 2 + e)
                    sp.dma_start(slab[:, e, :], w_odd[ds(hp * 2 + (e + 2), 1)].rearrange("o p n -> (o p) n")
                                 ).then_inc(slab_in[e], 16)
            after(sp, pr_done, C_HEADS - 1)
            sp.dma_start(wo_odd, w_out_o).then_inc(wout_in, 16)
            after(sp, wo_out, 2 * TB - 1)
            sp.dma_start(wrow, w_ffn[1:2, :].partition_broadcast(P)).then_inc(ffn_in, 16)
            after(sp, acc_out, 2 * TB - 1)
            sp.dma_start(wfin, w_fin.partition_broadcast(P)).then_inc(fin_in, 16)
            for b in range(TB):
                after(sp, og_final, b)
                sp.dma_start(out[b * P:(b + 1) * P, :], XN if b % 2 == 0 else XN2).then_inc(stored[b % 2], 16)
            for s in stored:
                sp.wait_ge(s, 16 * TB // 2)

        @block.gpsimd
        def _(pool):
            g = nc.gpsimd
            link = Chain(pool, pool_chain)
            pool.wait_ge(primed, 1)
            link(g.memset(half[:], -0.5))
            link(g.memset(ident_z[:], 0.0))
            link(g.affine_select(out=ident, in_=ident, compare_op=ALU.not_equal, fill=1.0, base=0,
                                 pattern=[[-1, P]], channel_multiplier=1))
            pool.sem_inc(half_set, 1)
            link(g.iota(alibi[:], [[1, SEQ]], base=-(SEQ - P), channel_multiplier=-1,
                        allow_small_or_imprecise_dtypes=True))
            link(g.affine_select(out=alibi[:], in_=alibi[:], compare_op=ALU.is_ge, fill=NEG, base=SEQ - P,
                                 pattern=[[-1, SEQ]], channel_multiplier=1))
            link(g.iota(alibi_c, [[-P, TB], [CMP_STRIDE, N_CMP]], base=CMP_BLOCK - 1, channel_multiplier=-1,
                        allow_small_or_imprecise_dtypes=True))
            link(g.affine_select(out=alibi_c, in_=alibi_c, compare_op=ALU.is_ge, fill=NEG,
                                 base=-(CMP_BLOCK - 1), pattern=[[P, TB], [-CMP_STRIDE, N_CMP]],
                                 channel_multiplier=1))
            link(g.memset(valid_c, 1.0))
            link(g.affine_select(out=valid_c, in_=valid_c, compare_op=ALU.is_ge, fill=0.0,
                                 base=-(CMP_BLOCK - 1), pattern=[[P, TB], [-CMP_STRIDE, N_CMP]],
                                 channel_multiplier=1))
            link(g.iota(iota16[:], [[1, TOPK]], base=0, channel_multiplier=0,
                        allow_small_or_imprecise_dtypes=True))
            link(g.memset(level_mask[:], 1))
            for lev in range(LEVELS):
                n = 1 << lev
                m = level_mask[:, lev, :].rearrange("p (b h l) -> p b h l", h=2, l=n)
                link(g.affine_select(out=m, in_=m, compare_op=ALU.is_ge, fill=0.0, base=0,
                                     pattern=[[-2 * n, P // (2 * n)], [0, 2], [0, n]], channel_multiplier=1))
                link(g.affine_select(out=m, in_=m, compare_op=ALU.is_ge, fill=0.0, base=n - 1,
                                     pattern=[[2 * n, P // (2 * n)], [0, 2], [0, n]], channel_multiplier=-1))
                link(g.memset(m[:, :, 0, :], 0))
            d = level_mask[:, LEVELS, :]
            link(g.affine_select(out=d, in_=d, compare_op=ALU.is_equal, fill=0.0, base=0,
                                 pattern=[[-1, P]], channel_multiplier=1))
            pool.wait_ge(small_in, 16 * 8)
            link(g.affine_select(out=ws_sb, in_=ws_sb, compare_op=ALU.is_ge, fill=0.0, base=0,
                                 pattern=[[0, A_GROUPS], [1, P]], channel_multiplier=-1))
            pool.sem_inc(consts, 1)

            def inverse_root(src, dst, n, count):
                link(g.tensor_scalar(dst, src, 1.0 / count, EPS, ALU.mult, ALU.add))
                link(g.tensor_tensor(dst, dst, half[:, 0:n], ALU.pow))

            after(pool, ss_ready, 0)
            inverse_root(stat[:, 0:TB], rstd[:, 0:TB], TB, D_MODEL)
            pool.sem_inc(rs_ready.sem, 1)
            for tb in range(TB):
                after(pool, ln_ss, tb)
                inverse_root(mean[:], rstd[:, 4:8], 4, P)
                pool.sem_inc(ln_rs.sem, 1)

            def peer(layer):
                after(pool, ss_ready, 1 + 2 * layer)
                inverse_root(stat[:, 0:TB], rstd[:, 0:TB], TB, D_MODEL)
                pool.sem_inc(rs_ready.sem, 1)
                tab = uv[layer]
                with pool.Fori(0, LAYER_UNITS // 2) as up:
                    for e in range(2):
                        after(pool, routed, up * 2 + (e + layer * (LAYER_UNITS + 1)))
                        for k in range(TOPK):
                            after(pool, slot_done, up * (2 * TOPK) + (e * TOPK + k - NBUF + layer * LAYER_SLOTS))
                            g.indirect_dma_start(
                                out=gath[:, k % NBUF, :], out_offset=None, in_=tab,
                                in_offset=bass.IndirectOffsetOnAxis(
                                    ap=experts[:, e * TOPK + k:e * TOPK + k + 1], axis=0),
                            ).then_inc(gathered[k % NBUF], 16)

            peer(0)

            after(pool, ss_ready, 2)
            inverse_root(stat[:, 0:TB], rstd[:, 0:TB], TB, D_MODEL)
            pool.sem_inc(rs_ready.sem, 1)
            link.reset()
            with pool.Fori(0, C_HEADS) as h:
                for lev in range(LEVELS):
                    n = 1 << lev
                    after(pool, e_ready, h * LEVELS + lev)
                    after(pool, lv_done, h * (LEVELS + 1) + (-2, -3)[lev] if lev < 2 else h * (LEVELS + 1) + (lev - 2))
                    left = "p (b h l) -> p b h l"
                    o_ = kE[:, lev % 2, :].rearrange(left, h=2, l=n)[:, :, 0, :]
                    k_ = kk.rearrange(left, h=2, l=n)[:, :, 0, :]
                    e_ = dE[:, lev % 2, :].rearrange(left, h=2, l=n)[:, :, 0, :]
                    g.tensor_tensor(o_, k_, e_, ALU.mult).then_inc(ke_ready.sem, 1)
                after(pool, oss_ready, h)
                inverse_root(mean[:], rstd[:, 4:8], 4, P)
                pool.sem_inc(ors_ready.sem, 1)
                link.reset()

            peer(1)
            after(pool, ss_ready, 4)
            inverse_root(stat[:, 0:TB], rstd[:, 0:TB], TB, D_MODEL)
            pool.sem_inc(rs_ready.sem, 1)

        @block.scalar
        def _(act):
            a = nc.scalar
            link = Chain(act, act_chain)
            act.wait_ge(primed, 1)
            act.wait_ge(small_in, 16 * 8)
            for ch in range(8):
                after(act, fm_done, ch)
                dst = qT[:, ch, :] if ch < 4 else (kvc[:, ch - 4, :] if ch < 6 else kT[:, ch - 6, :])
                a.activation(dst, PS[:, 6 + ch % 2, :], ACT.Copy).then_inc(fm_out.sem, 1)
            for tb in range(TB):
                after(act, tm_done, tb)
                after(act, a_ready, tb - 1)
                a.activation(gu, PS[:, 3 * (tb % 2), :], ACT.Gelu_apprx_tanh)
                a.activation(gv, PS[:, 3 * (tb % 2) + 1, :], ACT.Gelu_apprx_tanh).then_inc(uv_out.sem, 1)
                a.activation(vsw[:, tb, :, :], PS[:, 3 * (tb % 2) + 2, 0:256].rearrange("p (a b) -> p a b", a=2),
                             ACT.Copy)
                a.activation(gates[:, tb, :], PS[:, 3 * (tb % 2) + 2, 256:280], ACT.Copy).then_inc(vsw_out.sem, 1)
                after(act, aT_done, tb)
                a.activation(mixT[:, 0:4, tb * P:(tb + 1) * P], v3(PS[:, 7, :], 4), ACT.Copy).then_inc(aT_out.sem, 1)
            after(act, vsw_out, TB - 1)
            link(a.activation(gates.rearrange("p a b -> p (a b)"), gates.rearrange("p a b -> p (a b)"), ACT.Sigmoid))
            act.sem_inc(gate_sig.sem, 1)
            after(act, posb_done, 0)
            link(a.activation(posb[:], PS[:, 0, 0:2], ACT.Copy))
            after(act, hid_done, 0)
            for kv in range(2):
                i = a.activation(hid[:, kv, :], PS[:, 1, kv * 64:kv * 64 + 2 * N_CMP], ACT.Gelu_apprx_tanh,
                                 bias=posb[:, kv:kv + 1])
            i.then_inc(hid_out.sem, 1)
            after(act, cmp_done, 0)
            a.activation(kcmp[:], PS[:, 2, 0:N_CMP], ACT.Copy)
            a.activation(vcmp[:], PS[0:N_CMP, 3, 0:2 * HD], ACT.Copy).then_inc(cmp_out.sem, 1)
            with act.Fori(0, 4) as c:
                after(act, sc_done, c * UNITS - 1)
                i = a.activation(qst, qT[:, ds(c, 1), :].rearrange("p a b -> p (a b)"), ACT.Copy)
                i.then_inc(q_staged.sem, 1)

                def exps(i):
                    qb, e = unit(i)
                    par, nk = i % 2, (qb + 1) * P
                    after(act, z_ready, c * UNITS + i)
                    after(act, pT_done, c * UNITS + (i - 2))
                    a.activation(pc[:, par, :], zc[:, par, :], ACT.Exp, bias=nmax[:, par, 2:3],
                                 scale=0.125).then_inc(ec_ready.sem, 1)
                    for br in range(2):
                        last = a.activation(ps_[:, par, br * SEQ:br * SEQ + nk], zs[:, par, br * SEQ:br * SEQ + nk],
                                            ACT.Exp, bias=nmax[:, par, br:br + 1], scale=0.125,
                                            accum_out=sums[:, par, br:br + 1])
                    last.then_inc(p_ready.sem, 1)

                exps(0)
                for i in range(UNITS):
                    qb, e = unit(i)
                    par, nk = i % 2, (qb + 1) * P
                    after(act, pT_done, c * UNITS + i)
                    after(act, pv_done, c * UNITS + (i - 2))
                    a.activation(pcT[:, par, :], PS[0:N_CMP, 6 + par, 256:384], ACT.Copy)
                    a.activation(pTs[:, par, :].rearrange("p (a b) -> p a b", a=2)[:, :, 0:nk], PS[:, 4:6, 0:nk],
                                 ACT.Copy).then_inc(pT_out.sem, 1)
                    if i + 1 < UNITS:
                        exps(i + 1)
                after(act, oT_done, c)
                a.activation(mixT[:, ds(c + 4, 1), :].rearrange("p a b -> p (a b)"), PS[:, 4, :],
                             ACT.Copy).then_inc(oT_out.sem, 1)

            def peer(layer):
                U0, R0, S0, B0 = layer * LAYER_UNITS, layer * (LAYER_UNITS + 1), layer * LAYER_SLOTS, layer * (TB + 1)
                G0 = S0 // GRP

                def route(r):
                    after(act, rq_done, r)
                    a.activation(q_sb, v3(PS[:, 4, 0:256], 2), ACT.Copy).then_inc(rq_out.sem, 1)
                    after(act, rqT_done, r)
                    a.activation(qT_sb, v3(PS[:, 5, 0:256], 2), ACT.Copy).then_inc(rqT_out.sem, 1)

                def soft(r):
                    after(act, gexp_in, r)
                    a.activation(gexp, best, ACT.Exp, bias=gstat[:, 0:1],
                                 accum_out=gstat[:, 1:2]).then_inc(gexp_out.sem, 1)

                def diags(e, grp_index, slot_index, grp):
                    after(act, w_ready, grp_index)
                    for k in range(grp * GRP, grp * GRP + GRP):
                        after(act, slot_done, slot_index + (k - NBUF))
                        a.activation(diag[:, k % NBUF, :], ident, ACT.Copy,
                                     scale=wts[:, e * TOPK + k:e * TOPK + k + 1]).then_inc(diag_ready.sem, 1)

                after(act, pxT_done, B0)
                for j in range(2):
                    i = a.activation(hTb[:, 4 * j:4 * j + 4, :], v3(PS[:, 2 + j, :], 4), ACT.Copy)
                i.then_inc(pxT_out.sem, 1)
                route(R0)
                soft(R0)

                def pair(b, u, last):
                    for e in range(2):
                        if last and e == 1:
                            after(act, pxT_done, b + (B0 + 1))
                            after(act, rq_done, u + (R0 + 1))
                            for j in range(2):
                                i = a.activation(hTb[:, 4 * j:4 * j + 4, :], v3(PS[:, 2 + j, :], 4), ACT.Copy)
                            i.then_inc(pxT_out.sem, 1)
                        route(u + (e + 1 + R0))
                        for grp in range(TOPK // GRP):
                            gi = u * (TOPK // GRP) + (e * (TOPK // GRP) + grp + G0)
                            after(act, dots_ready, gi)
                            q0 = e * TOPK + grp * GRP
                            a.activation(gact[:, q0:q0 + GRP], dots[:, q0:q0 + GRP], ACT.Gelu_apprx_tanh
                                         ).then_inc(gelu_ready.sem, 1)
                            diags(e, gi, u * TOPK + (e * TOPK + S0), grp)
                        soft(u + (e + 1 + R0))

                with act.Fori(0, TB) as b:
                    with act.Fori(0, P_HEADS // 2 - 1) as hp:
                        pair(b, b * P_HEADS + hp * 2, False)
                    pair(b, b * P_HEADS + (P_HEADS - 2), True)

            peer(0)

            link.reset()
            link(a.activation(lb[:, 0, :], lb[:, 1, :], ACT.Sigmoid))
            act.sem_inc(lf_ready.sem, 1)
            with act.Fori(0, C_HEADS // 2) as hp:
                for e in range(2):
                    h = hp * 2 + e
                    after(act, pr_done, h)
                    after(act, og_ready, h - 1)
                    a.activation(sigm, PS[:, 1, :], ACT.Sigmoid)
                    a.activation(dE[:, 0, :], PS[:, 0, :], ACT.Sigmoid)
                    gi = PS[:, 2:4, :].rearrange("p a (b c) -> p (a b) c", b=2)
                    a.activation(v3(iS, 4), gi[:, :, 0:P], ACT.Copy).then_inc(i_out.sem, 1)
                    a.activation(v3(dE[:, 1, :], 4), gi[:, :, P:2 * P], ACT.Sigmoid).then_inc(sig_ready.sem, 1)
                    after(act, fg_ready, h)
                    a.activation(bb, fg, ACT.Ln).then_inc(lf_ready.sem, 1)
                    for lev in range(LEVELS):
                        after(act, dd_ready, h * LEVELS + lev)
                        a.activation(dE[:, lev % 2, :], dE[:, lev % 2, :], ACT.Exp).then_inc(e_ready.sem, 1)
                    after(act, kds_ready, h)
                    a.activation(eb, bb, ACT.Exp)
                    a.activation(kd, kd, ACT.Exp).then_inc(ebe_ready.sem, 1)
                    after(act, kdT_done, h)
                    a.activation(kdT, PS[:, 0, :], ACT.Copy).then_inc(kdT_out.sem, 1)
                    after(act, oi_done, h)
                    a.activation(v3(sigm, 4), v3(PS[:, 6, :], 4), ACT.Square).then_inc(osq_ready.sem, 1)
                    after(act, ogT_done, h)
                    a.activation(mixT[:, ds(h, 1), :].rearrange("p a b -> p (a b)"), PS[:, 7, :],
                                 ACT.Copy).then_inc(ogT_out.sem, 1)

            peer(1)

        @block.vector
        def _(dve):
            v = nc.vector
            link = Chain(dve, dve_chain)
            dve.wait_ge(primed, 1)
            dve.wait_ge(small_in, 16 * 8)
            link(v.memset(slope[:, 0:1], 4.0))
            link(v.memset(slope[:, 1:2], 0.25))
            link(v.tensor_tensor(lb[:, 1, :], lbraw[:, 1, :], lbraw[:, 0, :], ALU.subtract))
            dve.wait_ge(x_in, 16)

            def squares(n):
                for tb in range(TB):
                    link(v.tensor_tensor_reduce(out=xnS[:, tb % 2, :], in0=X[:, tb, :], in1=X[:, tb, :], scale=1.0,
                                                scalar=0.0, op0=ALU.mult, op1=ALU.add, accum_out=stat[:, tb:tb + 1]))
                dve.sem_inc(ss_ready.sem, 1)

            def normed_transposed(layer):
                dve.wait_ge(half_set, 1)
                for tb in range(TB):
                    n = layer * TB + tb
                    after(dve, xT_done, n - 2)
                    v.tensor_scalar(xnS[:, tb % 2, :], X[:, tb, :], rstd[:, tb:tb + 1], None, ALU.mult
                                    ).then_inc(xn_ready.sem, 1)
                    after(dve, xT_done, n)
                    v.tensor_tensor(hT[:, :, tb * P:(tb + 1) * P],
                                    PS[:, 0:2, :].rearrange("p a (b c) -> p (a b) c", b=4),
                                    bc(wcol[:, layer, :], P), ALU.mult).then_inc(hT_ready.sem, 1)

            squares(0)
            after(dve, rs_ready, 0)
            normed_transposed(0)
            dve.wait_ge(consts, 1)
            for tb in range(TB):
                after(dve, uv_out, tb)
                after(dve, mix_done, tb - 1)
                link(v.tensor_reduce(mean[:], v3(gv, 4), AXX, ALU.add))
                link(v.tensor_scalar(mean[:], mean[:], 1.0 / P, None, ALU.mult))
                link(v.tensor_tensor(v3(gvn, 4), v3(gv, 4), bc(mean[:], P), ALU.subtract))
                link(v.tensor_tensor(gsq, gvn, gvn, ALU.mult))
                link(v.tensor_reduce(mean[:], v3(gsq, 4), AXX, ALU.add))
                dve.sem_inc(ln_ss.sem, 1)
                link(v.tensor_tensor(gvn, gvn, lnw, ALU.mult))
                after(dve, ln_rs, tb)
                v.tensor_tensor(v3(gvn, 4), v3(gvn, 4), bc(rstd[:, 4:8], P), ALU.mult).then_inc(ln_done.sem, 1)
                after(dve, mix_done, tb)
                for gr in range(A_GROUPS):
                    last = v.scalar_tensor_tensor(gsq[:, gr * P:(gr + 1) * P], PS[:, 6, gr * P:(gr + 1) * P],
                                                  bs_sb[:, gr:gr + 1], gu[:, gr * P:(gr + 1) * P], ALU.add, ALU.mult)
                last.then_inc(a_ready.sem, 1)
                after(dve, aT_done, tb)
            link.reset()
            after(dve, gate_sig, 0)
            gview = gates.rearrange("p b (e c r) -> p b e c r", e=2, c=4)
            with dve.Fori(0, 4) as c:
                for e in range(2):
                    link(v.tensor_copy(gst[:, :, e, :], gates[:, :, ds(c * 3 + 12 * e, 3)]))

                def biased(i):
                    qb, e = unit(i)
                    par, nk = i % 2, (qb + 1) * P
                    after(dve, sc_done, c * UNITS + i)
                    after(dve, p_ready, c * UNITS + (i - 2))
                    z = zs[:, par, :].rearrange("p (a b) -> p a b", a=2)[:, :, 0:nk]
                    v.scalar_tensor_tensor(zc[:, par, :], alibi_c[:, qb, :], slope[:, e:e + 1],
                                           PS[:, 6 + par, 192:192 + N_CMP], ALU.mult, ALU.add)
                    link(v.scalar_tensor_tensor(z, bmid(alibi[:, SEQ - nk:SEQ], 2), slope[:, e:e + 1],
                                                PS[:, 2 * par:2 * par + 2, 0:nk], ALU.mult, ALU.add))
                    v.tensor_reduce(nmax[:, par, 2:3], zc[:, par, :], AXX, ALU.max)
                    link(v.tensor_reduce(nmax[:, par, 0:2], z, AXX, ALU.max))
                    link(v.tensor_scalar(nmax[:, par, :], nmax[:, par, :], -0.125, None, ALU.mult))
                    dve.sem_inc(z_ready.sem, 1)

                def combine(i):
                    qb, e = unit(i)
                    par = i % 2
                    after(dve, pv_done, c * UNITS + i)
                    link(v.tensor_scalar(coef[:], sums[:, par, :], 1e-30, None, ALU.max))
                    link(v.reciprocal(coef[:], coef[:]))
                    link(v.tensor_tensor(coef[:, 0:2], coef[:, 0:2], gst[:, qb, e, 1:3], ALU.mult))
                    link(v.tensor_tensor(coef[:, 2:3], coef[:, 2:3], gst[:, qb, e, 0:1], ALU.mult))
                    o = v3(ot, 4)[:, qb, e * HD:(e + 1) * HD]
                    pv = PS[:, 6 + par, 0:192].rearrange("p (a b) -> p a b", a=3)
                    link(v.tensor_scalar(o, pv[:, 0, :], coef[:, 0:1], None, ALU.mult))
                    link(v.scalar_tensor_tensor(o, pv[:, 1, :], coef[:, 1:2], o, ALU.mult, ALU.add))
                    link(v.scalar_tensor_tensor(o, pv[:, 2, :], coef[:, 2:3], o, ALU.mult, ALU.add))
                    dve.sem_inc(o_ready.sem, 1)

                after(dve, oT_done, c - 1)
                biased(0)
                for i in range(UNITS):
                    qb, e = unit(i)
                    par = i % 2
                    after(dve, ec_ready, c * UNITS + i)
                    v.tensor_tensor_reduce(out=pc[:, par, :], in0=pc[:, par, :], in1=valid_c[:, qb, :], scale=1.0,
                                           scalar=0.0, op0=ALU.mult, op1=ALU.add, accum_out=sums[:, par, 2:3]
                                           ).then_inc(pc_ready.sem, 1)
                    if i:
                        combine(i - 1)
                    if i + 1 < UNITS:
                        biased(i + 1)
                combine(UNITS - 1)
                link(v.tensor_scalar(slope[:], slope[:], 0.5, None, ALU.mult))
                link.reset()

            def residual(layer):
                for tb in range(TB):
                    n = layer * TB + tb
                    after(dve, wo_done, n)
                    p = 2 * (tb % 2)
                    v.tensor_tensor(X[:, tb, :].rearrange("p (a b) -> p a b", a=2),
                                    X[:, tb, :].rearrange("p (a b) -> p a b", a=2), PS[:, p:p + 2, :], ALU.add
                                    ).then_inc(wo_out.sem, 1)
                after(dve, wo_out, layer * TB + TB - 1)

            residual(0)

            def peer(layer):
                U0, R0, S0, B0 = layer * LAYER_UNITS, layer * (LAYER_UNITS + 1), layer * LAYER_SLOTS, layer * (TB + 1)
                G0 = S0 // GRP
                squares(1 + 2 * layer)
                after(dve, rs_ready, 1 + 2 * layer)
                dve.wait_ge(ffn_in, 16 * (layer + 1))
                link.reset()

                def prologue(b):
                    link(v.tensor_copy(rsb[:], rstd[:, ds(b, 1)]))
                    link(v.scalar_tensor_tensor(XN2, X[:, ds(b, 1), :].rearrange("p a d -> p (a d)"), rsb[:], wrow,
                                                ALU.mult, ALU.mult))
                    dve.sem_inc(pxn_ready.sem, 1)

                def top16(vals, idx, src, spare):
                    link(v.max(vals[:, 0:8], src))
                    link(v.max_index(idx[:, 0:8], vals[:, 0:8], src))
                    link(v.match_replace(spare, vals[:, 0:8], src, -3e38))
                    link(v.max(vals[:, 8:16], spare))
                    link(v.max_index(idx[:, 8:16], vals[:, 8:16], spare))

                def scores_in(r):
                    after(dve, rs_done, r)
                    link(v.tensor_copy(s1, v3(PS[:, 6, 0:256], 2)))
                    dve.sem_inc(rs_out.sem, 1)
                    top16(vtop[:, 0, :], itop[:, 0, :], s1[:, 0, :], s2[:, 0, :])

                def second_half():
                    top16(vtop[:, 1, :], itop[:, 1, :], s1[:, 1, :], s2[:, 1, :])
                    link(v.tensor_copy(itopf, itop))

                def candidates(r):
                    link(v.tensor_tensor(v3(cand, TOPK), bc(vtop[:, 0, :], TOPK), bmid(vtop[:, 1, :], TOPK), ALU.add))
                    top16(best, bpos, cand, cand2)
                    link(v.tensor_scalar(gstat[:, 0:1], best[:, 0:1], -1.0, None, ALU.mult))
                    dve.sem_inc(gexp_in.sem, 1)

                def chosen(e):
                    link(v.tensor_scalar(bij[:, 0, :], bpos, 4, None, ALU.logical_shift_right))
                    link(v.tensor_scalar(bij[:, 1, :], bpos, 15, None, ALU.bitwise_and))
                    link(v.tensor_copy(bijf, bij))
                    for p in range(2):
                        oh = oneh[:, p, :, :]
                        link(v.tensor_tensor(oh, bc(bijf[:, p, :], TOPK), bmid(iota16[:], TOPK), ALU.is_equal))
                        link(v.tensor_tensor(oh, oh, bmid(itopf[:, p, :], TOPK), ALU.mult))
                        link(v.tensor_reduce(esel[:, p, :], oh, AXX, ALU.add))
                    link(v.scalar_tensor_tensor(experts[:, e * TOPK:(e + 1) * TOPK], esel[:, 0, :], float(NKEYS),
                                                esel[:, 1, :], ALU.mult, ALU.add))

                def gates_of(e, r):
                    after(dve, gexp_out, r)
                    link(v.reciprocal(gstat[:, 2:3], gstat[:, 1:2]))
                    link(v.tensor_scalar(gate[:, e, :], gexp, gstat[:, 2:3], None, ALU.mult))
                    dve.sem_inc(routed.sem, 1)

                link(v.tensor_copy(rsb[:], rstd[:, 0:1]))
                link(v.scalar_tensor_tensor(XN2, X[:, 0, :], rsb[:], wrow, ALU.mult, ALU.mult))
                dve.sem_inc(pxn_ready.sem, 1)
                scores_in(R0)
                second_half()
                candidates(R0)
                chosen(0)
                gates_of(0, R0)
                link.reset()

                def pair(b, u, last):
                    for e in range(2):
                        r = u + (e + 1 + R0)
                        if last and e == 1:
                            prologue(b + 1)
                        for grp in range(TOPK // GRP):
                            gi = u * (TOPK // GRP) + (e * (TOPK // GRP) + grp + G0)
                            for k in range(grp * GRP, grp * GRP + GRP):
                                buf = k % NBUF
                                rounds = TOPK // NBUF
                                reached(dve, gathered[buf],
                                        u * (16 * rounds) + 16 * (rounds * (U0 + e) + k // NBUF + 1))
                                q = e * TOPK + k
                                i = v.tensor_tensor_reduce(out=gath[:, buf, 0:D_MODEL], in0=gath[:, buf, 0:D_MODEL],
                                                           in1=XN, scale=1.0, scalar=0.0, op0=ALU.mult, op1=ALU.add,
                                                           accum_out=dots[:, q:q + 1])
                            link(i)
                            dve.sem_inc(dots_ready.sem, 1)
                            after(dve, gelu_ready, gi)
                            q0 = e * TOPK + grp * GRP
                            v.tensor_tensor(wts[:, q0:q0 + GRP], gact[:, q0:q0 + GRP],
                                            gate[:, e, grp * GRP:grp * GRP + GRP], ALU.mult).then_inc(w_ready.sem, 1)
                            if grp == 0:
                                scores_in(r)
                            if grp == 1:
                                second_half()
                            if grp == 2:
                                candidates(r)
                            if grp == 3:
                                chosen(1 - e)
                                gates_of(1 - e, r)
                        link.reset()

                with dve.Fori(0, TB) as b:
                    link(v.tensor_copy(XN, XN2))
                    link.reset()
                    with dve.Fori(0, P_HEADS // 2 - 1) as hp:
                        pair(b, b * P_HEADS + hp * 2, False)
                    pair(b, b * P_HEADS + (P_HEADS - 2), True)
                    after(dve, acc_done, b + layer * TB)
                    xb = X[:, ds(b, 1), :].rearrange("p a (c d) -> p (a c) d", c=2)
                    link(v.tensor_tensor(xb, xb, PS[:, 0:2, :], ALU.add))
                    dve.sem_inc(acc_out.sem, 1)
                    link.reset()

            peer(0)

            squares(2)
            after(dve, rs_ready, 2)
            normed_transposed(1)
            link(v.memset(scan_keep[:], 1.0))
            link(v.memset(v3(scan_keep[:], TB)[:, :, 0:1], 0.0))
            link(v.memset(attn, 0.0))
            link(v.memset(qE, 0.0))
            link(v.memset(kE, 0.0))
            after(dve, lf_ready, 0)
            dve.wait_ge(lb_in, 16)
            link(v.tensor_scalar(lb[:, 1, :], lb[:, 0, :], -1.0, 1.0, ALU.mult, ALU.add))
            link.reset()
            with dve.Fori(0, C_HEADS // 2) as hp:
                for e in range(2):
                    h = hp * 2 + e
                    for j in range(2):
                        link(v.tensor_copy(lbst[:, j, 0:1], lb[:, j, ds(h, 1)]))
                    after(dve, sig_ready, h)
                    link(v.tensor_scalar(fg, sigm, lbst[:, 1, 0:1], lbst[:, 0, 0:1], ALU.mult, ALU.add))
                    link(v.tensor_scalar(kk, fg, -1.0, 1.0, ALU.mult, ALU.add))
                    link(v.tensor_scalar(fg, fg, 2.0 ** -63, None, ALU.max))
                    dve.sem_inc(fg_ready.sem, 1)
                    link(v.tensor_tensor(qs, PS[:, 0, :], dE[:, 0, :], ALU.mult))
                    gi = PS[:, 2:4, :].rearrange("p a (b c) -> p (a b) c", b=2)
                    link(v.tensor_tensor(v3(gs, 4), gi[:, :, P:2 * P], v3(dE[:, 1, :], 4), ALU.mult))
                    link(v.tensor_tensor(v3(gs, 4), v3(gs, 4), bmid(hgw[:, ds(h * P, P)], 4), ALU.mult))
                    dve.sem_inc(qk_ready.sem, 1)
                    after(dve, lf_ready, h + 1)
                    link(v.tensor_tensor_scan(bb, scan_keep[:], bb, 0.0, ALU.mult, ALU.add))
                    halves = "p (b h l) -> p b h l"

                    def distance(lev):
                        n = 1 << lev
                        b_ = bb.rearrange(halves, h=2, l=n)
                        d_ = dE[:, lev % 2, :].rearrange(halves, h=2, l=n)
                        ref = b_[:, :, 0, n - 1:n].broadcast_to([P, SEQ // (2 * n), n])
                        if lev >= 2:
                            after(dve, ke_ready, h * LEVELS + (lev - 2))
                            after(dve, qe_ready, h * LEVELS + (lev - 2))
                        link(v.tensor_tensor(d_[:, :, 0, :], ref, b_[:, :, 0, :], ALU.subtract))
                        v.tensor_tensor(d_[:, :, 1, :], b_[:, :, 1, :], ref, ALU.subtract).then_inc(dd_ready.sem, 1)

                    def evacuate(lev):
                        after(dve, lv_done, h * (LEVELS + 1) + lev)
                        link(v.copy_predicated(v3(attn, 4), bmid(level_mask[:, lev, :], 4),
                                               v3(PS[:, 4 + lev % 2, :], 4)))
                        dve.sem_inc(lv_out.sem, 1)

                    distance(0)
                    for lev in range(LEVELS):
                        n = 1 << lev
                        if lev + 1 < LEVELS:
                            distance(lev + 1)
                        after(dve, e_ready, h * LEVELS + lev)
                        if lev >= 2:
                            after(dve, lv_done, h * (LEVELS + 1) + (lev - 2))
                        v.tensor_tensor(qE[:, lev % 2, :].rearrange(halves, h=2, l=n)[:, :, 1, :],
                                        qs.rearrange(halves, h=2, l=n)[:, :, 1, :],
                                        dE[:, lev % 2, :].rearrange(halves, h=2, l=n)[:, :, 1, :], ALU.mult
                                        ).then_inc(qe_ready.sem, 1)
                        if lev:
                            evacuate(lev - 1)
                    link(v.tensor_tensor(v3(kd, 4), bc(v3(bb, 4)[:, :, P - 1], P), v3(bb, 4), ALU.subtract))
                    dve.sem_inc(kds_ready.sem, 1)
                    evacuate(LEVELS - 1)
                    evacuate(LEVELS)
                    after(dve, ebe_ready, h)
                    link(v.tensor_tensor(kd, kk, kd, ALU.mult))
                    link(v.tensor_tensor(qd, qs, eb, ALU.mult))
                    dve.sem_inc(kd_ready.sem, 1)
                    after(dve, kv_done, h)
                    link(v.tensor_copy(Sst[:, 0, :], PS[:, 1, 0:P]))
                    for b in (1, 2):
                        link(v.scalar_tensor_tensor(Sst[:, b, :], Sst[:, b - 1, :], v3(eb, 4)[:, b, P - 1:P],
                                                    PS[:, 1, b * P:(b + 1) * P], ALU.mult, ALU.add))
                    dve.sem_inc(s_ready.sem, 1)
                    after(dve, osq_ready, h)
                    link(v.tensor_reduce(mean[:], v3(sigm, 4), AXX, ALU.add))
                    dve.sem_inc(oss_ready.sem, 1)
                    link(v.tensor_tensor(v3(ob, 4), v3(PS[:, 6, :], 4), v3(gs, 4), ALU.mult))
                    after(dve, ors_ready, h)
                    v.tensor_tensor(v3(ob, 4), v3(ob, 4), bc(rstd[:, 4:8], P), ALU.mult).then_inc(og_ready.sem, 1)
                    after(dve, ogT_done, h)
                    link.reset()
            residual(1)
            peer(1)
            squares(4)
            after(dve, rs_ready, 4)
            dve.wait_ge(fin_in, 16)
            for b in range(TB):
                dst = XN if b % 2 == 0 else XN2
                if b >= 2:
                    dve.wait_ge(stored[b % 2], 16)
                v.scalar_tensor_tensor(dst, X[:, b, :], rstd[:, b:b + 1], wfin, ALU.mult, ALU.mult
                                       ).then_inc(og_final.sem, 1)

        @block.tensor
        def _(pe):
            t = nc.tensor
            pe.wait_ge(primed, 1)

            def transposes(layer):
                for tb in range(TB):
                    n = layer * TB + tb
                    after(pe, xn_ready, n)
                    after(pe, hT_ready, n - 1)
                    for c in range(KC):
                        i = t.transpose(PS[:, c // 4, (c % 4) * P:(c % 4 + 1) * P], xnS[:, tb % 2, c * P:(c + 1) * P],
                                        ident)
                    i.then_inc(xT_done.sem, 1)

            pe.wait_ge(half_set, 1)
            transposes(0)
            after(pe, hT_ready, TB - 1)
            pe.wait_ge(we_in, 32)
            for ch in range(8):
                after(pe, fm_out, ch - 2)
                for c in range(KC):
                    i = t.matmul(PS[:, 6 + ch % 2, :], We[:, c, TM_ALL + ch * P:TM_ALL + (ch + 1) * P], hT[:, c, :],
                                 start=c == 0, stop=c == KC - 1)
                i.then_inc(fm_done.sem, 1)
            pe.wait_ge(consts, 1)

            def token_major(tb):
                after(pe, uv_out, tb - 2)
                after(pe, vsw_out, tb - 2)
                p = 3 * (tb % 2)
                for j, (c0, c1) in enumerate(((0, 512), (512, 1024), (1024, TM_ALL))):
                    for c in range(KC):
                        i = t.matmul(PS[:, p + j, 0:c1 - c0], hT[:, c, tb * P:(tb + 1) * P], We[:, c, c0:c1],
                                     start=c == 0, stop=c == KC - 1)
                i.then_inc(tm_done.sem, 1)

            after(pe, fm_out, 7)
            token_major(0)
            for tb in range(TB):
                if tb + 1 < TB:
                    token_major(tb + 1)
                after(pe, ln_done, tb)
                after(pe, a_ready, tb - 1)
                for gr in range(A_GROUPS):
                    i = t.matmul(PS[:, 6, gr * P:(gr + 1) * P], ws_sb[:, gr, :], gvn[:, gr * P:(gr + 1) * P],
                                 start=True, stop=True)
                i.then_inc(mix_done.sem, 1)
                after(pe, a_ready, tb)
                after(pe, aT_out, tb - 1)
                for gr in range(A_GROUPS):
                    i = t.transpose(PS[:, 7, gr * P:(gr + 1) * P], gsq[:, gr * P:(gr + 1) * P], ident)
                i.then_inc(aT_done.sem, 1)
            pe.wait_ge(w1_in, 32)
            pe.wait_ge(dup_in, 16 * 8)
            after(pe, uv_out, TB - 1)
            after(pe, vsw_out, TB - 1)
            J = CMP_BLOCK // 2
            for kv in range(2):
                for j in range(J):
                    i = t.matmul(PS[:, 0, kv:kv + 1], w1[:, kv, j * P:(j + 1) * P], pos_sb[:, j:j + 1],
                                 start=j == 0, stop=j == J - 1)
            i.then_inc(posb_done.sem, 1)
            for kv, src in ((0, kcd), (1, vcd)):
                for j in range(J):
                    sv = src[:, :, 2 * j:2 * j + CMP_STRIDE * (N_CMP - 1) + 1:CMP_STRIDE]
                    i = t.matmul(PS[:, 1, kv * 64:kv * 64 + 2 * N_CMP].rearrange("p (a b) -> p a b", a=2),
                                 w1[:, kv, j * P:(j + 1) * P], sv, start=j == 0, stop=j == J - 1)
            i.then_inc(hid_done.sem, 1)
            after(pe, hid_out, 0)
            for g_ in range(2):
                t.matmul(PS[g_ * HD:(g_ + 1) * HD, 2, 0:N_CMP], w2s[:, 0, :], hid[:, 0, g_ * N_CMP:(g_ + 1) * N_CMP],
                         start=True, stop=True)
                i = t.matmul(PS[0:N_CMP, 3, g_ * HD:(g_ + 1) * HD], hid[:, 1, g_ * N_CMP:(g_ + 1) * N_CMP],
                             w2s[:, 1, :], start=True, stop=True)
            i.then_inc(cmp_done.sem, 1)
            after(pe, cmp_out, 0)
            after(pe, aT_out, TB - 1)
            with pe.Fori(0, 4) as c:
                after(pe, q_staged, c)

                def scores(i):
                    qb, e = unit(i)
                    par, nk = i % 2, (qb + 1) * P
                    after(pe, z_ready, c * UNITS + (i - 2))
                    after(pe, o_ready, c * UNITS + (i - 2))
                    r = slice(e * HD, (e + 1) * HD)
                    for br in range(2):
                        t.matmul(PS[:, 2 * par + br, 0:nk], qst[r, qb * P:(qb + 1) * P], kT[r, br, 0:nk],
                                 start=True, stop=True)
                    t.matmul(PS[:, 6 + par, 192:192 + N_CMP], qst[r, qb * P:(qb + 1) * P], kcmp[r, :],
                             start=True, stop=True).then_inc(sc_done.sem, 1)

                after(pe, oT_out, c - 1)
                scores(0)
                for i in range(UNITS):
                    qb, e = unit(i)
                    par = i % 2
                    if i + 1 < UNITS:
                        scores(i + 1)
                    after(pe, p_ready, c * UNITS + i)
                    after(pe, pc_ready, c * UNITS + i)
                    after(pe, pT_out, c * UNITS + (i - 1))
                    for br in range(2):
                        for kt in range(qb + 1):
                            t.transpose(PS[:, 4 + br, kt * P:(kt + 1) * P],
                                        ps_[:, par, br * SEQ + kt * P:br * SEQ + (kt + 1) * P], ident)
                    t.transpose(PS[0:N_CMP, 6 + par, 256:384], pc[:, par, :], ident).then_inc(pT_done.sem, 1)
                    after(pe, pT_out, c * UNITS + i)
                    for br in range(2):
                        for kt in range(qb + 1):
                            t.matmul(PS[:, 6 + par, br * HD:(br + 1) * HD],
                                     pTs[:, par, br * SEQ + kt * P:br * SEQ + (kt + 1) * P],
                                     vsw[:, kt, br, e * HD:(e + 1) * HD], start=kt == 0, stop=kt == qb)
                    t.matmul(PS[:, 6 + par, 2 * HD:3 * HD], pcT[:, par, :], vcmp[:, e * HD:(e + 1) * HD],
                             start=True, stop=True).then_inc(pv_done.sem, 1)
                after(pe, o_ready, c * UNITS + (UNITS - 1))
                for qb in range(TB):
                    i = t.transpose(PS[:, 4, qb * P:(qb + 1) * P], ot[:, qb * P:(qb + 1) * P], ident)
                i.then_inc(oT_done.sem, 1)

            def project_out(layer, w):
                pe.wait_ge(wout_in, 16 * (layer + 1))
                for tb in range(TB):
                    n = layer * TB + tb
                    after(pe, wo_out, n - 2)
                    for j in range(2):
                        for c in range(KC):
                            i = t.matmul(PS[:, 2 * (tb % 2) + j, :], mixT[:, c, tb * P:(tb + 1) * P],
                                         w[:, c, j * 512:(j + 1) * 512], start=c == 0, stop=c == KC - 1)
                    i.then_inc(wo_done.sem, 1)

            after(pe, oT_out, 3)
            project_out(0, w_out_sb)

            def peer(layer):
                U0, R0, S0, B0 = layer * LAYER_UNITS, layer * (LAYER_UNITS + 1), layer * LAYER_SLOTS, layer * (TB + 1)
                pe.wait_ge(wq_in, 32 * (layer + 1))
                after(pe, wo_out, layer * TB + TB - 1)

                def block_transposes(n):
                    after(pe, pxn_ready, n)
                    for c in range(KC):
                        i = t.transpose(PS[:, 2 + c // 4, (c % 4) * P:(c % 4 + 1) * P], XN2[:, c * P:(c + 1) * P],
                                        ident)
                    i.then_inc(pxT_done.sem, 1)
                    after(pe, pxT_out, n)

                def route(r, hcol):
                    for c in range(KC):
                        i = t.matmul(PS[:, 4, 0:256], hTb[:, c, :], wq[:, c, ds(hcol * 256, 256)],
                                     start=c == 0, stop=c == KC - 1)
                    i.then_inc(rq_done.sem, 1)
                    after(pe, rq_out, r)
                    for p in range(2):
                        i = t.transpose(PS[:, 5, p * P:(p + 1) * P], q_sb[:, p, :], ident)
                    i.then_inc(rqT_done.sem, 1)
                    after(pe, rqT_out, r)
                    after(pe, rs_out, r - 1)
                    for p in range(2):
                        i = t.matmul(PS[:, 6, p * P:(p + 1) * P], qT_sb[:, p, :],
                                     keysT[:, ds(hcol * 2 + p, 1), :].rearrange("p a b -> p (a b)"),
                                     start=True, stop=True)
                    i.then_inc(rs_done.sem, 1)

                def zero_products(start, stop):
                    for j in range(2):
                        i = t.matmul(PS[:, j, :], ident_z[0:1, P:2 * P], alibi[0:1, :], start=start, stop=stop)
                    return i

                def pair(b, u, hcol, last):
                    for e in range(2):
                        if last and e == 1:
                            block_transposes(b + (B0 + 1))
                            route(u + (e + 1 + R0), 0)
                        else:
                            route(u + (e + 1 + R0), hcol + (e + 1))
                        for k in range(TOPK):
                            after(pe, diag_ready, u * TOPK + (e * TOPK + k + S0))
                            for j in range(2):
                                i = t.matmul(PS[:, j, :], diag[:, k % NBUF, :],
                                             gath[:, k % NBUF, D_MODEL + j * 512:D_MODEL + (j + 1) * 512],
                                             start=False, stop=False)
                            i.then_inc(slot_done.sem, 1)

                block_transposes(B0)
                route(R0, 0)
                with pe.Fori(0, TB) as b:
                    after(pe, acc_out, b + (layer * TB - 1))
                    zero_products(True, False)
                    with pe.Fori(0, P_HEADS // 2 - 1) as hp:
                        pair(b, b * P_HEADS + hp * 2, hp * 2, False)
                    pair(b, b * P_HEADS + (P_HEADS - 2), P_HEADS - 2, True)
                    zero_products(False, True).then_inc(acc_done.sem, 1)

            peer(0)

            after(pe, acc_out, TB - 1)
            transposes(1)
            after(pe, hT_ready, 2 * TB - 1)
            with pe.Fori(0, C_HEADS // 2) as hp:
                for e in range(2):
                    h = hp * 2 + e
                    W = slab[:, e, :].rearrange("p (c n) -> p c n", c=KC)
                    reached(pe, slab_in[e], hp * 16 + 16)
                    after(pe, s_ready, h - 1)
                    after(pe, og_ready, h - 1)
                    for j in range(2):
                        for c in range(KC):
                            t.matmul(PS[:, j, :], W[:, c, j * P:(j + 1) * P], hT[:, c, :],
                                     start=c == 0, stop=c == KC - 1)
                    for tb in range(TB):
                        for c in range(KC):
                            i = t.matmul(PS[:, 2 + tb // 2, (tb % 2) * 256:(tb % 2 + 1) * 256],
                                         hT[:, c, tb * P:(tb + 1) * P], W[:, c, 256:512],
                                         start=c == 0, stop=c == KC - 1)
                    i.then_inc(pr_done.sem, 1)
                    for lev in range(LEVELS + 1):
                        after(pe, lv_out, h * (LEVELS + 1) + (lev - 2))
                        if lev < LEVELS:
                            after(pe, qe_ready, h * LEVELS + lev)
                            after(pe, ke_ready, h * LEVELS + lev)
                            q_, k_ = qE[:, lev % 2, :], kE[:, lev % 2, :]
                        else:
                            q_, k_ = qs, kk
                        for tb in range(TB):
                            i = t.matmul(PS[:, 4 + lev % 2, tb * P:(tb + 1) * P], k_[:, tb * P:(tb + 1) * P],
                                         q_[:, tb * P:(tb + 1) * P], start=True, stop=True)
                        i.then_inc(lv_done.sem, 1)
                    after(pe, kd_ready, h)
                    for tb in range(TB):
                        i = t.transpose(PS[:, 0, tb * P:(tb + 1) * P], kd[:, tb * P:(tb + 1) * P], ident)
                    i.then_inc(kdT_done.sem, 1)
                    after(pe, kdT_out, h)
                    after(pe, i_out, h)
                    for tb in range(TB):
                        i = t.matmul(PS[:, 1, tb * P:(tb + 1) * P], kdT[:, tb * P:(tb + 1) * P],
                                     iS[:, tb * P:(tb + 1) * P], start=True, stop=True)
                    i.then_inc(kv_done.sem, 1)
                    after(pe, s_ready, h)
                    after(pe, lv_out, h * (LEVELS + 1) + LEVELS)
                    for tb in range(TB):
                        o = PS[:, 6, tb * P:(tb + 1) * P]
                        if tb:
                            t.matmul(o, qd[:, tb * P:(tb + 1) * P], Sst[:, tb - 1, :], start=True, stop=False)
                        i = t.matmul(o, attn[:, tb * P:(tb + 1) * P], iS[:, tb * P:(tb + 1) * P],
                                     start=tb == 0, stop=True)
                    i.then_inc(oi_done.sem, 1)
                    after(pe, og_ready, h)
                    after(pe, ogT_out, h - 1)
                    for tb in range(TB):
                        i = t.transpose(PS[:, 7, tb * P:(tb + 1) * P], ob[:, tb * P:(tb + 1) * P], ident)
                    i.then_inc(ogT_done.sem, 1)
            after(pe, ogT_out, C_HEADS - 1)
            project_out(1, wo_odd)
            peer(1)


def kernel(**inputs):
    import numpy as np
    import concourse.bacc as bacc
    from concourse import mybir as mb
    from concourse.bass_utils import run_bass_kernel_spmd as run

    def arr(name):
        return np.asarray(inputs[name])

    def chunks(w):
        return w.reshape(-1, 128, w.shape[-1]).transpose(1, 0, 2)

    we = arr("even_w_in")[0]
    q = we[:, 1024:1536].reshape(1024, 8, 64)
    qpairs = np.stack([q[:, 0:4], q[:, 4:8]], axis=2).reshape(1024, 512)
    kc, vc, ks, vs, kw, vw = (we[:, 1536 + 128 * i:1664 + 128 * i] for i in range(6))
    we = np.concatenate([we[:, 0:1024], vs, vw, we[:, 2304:2328], qpairs, kc, vc, ks, kw], axis=1)

    wo = arr("even_w_out")[0]
    heads = wo[512:].reshape(8, 64, 1024)
    wo = np.concatenate([wo[:512], np.stack([heads[0:4], heads[4:8]], axis=1).reshape(512, 1024)], axis=0)

    def two_positions(w):
        return w.reshape(16, 2, 64, -1).transpose(1, 2, 0, 3).reshape(128, 16, -1)

    odd = arr("odd_w_in")[0].reshape(8, 128, 4, 8, 128)
    odd = odd.transpose(3, 1, 0, 2, 4).reshape(8, 128, 4096)
    data = {
        "x": arr("x")[0],
        "wcol_mix": arr("norm_mix").reshape(2, 8, 128).transpose(2, 0, 1),
        "w_ffn": arr("norm_ffn"),
        "w_fin": arr("final_norm").reshape(1, 1024),
        "w_even": chunks(we),
        "ln_w": arr("gmlp_ln_w"),
        "ws_t": arr("gmlp_w_s")[0].transpose(2, 0, 1),
        "b_s": arr("gmlp_b_s")[0].T,
        "pos": two_positions(arr("nsa_cmp_pos")[0].reshape(2048, 1)).reshape(128, 16),
        "ck1": two_positions(arr("nsa_ck_w1")[0]).reshape(128, 2048),
        "ck2": arr("nsa_ck_w2")[0],
        "cv1": two_positions(arr("nsa_cv_w1")[0]).reshape(128, 2048),
        "cv2": arr("nsa_cv_w2")[0],
        "w_out_e": chunks(wo),
        "w_odd": odd,
        "lbs": arr("hgrn_lower_bounds").reshape(2, 8, 128).transpose(2, 0, 1),
        "hg_w": arr("hgrn_norm_w"),
        "w_out_o": chunks(arr("odd_w_out")[0]),
        "w_q": arr("peer_w_q").reshape(2, 8, 128, 2048).transpose(0, 2, 1, 3),
        "keys": arr("peer_keys").reshape(2, 16, 128, 128).transpose(0, 3, 1, 2),
    }
    for layer in range(2):
        data[f"uv{layer}"] = np.concatenate([arr("peer_u")[layer], arr("peer_v")[layer]], axis=1)

    nc = bacc.Bacc("TRN2", target_bir_lowering=False, num_devices=1)
    arrays, args = {}, {}
    for name, a in data.items():
        a = np.ascontiguousarray(a)
        arrays[f"in_{name}_dram"] = a
        args[name] = nc.dram_tensor(f"in_{name}_dram", a.shape, mb.dt.from_np(a.dtype), kind="ExternalInput").ap()
    args["out"] = nc.dram_tensor("out_0_dram", (512, 1024), mb.dt.float32, kind="ExternalOutput").ap()
    args["uv"] = [args.pop("uv0"), args.pop("uv1")]
    build(nc, **args)
    r = run(nc, [arrays], core_ids=[0])
    return r.results[0]["out_0_dram"].reshape(1, 512, 1024)
```

```python
import concourse.bass as bass
from concourse import mybir
from contextlib import ExitStack

D_MODEL = 1024
SEQ = 512
DEPTH = 2
P = 128
TB = SEQ // P
KC = D_MODEL // P
EPS = 1e-6
NEG = -1e30
A_GROUPS = 4
B_HEADS = 8
HD = 64
CMP_BLOCK = 32
CMP_STRIDE = 16
N_CMP = (SEQ - CMP_BLOCK) // CMP_STRIDE + 1
W_EVEN = 2328
TM_UV = 1024
TM_ALL = 1304
C_HEADS = 8
LEVELS = 7
P_HEADS = 8
TOPK = 16
NKEYS = 128
ROW = 2 * D_MODEL
NBUF = 8
GRP = 4


class Event:

    def __init__(self, sem, prime=2):
        self.sem, self.prime = sem, prime

    def at(self, n):
        return n + self.prime + 1


class Chain:

    def __init__(self, eng, sem):
        self.eng, self.sem, self.n = eng, sem, 0

    def __call__(self, ins):
        self.n += 1
        ins.then_inc(self.sem, 1)
        self.eng.wait_ge(self.sem, self.n)

    def reset(self):
        self.eng.sem_clear(self.sem)
        self.n = 0


def build(nc, x, wcol_mix, w_ffn, w_fin, w_even, ln_w, ws_t, b_s, pos, ck1, ck2, cv1, cv2, w_out_e,
          w_odd, lbs, hg_w, w_out_o, w_q, keys, uv, out):
    fp32 = mybir.dt.float32
    u32 = mybir.dt.uint32
    i32 = mybir.dt.int32
    ALU = mybir.AluOpType
    ACT = mybir.ActivationFunctionType
    AXX = mybir.AxisListType.X
    ds = bass.ds

    with ExitStack() as ctx:
        def sb(name, shape, dt=fp32):
            return ctx.enter_context(nc.sbuf_tensor(name, shape, dt))

        def sem(name):
            return ctx.enter_context(nc.semaphore(name))

        events = []

        def event(name, prime=2):
            e = Event(sem(name), prime)
            events.append(e)
            return e

        RA = sb("region_a", [P, KC * W_EVEN])
        RG = sb("region_g", [P, NBUF * ROW])
        RH = sb("region_h", [P, KC * SEQ])
        RC = sb("region_c", [P, 5632])
        X = sb("x_res", [P, TB + 1, D_MODEL])
        ident_z = sb("ident_z", [P, 2 * P])
        ident = ident_z[:, 0:P]
        alibi = sb("alibi", [P, SEQ])
        level_mask = sb("level_mask", [P, LEVELS + 1, P], i32)
        iota16 = sb("iota16", [P, TOPK])
        scan_keep = alibi
        half = sb("half", [P, 8])
        wcol = sb("wcol", [P, DEPTH, KC])
        stat = sb("stat", [P, 8])
        rstd = sb("rstd", [P, 8])
        PS = ctx.enter_context(nc.psum_tensor("ps", [P, 8, 512], fp32))

        def carve(region, at, *shape):
            n = 1
            for s in shape:
                n *= s
            v = region[:, at:at + n]
            if len(shape) == 2:
                v = v.rearrange("p (a b) -> p a b", a=shape[0])
            if len(shape) == 3:
                v = v.rearrange("p (a b c) -> p a b c", a=shape[0], b=shape[1])
            return v

        def taker(region, start=0):
            at = [start]

            def take(*shape):
                n = 1
                for s in shape:
                    n *= s
                v = carve(region, at[0], *shape)
                at[0] += n
                assert at[0] <= region.shape[1], (at[0], region.shape)
                return v
            return take

        hT = carve(RH, 0, KC, SEQ)

        We = carve(RA, 0, KC, W_EVEN)
        tg = taker(RG)
        w_out_sb = tg(KC, D_MODEL)
        mixT = tg(KC, SEQ)
        qT = tg(4, SEQ)
        kcd = tg(2, SEQ)
        vcd = tg(2, SEQ)
        tc = taker(RC)
        xnS = tc(2, D_MODEL)
        kT = tc(2, SEQ)
        vsw = tc(TB, 2, P)
        gates = tc(TB, 24)
        gu = tc(SEQ)
        gv = tc(SEQ)
        kvc = X[:, TB, :].rearrange("p (a b) -> p a b", a=2)
        alibi_c = tc(TB, N_CMP)
        valid_c = tc(TB, N_CMP)
        bs_sb = sb("bs_sb", [P, A_GROUPS])
        mean = sb("mean", [P, 4])
        w2s = sb("w2s", [P, 2, HD])
        pos_sb = sb("pos_sb", [P, CMP_BLOCK // 2])
        posb = sb("posb", [P, 2])
        hid = sb("hid", [P, 2, 2 * N_CMP])
        kcmp = sb("kcmp", [P, N_CMP])
        vcmp = sb("vcmp", [N_CMP, 2 * HD])
        slope = sb("slope", [P, 2])
        gst = sb("gst", [P, TB, 2, 3])
        nmax = sb("nmax", [P, 2, 2])
        sums = sb("sums", [P, 2, 2])
        coef = sb("coef", [P, 2])
        cmax = sb("cmax", [P, 2, TB])
        csum = sb("csum", [P, 2, TB])
        ws_sb = carve(RG, 8192 + 4 * SEQ, 4, P)
        lnw = carve(RG, 8192 + 5 * SEQ, SEQ)
        gsq = carve(RG, 8192 + 6 * SEQ, SEQ)
        gvn = carve(RG, 8192 + 7 * SEQ, SEQ)
        w1 = carve(RG, 0, 2, CMP_BLOCK // 2 * P)
        zs = carve(RH, 0, 2, 2 * SEQ)
        ps_ = carve(RH, 4 * SEQ, 2, 2 * SEQ)
        pTs = carve(RC, 0, 2, 2 * SEQ)
        pcT = X[0:N_CMP, TB, :].rearrange("p (a b c) -> p a b c", a=2, b=TB)
        pc = carve(RG, 8192 + KC * SEQ + 4 * SEQ, 2, TB, N_CMP)
        qst = gu
        ot = gv

        slab = carve(RG, 0, 2, KC * 512)
        wo_odd = carve(RG, 0, KC, D_MODEL)
        og = taker(RG, 8192 + KC * SEQ)
        qs, kk, bb, fg, gs, iS, sigm, ob = (og(SEQ) for _ in range(8))
        oc2 = taker(RC)
        dE = oc2(2, SEQ)
        qE = oc2(2, SEQ)
        kE = oc2(2, SEQ)
        attn = oc2(SEQ)
        kdT = oc2(SEQ)
        qd = oc2(SEQ)
        kd = oc2(SEQ)
        eb = oc2(SEQ)
        Sst = sb("state", [P, TB - 1, P])
        hgw = X[:, TB, :]
        lb = sb("lb", [P, 2, 8])
        lbst = sb("lbst", [P, 2, 2])
        lbraw = sb("lbraw", [P, 2, 8])

        wq = carve(RA, 0, KC, 2 * D_MODEL)
        keysT = carve(RA, KC * 2 * D_MODEL, 2 * P_HEADS, NKEYS)
        gath = carve(RG, 0, NBUF, ROW)
        th = taker(RH)
        XN = th(D_MODEL)
        XN2 = th(D_MODEL)
        hTb = th(KC, P)
        wrow = th(D_MODEL)
        tp = taker(RC)
        diag = tp(NBUF, P)
        q_sb = tp(2, P)
        qT_sb = tp(2, P)
        s1 = tp(2, P)
        s2 = tp(2, P)
        cand = tp(2 * P)
        cand2 = tp(2 * P)
        oneh = tp(2, TOPK, TOPK)
        vtop = tp(2, TOPK)
        itop = tp(2, TOPK).bitcast(u32)
        itopf = tp(2, TOPK)
        best = tp(TOPK)
        bpos = tp(TOPK).bitcast(u32)
        bij = tp(2, TOPK).bitcast(u32)
        bijf = tp(2, TOPK)
        esel = tp(2, TOPK)
        experts = sb("experts", [P, 2 * TOPK], u32)
        gexp = tp(TOPK)
        gate = sb("gate", [P, 2, TOPK])
        gstat = sb("gstat", [P, 4])
        dots = tp(2 * TOPK)
        gact = tp(2 * TOPK)
        wts = tp(2 * TOPK)
        rsb = sb("rsb", [P, 1])
        wfin = wrow

        primed = sem("primed")
        consts = sem("consts")
        pool_chain, dve_chain, act_chain = sem("pool_chain"), sem("dve_chain"), sem("act_chain")
        half_set = sem("half_set")
        x_in, we_in, small_in, w1_in, wout_in = (sem(n) for n in ("x_in", "we_in", "small_in", "w1_in", "wout_in"))
        dup_in = sem("dup_in")
        wq_in, ffn_in, lb_in = sem("wq_in"), sem("ffn_in"), sem("lb_in")
        slab_in = [sem("slab_in0"), sem("slab_in1")]
        fin_in, stored = sem("fin_in"), [sem("stored0"), sem("stored1")]
        ss_ready, rs_ready = event("ss_ready"), event("rs_ready")
        xn_ready, xT_done, hT_ready = event("xn_ready"), event("xT_done"), event("hT_ready")
        fm_done, fm_out = event("fm_done"), event("fm_out")
        tm_done, uv_out, vsw_out = event("tm_done"), event("uv_out"), event("vsw_out")
        ln_ss, ln_rs, ln_done = event("ln_ss"), event("ln_rs"), event("ln_done")
        mix_done, a_ready, aT_done, aT_out = event("mix_done"), event("a_ready"), event("aT_done"), event("aT_out")
        posb_done, posb_out, hid_done, hid_out, cmp_done, cmp_out = (
            event(n) for n in ("posb_done", "posb_out", "hid_done", "hid_out", "cmp_done", "cmp_out"))
        q_staged, gate_sig = event("q_staged"), event("gate_sig")
        sc_done, z_ready, ec_ready, pc_ready, p_ready, pT_done, pT_out, pv_done, o_ready = (
            event(n) for n in ("sc_done", "z_ready", "ec_ready", "pc_ready", "p_ready", "pT_done", "pT_out",
                               "pv_done", "o_ready"))
        oT_done, oT_out = event("oT_done"), event("oT_out")
        cs_done, pcT_done, pcT_out = event("cs_done"), event("pcT_done"), event("pcT_out")
        wo_done, wo_out = event("wo_done"), event("wo_out")
        pr_done = event("pr_done")
        sig_ready, fg_ready, lf_ready, dd_ready, e_ready, qe_ready, ke_ready, lv_out = (
            event(n) for n in ("sig_ready", "fg_ready", "lf_ready", "dd_ready", "e_ready", "qe_ready",
                               "ke_ready", "lv_out"))
        lv_done = event("lv_done", 4)
        og_final = event("og_final")
        i_out, kds_ready, ebe_ready, kd_ready, kdT_done, kdT_out, kv_done, s_ready, oi_done, osq_ready = (
            event(n) for n in ("i_out", "kds_ready", "ebe_ready", "kd_ready", "kdT_done", "kdT_out", "kv_done",
                               "s_ready", "oi_done", "osq_ready"))
        oss_ready, ors_ready, og_ready, ogT_done, ogT_out = (
            event(n) for n in ("oss_ready", "ors_ready", "og_ready", "ogT_done", "ogT_out"))
        qk_ready, ig_free = event("qk_ready"), event("ig_free")
        pxn_ready, pxT_done, pxT_out = event("pxn_ready"), event("pxT_done"), event("pxT_out")
        rq_done, rq_out, rqT_done, rqT_out, rs_done, rs_out = (
            event(n) for n in ("rq_done", "rq_out", "rqT_done", "rqT_out", "rs_done", "rs_out"))
        routed, gexp_in, gexp_out = event("routed"), event("gexp_in"), event("gexp_out")
        dots_ready, gelu_ready, w_ready, diag_ready = (
            event(n) for n in ("dots_ready", "gelu_ready", "w_ready", "diag_ready"))
        slot_done = event("slot_done", NBUF)
        acc_done, acc_out = event("acc_done"), event("acc_out")
        gathered = [sem(f"gathered{i}") for i in range(NBUF)]

        block = ctx.enter_context(nc.Block())

        def after(eng, ev, n):
            v = ev.at(n)
            if isinstance(v, int):
                eng.wait_ge(ev.sem, v)
            else:
                r = eng.to_reg(v)
                eng.wait_ge(primed, 1)
                eng.wait_ge(ev.sem, r)

        def reached(eng, s, v):
            if isinstance(v, int):
                eng.wait_ge(s, v)
            else:
                r = eng.to_reg(v)
                eng.wait_ge(primed, 1)
                eng.wait_ge(s, r)

        def bc(ap, n):
            shape = list(ap.shape)
            return ap.unsqueeze(len(shape)).broadcast_to(shape + [n])

        def bmid(ap, n):
            return ap.unsqueeze(1).broadcast_to([ap.shape[0], n, ap.shape[1]])

        def v3(ap, a):
            return ap.rearrange("p (a b) -> p a b", a=a)

        UNITS = 8

        def unit(i):
            return i // 2, i % 2

        OUT_BANKS = (0, 6, 0, 2)
        LAYER_SLOTS = TB * P_HEADS * TOPK
        LAYER_UNITS = TB * P_HEADS

        @block.sync
        def _(sp):
            for e in events:
                sp.sem_inc(e.sem, e.prime)
            sp.sem_inc(primed, 1)
            sp.dma_start(X[:, 0:TB, :], x.rearrange("(b p) d -> p b d", p=P)).then_inc(x_in, 16)
            sp.dma_start(wcol[:], wcol_mix).then_inc(small_in, 16)
            sp.dma_start(bs_sb[:], b_s).then_inc(small_in, 16)
            sp.dma_start(lnw, ln_w.partition_broadcast(P)).then_inc(small_in, 16)
            sp.dma_start(ws_sb, ws_t).then_inc(small_in, 16)
            sp.dma_start(pos_sb[:], pos).then_inc(small_in, 16)
            sp.dma_start(w2s[:, 0, :], ck2).then_inc(small_in, 16)
            sp.dma_start(w2s[:, 1, :], cv2).then_inc(small_in, 16)
            sp.dma_start(lbraw[:], lbs).then_inc(small_in, 16)
            sp.dma_start(We[:, :, TM_ALL:W_EVEN], w_even[:, :, TM_ALL:W_EVEN]).then_inc(we_in, 16)
            sp.dma_start(We[:, :, 0:TM_ALL], w_even[:, :, 0:TM_ALL]).then_inc(we_in, 16)
            sp.dma_start(w1[:, 0, :], ck1).then_inc(w1_in, 16)
            sp.dma_start(w1[:, 1, :], cv1).then_inc(w1_in, 16)
            after(sp, fm_out, 7)
            for kv, dst in ((0, kcd), (1, vcd)):
                for g in range(2):
                    src = kvc[g * HD:(g + 1) * HD, kv, :]
                    sp.dma_start(dst[0:HD, g, :], src).then_inc(dup_in, 16)
                    sp.dma_start(dst[HD:P, g, 0:SEQ - 1], src[:, 1:SEQ]).then_inc(dup_in, 16)
            after(sp, hid_done, 0)
            sp.dma_start(w_out_sb, w_out_e).then_inc(wout_in, 16)
            after(sp, tm_done, TB - 1)
            sp.dma_start(wq, w_q[0]).then_inc(wq_in, 16)
            sp.dma_start(keysT, keys[0]).then_inc(wq_in, 16)
            after(sp, oT_out, 3)
            sp.dma_start(wrow, w_ffn[0:1, :].partition_broadcast(P)).then_inc(ffn_in, 16)
            after(sp, acc_out, TB - 1)
            sp.dma_start(slab[:, 0, :], w_odd[0]).then_inc(slab_in[0], 16)
            sp.dma_start(hgw, hg_w.partition_broadcast(P)).then_inc(lb_in, 16)
            sp.dma_start(slab[:, 1, :], w_odd[1]).then_inc(slab_in[1], 16)
            sp.dma_start(wq, w_q[1]).then_inc(wq_in, 16)
            sp.dma_start(keysT, keys[1]).then_inc(wq_in, 16)
            with sp.Fori(0, C_HEADS // 2 - 1) as hp:
                for e in range(2):
                    after(sp, pr_done, hp * 2 + e)
                    sp.dma_start(slab[:, e, :], w_odd[ds(hp * 2 + (e + 2), 1)].rearrange("o p n -> (o p) n")
                                 ).then_inc(slab_in[e], 16)
            after(sp, pr_done, C_HEADS - 1)
            sp.dma_start(wo_odd, w_out_o).then_inc(wout_in, 16)
            sp.dma_start(wrow, w_ffn[1:2, :].partition_broadcast(P)).then_inc(ffn_in, 16)
            after(sp, acc_out, 2 * TB - 1)
            sp.dma_start(wfin, w_fin.partition_broadcast(P)).then_inc(fin_in, 16)
            for b in range(TB):
                after(sp, og_final, b)
                sp.dma_start(out[b * P:(b + 1) * P, :], XN if b % 2 == 0 else XN2).then_inc(stored[b % 2], 16)
            for s in stored:
                sp.wait_ge(s, 16 * TB // 2)

        @block.gpsimd
        def _(pool):
            g = nc.gpsimd
            link = Chain(pool, pool_chain)
            pool.wait_ge(primed, 1)
            link(g.memset(half[:], -0.5))
            link(g.memset(ident_z[:], 0.0))
            link(g.affine_select(out=ident, in_=ident, compare_op=ALU.not_equal, fill=1.0, base=0,
                                 pattern=[[-1, P]], channel_multiplier=1))
            pool.sem_inc(half_set, 1)
            link(g.iota(alibi[:], [[1, SEQ]], base=-(SEQ - P), channel_multiplier=-1,
                        allow_small_or_imprecise_dtypes=True))
            link(g.affine_select(out=alibi[:], in_=alibi[:], compare_op=ALU.is_ge, fill=NEG, base=SEQ - P,
                                 pattern=[[-1, SEQ]], channel_multiplier=1))
            link(g.iota(alibi_c, [[-P, TB], [CMP_STRIDE, N_CMP]], base=CMP_BLOCK - 1, channel_multiplier=-1,
                        allow_small_or_imprecise_dtypes=True))
            link(g.affine_select(out=alibi_c, in_=alibi_c, compare_op=ALU.is_ge, fill=NEG,
                                 base=-(CMP_BLOCK - 1), pattern=[[P, TB], [-CMP_STRIDE, N_CMP]],
                                 channel_multiplier=1))
            link(g.memset(valid_c, 1.0))
            link(g.affine_select(out=valid_c, in_=valid_c, compare_op=ALU.is_ge, fill=0.0,
                                 base=-(CMP_BLOCK - 1), pattern=[[P, TB], [-CMP_STRIDE, N_CMP]],
                                 channel_multiplier=1))
            link(g.iota(iota16[:], [[1, TOPK]], base=0, channel_multiplier=0,
                        allow_small_or_imprecise_dtypes=True))
            link(g.memset(level_mask[:], 1))
            for lev in range(LEVELS):
                n = 1 << lev
                m = level_mask[:, lev, :].rearrange("p (b h l) -> p b h l", h=2, l=n)
                link(g.affine_select(out=m, in_=m, compare_op=ALU.is_ge, fill=0.0, base=0,
                                     pattern=[[-2 * n, P // (2 * n)], [0, 2], [0, n]], channel_multiplier=1))
                link(g.affine_select(out=m, in_=m, compare_op=ALU.is_ge, fill=0.0, base=n - 1,
                                     pattern=[[2 * n, P // (2 * n)], [0, 2], [0, n]], channel_multiplier=-1))
                link(g.memset(m[:, :, 0, :], 0))
            d = level_mask[:, LEVELS, :]
            link(g.affine_select(out=d, in_=d, compare_op=ALU.is_equal, fill=0.0, base=0,
                                 pattern=[[-1, P]], channel_multiplier=1))
            pool.wait_ge(small_in, 16 * 8)
            link(g.affine_select(out=ws_sb, in_=ws_sb, compare_op=ALU.is_ge, fill=0.0, base=0,
                                 pattern=[[0, A_GROUPS], [1, P]], channel_multiplier=-1))
            pool.sem_inc(consts, 1)

            def inverse_root(src, dst, n, count):
                link(g.tensor_scalar(dst, src, 1.0 / count, EPS, ALU.mult, ALU.add))
                link(g.tensor_tensor(dst, dst, half[:, 0:n], ALU.pow))

            after(pool, ss_ready, 0)
            inverse_root(stat[:, 0:TB], rstd[:, 0:TB], TB, D_MODEL)
            pool.sem_inc(rs_ready.sem, 1)
            for tb in range(TB):
                after(pool, ln_ss, tb)
                inverse_root(mean[:], rstd[:, 4:8], 4, P)
                pool.sem_inc(ln_rs.sem, 1)

            def peer(layer):
                for first, n in ((0, 1), (1, TB - 1)):
                    after(pool, ss_ready, 1 + 3 * layer + first)
                    inverse_root(stat[:, first:first + n], rstd[:, first:first + n], n, D_MODEL)
                    pool.sem_inc(rs_ready.sem, 1)
                after(pool, wo_done, layer * TB + TB - 1)
                tab = uv[layer]
                with pool.Fori(0, LAYER_UNITS // 2) as up:
                    for e in range(2):
                        after(pool, routed, up * 2 + (e + layer * (LAYER_UNITS + 1)))
                        for k in range(TOPK):
                            after(pool, slot_done, up * (2 * TOPK) + (e * TOPK + k - NBUF + layer * LAYER_SLOTS))
                            g.indirect_dma_start(
                                out=gath[:, k % NBUF, :], out_offset=None, in_=tab,
                                in_offset=bass.IndirectOffsetOnAxis(
                                    ap=experts[:, e * TOPK + k:e * TOPK + k + 1], axis=0),
                            ).then_inc(gathered[k % NBUF], 16)

            peer(0)

            after(pool, ss_ready, 3)
            inverse_root(stat[:, 0:TB], rstd[:, 0:TB], TB, D_MODEL)
            pool.sem_inc(rs_ready.sem, 1)
            link.reset()
            with pool.Fori(0, C_HEADS) as h:
                for lev in range(LEVELS):
                    n = 1 << lev
                    after(pool, e_ready, h * LEVELS + lev)
                    after(pool, lv_done, h * (LEVELS + 1) + (-2, -3)[lev] if lev < 2 else h * (LEVELS + 1) + (lev - 2))
                    left = "p (b h l) -> p b h l"
                    o_ = kE[:, lev % 2, :].rearrange(left, h=2, l=n)[:, :, 0, :]
                    k_ = kk.rearrange(left, h=2, l=n)[:, :, 0, :]
                    e_ = dE[:, lev % 2, :].rearrange(left, h=2, l=n)[:, :, 0, :]
                    g.tensor_tensor(o_, k_, e_, ALU.mult).then_inc(ke_ready.sem, 1)
                after(pool, oss_ready, h)
                inverse_root(mean[:], rstd[:, 4:8], 4, P)
                pool.sem_inc(ors_ready.sem, 1)
                link.reset()

            peer(1)
            after(pool, ss_ready, 6)
            inverse_root(stat[:, 0:TB], rstd[:, 0:TB], TB, D_MODEL)
            pool.sem_inc(rs_ready.sem, 1)

        @block.scalar
        def _(act):
            a = nc.scalar
            link = Chain(act, act_chain)
            act.wait_ge(primed, 1)
            act.wait_ge(small_in, 16 * 8)
            for ch in range(8):
                after(act, fm_done, ch)
                dst = qT[:, ch, :] if ch < 4 else (kvc[:, ch - 4, :] if ch < 6 else kT[:, ch - 6, :])
                a.activation(dst, PS[:, 6 + ch % 2, :], ACT.Copy).then_inc(fm_out.sem, 1)
            for tb in range(TB):
                after(act, tm_done, tb)
                after(act, a_ready, tb - 1)
                a.activation(gu, PS[:, 3 * (tb % 2), :], ACT.Gelu_apprx_tanh)
                a.activation(gv, PS[:, 3 * (tb % 2) + 1, :], ACT.Gelu_apprx_tanh).then_inc(uv_out.sem, 1)
                a.activation(vsw[:, tb, :, :], PS[:, 3 * (tb % 2) + 2, 0:256].rearrange("p (a b) -> p a b", a=2),
                             ACT.Copy)
                a.activation(gates[:, tb, :], PS[:, 3 * (tb % 2) + 2, 256:280], ACT.Copy).then_inc(vsw_out.sem, 1)
                if tb == 0:
                    after(act, posb_done, 0)
                    link(a.activation(posb[:], PS[:, 6, 0:2], ACT.Copy))
                    after(act, hid_done, 0)
                    for kv in range(2):
                        i = a.activation(hid[:, kv, :], PS[:, 7, kv * 64:kv * 64 + 2 * N_CMP], ACT.Gelu_apprx_tanh,
                                         bias=posb[:, kv:kv + 1])
                    i.then_inc(hid_out.sem, 1)
                    after(act, cmp_done, 0)
                    a.activation(kcmp[:], PS[:, 3, 0:N_CMP], ACT.Copy)
                    a.activation(vcmp[:], PS[0:N_CMP, 4, 0:2 * HD], ACT.Copy).then_inc(cmp_out.sem, 1)
                after(act, aT_done, tb)
                a.activation(mixT[:, 0:4, tb * P:(tb + 1) * P], v3(PS[:, 7, :], 4), ACT.Copy).then_inc(aT_out.sem, 1)
            after(act, vsw_out, TB - 1)
            link(a.activation(gates.rearrange("p a b -> p (a b)"), gates.rearrange("p a b -> p (a b)"), ACT.Sigmoid))
            act.sem_inc(gate_sig.sem, 1)
            with act.Fori(0, 4) as c:
                after(act, sc_done, c * UNITS - 1)
                i = a.activation(qst, qT[:, ds(c, 1), :].rearrange("p a b -> p (a b)"), ACT.Copy)
                i.then_inc(q_staged.sem, 1)

                after(act, z_ready, c * (UNITS + 1))
                a.activation(pc.rearrange("p a b c -> p (a b c)"), pc.rearrange("p a b c -> p (a b c)"), ACT.Exp,
                             scale=0.125).then_inc(ec_ready.sem, 1)

                def exps(i):
                    qb, e = unit(i)
                    par, nk = i % 2, (qb + 1) * P
                    after(act, z_ready, c * (UNITS + 1) + (i + 1))
                    after(act, pT_done, c * UNITS + (i - 2))
                    for br in range(2):
                        last = a.activation(ps_[:, par, br * SEQ:br * SEQ + nk], zs[:, par, br * SEQ:br * SEQ + nk],
                                            ACT.Exp, bias=nmax[:, par, br:br + 1], scale=0.125,
                                            accum_out=sums[:, par, br:br + 1])
                    last.then_inc(p_ready.sem, 1)

                exps(0)
                after(act, pcT_done, c)
                a.activation(pcT[:, :, :, :].rearrange("p a b c -> p a (b c)"),
                             PS[0:N_CMP, 6:8, :], ACT.Copy).then_inc(pcT_out.sem, 1)
                for i in range(UNITS):
                    qb, e = unit(i)
                    par, nk = i % 2, (qb + 1) * P
                    after(act, pT_done, c * UNITS + i)
                    after(act, pv_done, c * UNITS + (i - 2))
                    a.activation(pTs[:, par, :].rearrange("p (a b) -> p a b", a=2)[:, :, 0:nk], PS[:, 4:6, 0:nk],
                                 ACT.Copy).then_inc(pT_out.sem, 1)
                    if i + 1 < UNITS:
                        exps(i + 1)
                after(act, oT_done, c)
                a.activation(mixT[:, ds(c + 4, 1), :].rearrange("p a b -> p (a b)"), PS[:, 4, :],
                             ACT.Copy).then_inc(oT_out.sem, 1)

            def peer(layer):
                U0, R0, S0, B0 = layer * LAYER_UNITS, layer * (LAYER_UNITS + 1), layer * LAYER_SLOTS, layer * (TB + 1)
                G0 = S0 // GRP

                def route(r):
                    after(act, rq_done, r)
                    a.activation(q_sb, v3(PS[:, 4, 0:256], 2), ACT.Copy).then_inc(rq_out.sem, 1)
                    after(act, rqT_done, r)
                    a.activation(qT_sb, v3(PS[:, 5, 0:256], 2), ACT.Copy).then_inc(rqT_out.sem, 1)

                def soft(r):
                    after(act, gexp_in, r)
                    a.activation(gexp, best, ACT.Exp, bias=gstat[:, 0:1],
                                 accum_out=gstat[:, 1:2]).then_inc(gexp_out.sem, 1)

                def diags(e, grp_index, slot_index, grp):
                    after(act, w_ready, grp_index)
                    for k in range(grp * GRP, grp * GRP + GRP):
                        after(act, slot_done, slot_index + (k - NBUF))
                        a.activation(diag[:, k % NBUF, :], ident, ACT.Copy,
                                     scale=wts[:, e * TOPK + k:e * TOPK + k + 1]).then_inc(diag_ready.sem, 1)

                after(act, pxT_done, B0)
                for j in range(2):
                    i = a.activation(hTb[:, 4 * j:4 * j + 4, :], v3(PS[:, 2 + j, :], 4), ACT.Copy)
                i.then_inc(pxT_out.sem, 1)
                route(R0)
                soft(R0)

                def pair(b, u, last):
                    for e in range(2):
                        if last and e == 1:
                            after(act, pxT_done, b + (B0 + 1))
                            after(act, rq_done, u + (R0 + 1))
                            for j in range(2):
                                i = a.activation(hTb[:, 4 * j:4 * j + 4, :], v3(PS[:, 2 + j, :], 4), ACT.Copy)
                            i.then_inc(pxT_out.sem, 1)
                        route(u + (e + 1 + R0))
                        for grp in range(TOPK // GRP):
                            gi = u * (TOPK // GRP) + (e * (TOPK // GRP) + grp + G0)
                            after(act, dots_ready, gi)
                            q0 = e * TOPK + grp * GRP
                            a.activation(gact[:, q0:q0 + GRP], dots[:, q0:q0 + GRP], ACT.Gelu_apprx_tanh
                                         ).then_inc(gelu_ready.sem, 1)
                            diags(e, gi, u * TOPK + (e * TOPK + S0), grp)
                            if grp == 1:
                                soft(u + (e + 1 + R0))

                with act.Fori(0, TB) as b:
                    with act.Fori(0, P_HEADS // 2 - 1) as hp:
                        pair(b, b * P_HEADS + hp * 2, False)
                    pair(b, b * P_HEADS + (P_HEADS - 2), True)

            peer(0)

            link.reset()
            link(a.activation(lb[:, 0, :], lb[:, 1, :], ACT.Sigmoid))
            act.sem_inc(lf_ready.sem, 1)
            with act.Fori(0, C_HEADS // 2) as hp:
                for e in range(2):
                    h = hp * 2 + e
                    after(act, pr_done, h)
                    after(act, og_ready, h - 1)
                    a.activation(sigm, PS[:, 1, :], ACT.Sigmoid)
                    a.activation(dE[:, 0, :], PS[:, 0, :], ACT.Sigmoid).then_inc(sig_ready.sem, 1)
                    gi = PS[:, 2:4, :].rearrange("p a (b c) -> p (a b) c", b=2)
                    a.activation(v3(iS, 4), gi[:, :, 0:P], ACT.Copy)
                    a.activation(v3(dE[:, 1, :], 4), gi[:, :, P:2 * P], ACT.Sigmoid).then_inc(i_out.sem, 1)
                    after(act, fg_ready, h)
                    a.activation(bb, fg, ACT.Ln).then_inc(lf_ready.sem, 1)
                    for lev in range(LEVELS):
                        after(act, dd_ready, h * LEVELS + lev)
                        a.activation(dE[:, lev % 2, :], dE[:, lev % 2, :], ACT.Exp).then_inc(e_ready.sem, 1)
                    after(act, kds_ready, h)
                    a.activation(eb, bb, ACT.Exp)
                    a.activation(kd, kd, ACT.Exp).then_inc(ebe_ready.sem, 1)
                    after(act, kdT_done, h)
                    a.activation(kdT, PS[:, 6, :], ACT.Copy).then_inc(kdT_out.sem, 1)
                    after(act, oi_done, h)
                    a.activation(v3(sigm, 4), v3(PS[:, 6, :], 4), ACT.Square).then_inc(osq_ready.sem, 1)
                    after(act, ogT_done, h)
                    a.activation(mixT[:, ds(h, 1), :].rearrange("p a b -> p (a b)"), PS[:, 7, :],
                                 ACT.Copy).then_inc(ogT_out.sem, 1)

            peer(1)

        @block.vector
        def _(dve):
            v = nc.vector
            link = Chain(dve, dve_chain)
            dve.wait_ge(primed, 1)
            dve.wait_ge(small_in, 16 * 8)
            link(v.memset(slope[:, 0:1], 4.0))
            link(v.memset(slope[:, 1:2], 0.25))
            link(v.tensor_tensor(lb[:, 1, :], lbraw[:, 1, :], lbraw[:, 0, :], ALU.subtract))
            dve.wait_ge(x_in, 16)

            def squares():
                for tb in range(TB):
                    link(v.tensor_tensor_reduce(out=xnS[:, tb % 2, :], in0=X[:, tb, :], in1=X[:, tb, :], scale=1.0,
                                                scalar=0.0, op0=ALU.mult, op1=ALU.add, accum_out=stat[:, tb:tb + 1]))
                dve.sem_inc(ss_ready.sem, 1)

            def normed_transposed(layer):
                dve.wait_ge(half_set, 1)
                for tb in range(TB):
                    n = layer * TB + tb
                    after(dve, xT_done, n - 2)
                    v.tensor_scalar(xnS[:, tb % 2, :], X[:, tb, :], rstd[:, tb:tb + 1], None, ALU.mult
                                    ).then_inc(xn_ready.sem, 1)
                    after(dve, xT_done, n)
                    v.tensor_tensor(hT[:, :, tb * P:(tb + 1) * P],
                                    PS[:, 0:2, :].rearrange("p a (b c) -> p (a b) c", b=4),
                                    bc(wcol[:, layer, :], P), ALU.mult).then_inc(hT_ready.sem, 1)

            squares()
            after(dve, rs_ready, 0)
            normed_transposed(0)
            dve.wait_ge(consts, 1)
            for tb in range(TB):
                after(dve, uv_out, tb)
                after(dve, mix_done, tb - 1)
                link(v.tensor_reduce(mean[:], v3(gv, 4), AXX, ALU.add))
                link(v.tensor_scalar(mean[:], mean[:], 1.0 / P, None, ALU.mult))
                link(v.tensor_tensor(v3(gvn, 4), v3(gv, 4), bc(mean[:], P), ALU.subtract))
                link(v.tensor_tensor(gsq, gvn, gvn, ALU.mult))
                link(v.tensor_reduce(mean[:], v3(gsq, 4), AXX, ALU.add))
                dve.sem_inc(ln_ss.sem, 1)
                link(v.tensor_tensor(gvn, gvn, lnw, ALU.mult))
                after(dve, ln_rs, tb)
                v.tensor_tensor(v3(gvn, 4), v3(gvn, 4), bc(rstd[:, 4:8], P), ALU.mult).then_inc(ln_done.sem, 1)
                after(dve, mix_done, tb)
                for gr in range(A_GROUPS):
                    last = v.scalar_tensor_tensor(gsq[:, gr * P:(gr + 1) * P], PS[:, 6, gr * P:(gr + 1) * P],
                                                  bs_sb[:, gr:gr + 1], gu[:, gr * P:(gr + 1) * P], ALU.add, ALU.mult)
                last.then_inc(a_ready.sem, 1)
                after(dve, aT_done, tb)
            link.reset()
            after(dve, gate_sig, 0)
            gview = gates.rearrange("p b (e c r) -> p b e c r", e=2, c=4)
            with dve.Fori(0, 4) as c:
                for e in range(2):
                    link(v.tensor_copy(gst[:, :, e, :], gates[:, :, ds(c * 3 + 12 * e, 3)]))
                after(dve, cs_done, c)
                for e in range(2):
                    link(v.scalar_tensor_tensor(pc[:, e, :, :], alibi_c, slope[:, e:e + 1],
                                                PS[:, 4 + e, 0:TB * N_CMP].rearrange("p (a b) -> p a b", a=TB),
                                                ALU.mult, ALU.add))
                pc3 = pc.rearrange("p a b c -> p (a b) c")
                cm, cs = cmax[:].rearrange("p a b -> p (a b)"), csum[:].rearrange("p a b -> p (a b)")
                link(v.tensor_reduce(cm, pc3, AXX, ALU.max))
                link(v.tensor_tensor(pc3, pc3, bc(cm, N_CMP), ALU.subtract))
                dve.sem_inc(z_ready.sem, 1)

                def biased(i):
                    qb, e = unit(i)
                    par, nk = i % 2, (qb + 1) * P
                    after(dve, sc_done, c * UNITS + i)
                    after(dve, p_ready, c * UNITS + (i - 2))
                    z = zs[:, par, :].rearrange("p (a b) -> p a b", a=2)[:, :, 0:nk]
                    link(v.scalar_tensor_tensor(z, bmid(alibi[:, SEQ - nk:SEQ], 2), slope[:, e:e + 1],
                                                PS[:, 2 * par:2 * par + 2, 0:nk], ALU.mult, ALU.add))
                    link(v.tensor_reduce(nmax[:, par, :], z, AXX, ALU.max))
                    link(v.tensor_scalar(nmax[:, par, :], nmax[:, par, :], -0.125, None, ALU.mult))
                    dve.sem_inc(z_ready.sem, 1)

                def combine(i):
                    qb, e = unit(i)
                    par = i % 2
                    after(dve, p_ready, c * UNITS + i)
                    link(v.reciprocal(coef[:], sums[:, par, :]))
                    link(v.tensor_tensor(coef[:], coef[:], gst[:, qb, e, 1:3], ALU.mult))
                    after(dve, pv_done, c * UNITS + i)
                    o = v3(ot, 4)[:, qb, e * HD:(e + 1) * HD]
                    pv = PS[:, 6 + par, 0:192].rearrange("p (a b) -> p a b", a=3)
                    link(v.tensor_scalar(o, pv[:, 0, :], coef[:, 0:1], None, ALU.mult))
                    link(v.scalar_tensor_tensor(o, pv[:, 1, :], coef[:, 1:2], o, ALU.mult, ALU.add))
                    link(v.scalar_tensor_tensor(o, pv[:, 2, :], csum[:, e, qb:qb + 1], o, ALU.mult, ALU.add))
                    dve.sem_inc(o_ready.sem, 1)

                after(dve, oT_done, c - 1)
                biased(0)
                after(dve, ec_ready, c)
                vb = valid_c.rearrange("p b n -> p (b n)")
                for e in range(2):
                    pe_ = pc[:, e, :, :].rearrange("p b n -> p (b n)")
                    link(v.tensor_tensor(pe_, pe_, vb, ALU.mult))
                dve.sem_inc(pc_ready.sem, 1)
                link(v.tensor_reduce(cs, pc3, AXX, ALU.add))
                link(v.tensor_scalar(cs, cs, 1e-30, None, ALU.max))
                link(v.reciprocal(cs, cs))
                link(v.tensor_tensor(csum[:], csum[:], gst[:, :, :, 0].rearrange("p b e -> p e b"), ALU.mult))
                for i in range(UNITS):
                    if i + 1 < UNITS:
                        biased(i + 1)
                    combine(i)
                link(v.tensor_scalar(slope[:], slope[:], 0.5, None, ALU.mult))
                link.reset()

            def residual(layer, tb, mark):
                after(dve, wo_done, layer * TB + tb)
                p = OUT_BANKS[tb]
                link(v.tensor_tensor(X[:, tb, :].rearrange("p (a b) -> p a b", a=2),
                                     X[:, tb, :].rearrange("p (a b) -> p a b", a=2), PS[:, p:p + 2, :], ALU.add))
                dve.sem_inc(wo_out.sem, 1)
                link(v.tensor_tensor_reduce(out=XN, in0=X[:, tb, :], in1=X[:, tb, :], scale=1.0,
                                            scalar=0.0, op0=ALU.mult, op1=ALU.add, accum_out=stat[:, tb:tb + 1]))
                if mark:
                    dve.sem_inc(ss_ready.sem, 1)

            def peer(layer):
                U0, R0, S0, B0 = layer * LAYER_UNITS, layer * (LAYER_UNITS + 1), layer * LAYER_SLOTS, layer * (TB + 1)
                G0 = S0 // GRP
                residual(layer, 0, True)
                dve.wait_ge(ffn_in, 16 * (layer + 1))
                after(dve, rs_ready, 1 + 3 * layer)

                def prologue(b):
                    link(v.tensor_copy(rsb[:], rstd[:, ds(b, 1)]))
                    link(v.scalar_tensor_tensor(XN2, X[:, ds(b, 1), :].rearrange("p a d -> p (a d)"), rsb[:], wrow,
                                                ALU.mult, ALU.mult))
                    dve.sem_inc(pxn_ready.sem, 1)

                def top16(vals, idx, src, spare):
                    link(v.max(vals[:, 0:8], src))
                    link(v.max_index(idx[:, 0:8], vals[:, 0:8], src))
                    link(v.match_replace(spare, vals[:, 0:8], src, -3e38))
                    link(v.max(vals[:, 8:16], spare))
                    link(v.max_index(idx[:, 8:16], vals[:, 8:16], spare))

                def scores_in(r):
                    after(dve, rs_done, r)
                    link(v.tensor_copy(s1, v3(PS[:, 6, 0:256], 2)))
                    dve.sem_inc(rs_out.sem, 1)
                    top16(vtop[:, 0, :], itop[:, 0, :], s1[:, 0, :], s2[:, 0, :])

                def second_half():
                    top16(vtop[:, 1, :], itop[:, 1, :], s1[:, 1, :], s2[:, 1, :])
                    link(v.tensor_copy(itopf, itop))

                def candidates(r):
                    link(v.tensor_tensor(v3(cand, TOPK), bc(vtop[:, 0, :], TOPK), bmid(vtop[:, 1, :], TOPK), ALU.add))
                    top16(best, bpos, cand, cand2)
                    link(v.tensor_scalar(gstat[:, 0:1], best[:, 0:1], -1.0, None, ALU.mult))
                    dve.sem_inc(gexp_in.sem, 1)

                def chosen(e):
                    link(v.tensor_scalar(bij[:, 0, :], bpos, 4, None, ALU.logical_shift_right))
                    link(v.tensor_scalar(bij[:, 1, :], bpos, 15, None, ALU.bitwise_and))
                    link(v.tensor_copy(bijf, bij))
                    for p in range(2):
                        oh = oneh[:, p, :, :]
                        link(v.tensor_tensor(oh, bc(bijf[:, p, :], TOPK), bmid(iota16[:], TOPK), ALU.is_equal))
                        link(v.tensor_tensor(oh, oh, bmid(itopf[:, p, :], TOPK), ALU.mult))
                        link(v.tensor_reduce(esel[:, p, :], oh, AXX, ALU.add))
                    link(v.scalar_tensor_tensor(experts[:, e * TOPK:(e + 1) * TOPK], esel[:, 0, :], float(NKEYS),
                                                esel[:, 1, :], ALU.mult, ALU.add))

                def gates_of(e, r):
                    after(dve, gexp_out, r)
                    link(v.reciprocal(gstat[:, 2:3], gstat[:, 1:2]))
                    link(v.tensor_scalar(gate[:, e, :], gexp, gstat[:, 2:3], None, ALU.mult))
                    dve.sem_inc(routed.sem, 1)

                link(v.tensor_copy(rsb[:], rstd[:, 0:1]))
                link(v.scalar_tensor_tensor(XN2, X[:, 0, :], rsb[:], wrow, ALU.mult, ALU.mult))
                dve.sem_inc(pxn_ready.sem, 1)
                residual(layer, 1, False)
                scores_in(R0)
                second_half()
                candidates(R0)
                chosen(0)
                gates_of(0, R0)
                residual(layer, 2, False)
                residual(layer, 3, True)
                after(dve, rs_ready, 2 + 3 * layer)
                link.reset()

                def pair(b, u, last):
                    for e in range(2):
                        r = u + (e + 1 + R0)
                        if last and e == 1:
                            prologue(b + 1)
                        for grp in range(TOPK // GRP):
                            gi = u * (TOPK // GRP) + (e * (TOPK // GRP) + grp + G0)
                            for k in range(grp * GRP, grp * GRP + GRP):
                                buf = k % NBUF
                                rounds = TOPK // NBUF
                                reached(dve, gathered[buf],
                                        u * (16 * rounds) + 16 * (rounds * (U0 + e) + k // NBUF + 1))
                                q = e * TOPK + k
                                i = v.tensor_tensor_reduce(out=gath[:, buf, 0:D_MODEL], in0=gath[:, buf, 0:D_MODEL],
                                                           in1=XN, scale=1.0, scalar=0.0, op0=ALU.mult, op1=ALU.add,
                                                           accum_out=dots[:, q:q + 1])
                            link(i)
                            dve.sem_inc(dots_ready.sem, 1)
                            after(dve, gelu_ready, gi)
                            q0 = e * TOPK + grp * GRP
                            v.tensor_tensor(wts[:, q0:q0 + GRP], gact[:, q0:q0 + GRP],
                                            gate[:, e, grp * GRP:grp * GRP + GRP], ALU.mult).then_inc(w_ready.sem, 1)
                            if grp == 0:
                                scores_in(r)
                                second_half()
                            if grp == 1:
                                candidates(r)
                                chosen(1 - e)
                                gates_of(1 - e, r)
                        link.reset()

                with dve.Fori(0, TB) as b:
                    link(v.tensor_copy(XN, XN2))
                    link.reset()
                    with dve.Fori(0, P_HEADS // 2 - 1) as hp:
                        pair(b, b * P_HEADS + hp * 2, False)
                    pair(b, b * P_HEADS + (P_HEADS - 2), True)
                    after(dve, acc_done, b + layer * TB)
                    xb = X[:, ds(b, 1), :].rearrange("p a (c d) -> p (a c) d", c=2)
                    link(v.tensor_tensor(xb, xb, PS[:, 0:2, :], ALU.add))
                    dve.sem_inc(acc_out.sem, 1)
                    link.reset()

            peer(0)

            squares()
            after(dve, rs_ready, 3)
            normed_transposed(1)
            link(v.memset(scan_keep[:], 1.0))
            link(v.memset(v3(scan_keep[:], TB)[:, :, 0:1], 0.0))
            link(v.memset(attn, 0.0))
            link(v.memset(qE, 0.0))
            link(v.memset(kE, 0.0))
            after(dve, lf_ready, 0)
            dve.wait_ge(lb_in, 16)
            link(v.tensor_scalar(lb[:, 1, :], lb[:, 0, :], -1.0, 1.0, ALU.mult, ALU.add))
            link.reset()
            with dve.Fori(0, C_HEADS // 2) as hp:
                for e in range(2):
                    h = hp * 2 + e
                    for j in range(2):
                        link(v.tensor_copy(lbst[:, j, 0:1], lb[:, j, ds(h, 1)]))
                    after(dve, sig_ready, h)
                    link(v.tensor_scalar(fg, sigm, lbst[:, 1, 0:1], lbst[:, 0, 0:1], ALU.mult, ALU.add))
                    link(v.tensor_scalar(kk, fg, -1.0, 1.0, ALU.mult, ALU.add))
                    link(v.tensor_scalar(fg, fg, 2.0 ** -63, None, ALU.max))
                    dve.sem_inc(fg_ready.sem, 1)
                    link(v.tensor_tensor(qs, PS[:, 0, :], dE[:, 0, :], ALU.mult))
                    dve.sem_inc(qk_ready.sem, 1)
                    after(dve, lf_ready, h + 1)
                    link(v.tensor_tensor_scan(bb, scan_keep[:], bb, 0.0, ALU.mult, ALU.add))
                    halves = "p (b h l) -> p b h l"

                    def distance(lev):
                        n = 1 << lev
                        b_ = bb.rearrange(halves, h=2, l=n)
                        d_ = dE[:, lev % 2, :].rearrange(halves, h=2, l=n)
                        ref = b_[:, :, 0, n - 1:n].broadcast_to([P, SEQ // (2 * n), n])
                        if lev >= 2:
                            after(dve, ke_ready, h * LEVELS + (lev - 2))
                            after(dve, qe_ready, h * LEVELS + (lev - 2))
                        link(v.tensor_tensor(d_[:, :, 0, :], ref, b_[:, :, 0, :], ALU.subtract))
                        v.tensor_tensor(d_[:, :, 1, :], b_[:, :, 1, :], ref, ALU.subtract).then_inc(dd_ready.sem, 1)

                    def evacuate(lev):
                        after(dve, lv_done, h * (LEVELS + 1) + lev)
                        link(v.copy_predicated(v3(attn, 4), bmid(level_mask[:, lev, :], 4),
                                               v3(PS[:, 4 + lev % 2, :], 4)))
                        dve.sem_inc(lv_out.sem, 1)

                    distance(0)
                    gi = PS[:, 2:4, :].rearrange("p a (b c) -> p (a b) c", b=2)
                    after(dve, i_out, h)
                    link(v.tensor_tensor(v3(gs, 4), gi[:, :, P:2 * P], v3(dE[:, 1, :], 4), ALU.mult))
                    dve.sem_inc(ig_free.sem, 1)
                    link(v.tensor_tensor(v3(gs, 4), v3(gs, 4), bmid(hgw[:, ds(h * P, P)], 4), ALU.mult))
                    for lev in range(LEVELS):
                        n = 1 << lev
                        if lev + 1 < LEVELS:
                            distance(lev + 1)
                        after(dve, e_ready, h * LEVELS + lev)
                        if lev >= 2:
                            after(dve, lv_done, h * (LEVELS + 1) + (lev - 2))
                        v.tensor_tensor(qE[:, lev % 2, :].rearrange(halves, h=2, l=n)[:, :, 1, :],
                                        qs.rearrange(halves, h=2, l=n)[:, :, 1, :],
                                        dE[:, lev % 2, :].rearrange(halves, h=2, l=n)[:, :, 1, :], ALU.mult
                                        ).then_inc(qe_ready.sem, 1)
                        if lev:
                            evacuate(lev - 1)
                    link(v.tensor_tensor(v3(kd, 4), bc(v3(bb, 4)[:, :, P - 1], P), v3(bb, 4), ALU.subtract))
                    dve.sem_inc(kds_ready.sem, 1)
                    evacuate(LEVELS - 1)
                    evacuate(LEVELS)
                    after(dve, ebe_ready, h)
                    link(v.tensor_tensor(kd, kk, kd, ALU.mult))
                    link(v.tensor_tensor(qd, qs, eb, ALU.mult))
                    dve.sem_inc(kd_ready.sem, 1)
                    after(dve, kv_done, h)
                    link(v.tensor_copy(Sst[:, 0, :], PS[:, 7, 0:P]))
                    for b in (1, 2):
                        link(v.scalar_tensor_tensor(Sst[:, b, :], Sst[:, b - 1, :], v3(eb, 4)[:, b, P - 1:P],
                                                    PS[:, 7, b * P:(b + 1) * P], ALU.mult, ALU.add))
                    dve.sem_inc(s_ready.sem, 1)
                    after(dve, osq_ready, h)
                    link(v.tensor_reduce(mean[:], v3(sigm, 4), AXX, ALU.add))
                    dve.sem_inc(oss_ready.sem, 1)
                    link(v.tensor_tensor(v3(ob, 4), v3(PS[:, 6, :], 4), v3(gs, 4), ALU.mult))
                    after(dve, ors_ready, h)
                    v.tensor_tensor(v3(ob, 4), v3(ob, 4), bc(rstd[:, 4:8], P), ALU.mult).then_inc(og_ready.sem, 1)
                    after(dve, ogT_done, h)
                    link.reset()
            peer(1)
            squares()
            after(dve, rs_ready, 6)
            dve.wait_ge(fin_in, 16)
            for b in range(TB):
                dst = XN if b % 2 == 0 else XN2
                if b >= 2:
                    dve.wait_ge(stored[b % 2], 16)
                v.scalar_tensor_tensor(dst, X[:, b, :], rstd[:, b:b + 1], wfin, ALU.mult, ALU.mult
                                       ).then_inc(og_final.sem, 1)

        @block.tensor
        def _(pe):
            t = nc.tensor
            pe.wait_ge(primed, 1)

            def transposes(layer):
                for tb in range(TB):
                    n = layer * TB + tb
                    after(pe, xn_ready, n)
                    after(pe, hT_ready, n - 1)
                    for c in range(KC):
                        i = t.transpose(PS[:, c // 4, (c % 4) * P:(c % 4 + 1) * P], xnS[:, tb % 2, c * P:(c + 1) * P],
                                        ident)
                    i.then_inc(xT_done.sem, 1)

            pe.wait_ge(half_set, 1)
            transposes(0)
            after(pe, hT_ready, TB - 1)
            pe.wait_ge(we_in, 32)
            for ch in range(8):
                after(pe, fm_out, ch - 2)
                for c in range(KC):
                    i = t.matmul(PS[:, 6 + ch % 2, :], We[:, c, TM_ALL + ch * P:TM_ALL + (ch + 1) * P], hT[:, c, :],
                                 start=c == 0, stop=c == KC - 1)
                i.then_inc(fm_done.sem, 1)
            pe.wait_ge(consts, 1)

            def token_major(tb):
                after(pe, uv_out, tb - 2)
                after(pe, vsw_out, tb - 2)
                p = 3 * (tb % 2)
                for j, (c0, c1) in enumerate(((0, 512), (512, 1024), (1024, TM_ALL))):
                    for c in range(KC):
                        i = t.matmul(PS[:, p + j, 0:c1 - c0], hT[:, c, tb * P:(tb + 1) * P], We[:, c, c0:c1],
                                     start=c == 0, stop=c == KC - 1)
                i.then_inc(tm_done.sem, 1)

            after(pe, fm_out, 7)
            token_major(0)
            pe.wait_ge(w1_in, 32)
            pe.wait_ge(dup_in, 16 * 8)
            J = CMP_BLOCK // 2
            for kv in range(2):
                for j in range(J):
                    i = t.matmul(PS[:, 6, kv:kv + 1], w1[:, kv, j * P:(j + 1) * P], pos_sb[:, j:j + 1],
                                 start=j == 0, stop=j == J - 1)
            i.then_inc(posb_done.sem, 1)
            for kv, src in ((0, kcd), (1, vcd)):
                for j in range(J):
                    sv = src[:, :, 2 * j:2 * j + CMP_STRIDE * (N_CMP - 1) + 1:CMP_STRIDE]
                    i = t.matmul(PS[:, 7, kv * 64:kv * 64 + 2 * N_CMP].rearrange("p (a b) -> p a b", a=2),
                                 w1[:, kv, j * P:(j + 1) * P], sv, start=j == 0, stop=j == J - 1)
            i.then_inc(hid_done.sem, 1)
            after(pe, hid_out, 0)
            for g_ in range(2):
                t.matmul(PS[g_ * HD:(g_ + 1) * HD, 3, 0:N_CMP], w2s[:, 0, :], hid[:, 0, g_ * N_CMP:(g_ + 1) * N_CMP],
                         start=True, stop=True)
                i = t.matmul(PS[0:N_CMP, 4, g_ * HD:(g_ + 1) * HD], hid[:, 1, g_ * N_CMP:(g_ + 1) * N_CMP],
                             w2s[:, 1, :], start=True, stop=True)
            i.then_inc(cmp_done.sem, 1)
            after(pe, cmp_out, 0)
            for tb in range(TB):
                if tb + 1 < TB:
                    token_major(tb + 1)
                after(pe, ln_done, tb)
                after(pe, a_ready, tb - 1)
                for gr in range(A_GROUPS):
                    i = t.matmul(PS[:, 6, gr * P:(gr + 1) * P], ws_sb[:, gr, :], gvn[:, gr * P:(gr + 1) * P],
                                 start=True, stop=True)
                i.then_inc(mix_done.sem, 1)
                after(pe, a_ready, tb)
                after(pe, aT_out, tb - 1)
                for gr in range(A_GROUPS):
                    i = t.transpose(PS[:, 7, gr * P:(gr + 1) * P], gsq[:, gr * P:(gr + 1) * P], ident)
                i.then_inc(aT_done.sem, 1)
            after(pe, aT_out, TB - 1)
            with pe.Fori(0, 4) as c:
                after(pe, q_staged, c)

                def scores(i):
                    qb, e = unit(i)
                    par, nk = i % 2, (qb + 1) * P
                    after(pe, z_ready, c * (UNITS + 1) + (i - 1) if i >= 2 else c * (UNITS + 1) + (i - 2))
                    r = slice(e * HD, (e + 1) * HD)
                    for br in range(2):
                        k_ = t.matmul(PS[:, 2 * par + br, 0:nk], qst[r, qb * P:(qb + 1) * P], kT[r, br, 0:nk],
                                      start=True, stop=True)
                    k_.then_inc(sc_done.sem, 1)

                after(pe, oT_out, c - 1)
                after(pe, o_ready, c * UNITS - 1)
                for i in range(UNITS):
                    qb, e = unit(i)
                    r = slice(e * HD, (e + 1) * HD)
                    k_ = t.matmul(PS[:, 4 + e, qb * N_CMP:(qb + 1) * N_CMP], qst[r, qb * P:(qb + 1) * P],
                                  kcmp[r, :], start=True, stop=True)
                k_.then_inc(cs_done.sem, 1)
                scores(0)
                scores(1)
                after(pe, pc_ready, c)
                for i in range(UNITS):
                    qb, e = unit(i)
                    k_ = t.transpose(PS[0:N_CMP, 6 + e, qb * P:(qb + 1) * P], pc[:, e, qb, :], ident)
                k_.then_inc(pcT_done.sem, 1)
                after(pe, pcT_out, c)
                for i in range(UNITS):
                    qb, e = unit(i)
                    par = i % 2
                    after(pe, p_ready, c * UNITS + i)
                    after(pe, pT_out, c * UNITS + (i - 1))
                    for br in range(2):
                        for kt in range(qb + 1):
                            k_ = t.transpose(PS[:, 4 + br, kt * P:(kt + 1) * P],
                                             ps_[:, par, br * SEQ + kt * P:br * SEQ + (kt + 1) * P], ident)
                    k_.then_inc(pT_done.sem, 1)
                    if i + 2 < UNITS:
                        scores(i + 2)
                    after(pe, pT_out, c * UNITS + i)
                    after(pe, o_ready, c * UNITS + (i - 2))
                    for br in range(2):
                        for kt in range(qb + 1):
                            t.matmul(PS[:, 6 + par, br * HD:(br + 1) * HD],
                                     pTs[:, par, br * SEQ + kt * P:br * SEQ + (kt + 1) * P],
                                     vsw[:, kt, br, e * HD:(e + 1) * HD], start=kt == 0, stop=kt == qb)
                    t.matmul(PS[:, 6 + par, 2 * HD:3 * HD], pcT[:, e, qb, :], vcmp[:, e * HD:(e + 1) * HD],
                             start=True, stop=True).then_inc(pv_done.sem, 1)
                after(pe, o_ready, c * UNITS + (UNITS - 1))
                for qb in range(TB):
                    i = t.transpose(PS[:, 4, qb * P:(qb + 1) * P], ot[:, qb * P:(qb + 1) * P], ident)
                i.then_inc(oT_done.sem, 1)

            def project_out(layer, w, tb, js):
                for j in js:
                    for c in range(KC):
                        i = t.matmul(PS[:, OUT_BANKS[tb] + j, :], mixT[:, c, tb * P:(tb + 1) * P],
                                     w[:, c, j * 512:(j + 1) * 512], start=c == 0, stop=c == KC - 1)
                if 1 in js:
                    i.then_inc(wo_done.sem, 1)

            def peer(layer):
                U0, R0, S0, B0 = layer * LAYER_UNITS, layer * (LAYER_UNITS + 1), layer * LAYER_SLOTS, layer * (TB + 1)

                def block_transposes(n):
                    after(pe, pxn_ready, n)
                    for c in range(KC):
                        i = t.transpose(PS[:, 2 + c // 4, (c % 4) * P:(c % 4 + 1) * P], XN2[:, c * P:(c + 1) * P],
                                        ident)
                    i.then_inc(pxT_done.sem, 1)

                def route(r, hcol):
                    for c in range(KC):
                        i = t.matmul(PS[:, 4, 0:256], hTb[:, c, :], wq[:, c, ds(hcol * 256, 256)],
                                     start=c == 0, stop=c == KC - 1)
                    i.then_inc(rq_done.sem, 1)
                    after(pe, rq_out, r)
                    for p in range(2):
                        i = t.transpose(PS[:, 5, p * P:(p + 1) * P], q_sb[:, p, :], ident)
                    i.then_inc(rqT_done.sem, 1)
                    after(pe, rqT_out, r)
                    after(pe, rs_out, r - 1)
                    for p in range(2):
                        i = t.matmul(PS[:, 6, p * P:(p + 1) * P], qT_sb[:, p, :],
                                     keysT[:, ds(hcol * 2 + p, 1), :].rearrange("p a b -> p (a b)"),
                                     start=True, stop=True)
                    i.then_inc(rs_done.sem, 1)

                def zero_products(start, stop):
                    for j in range(2):
                        i = t.matmul(PS[:, j, :], ident_z[0:1, P:2 * P], alibi[0:1, :], start=start, stop=stop)
                    return i

                def pair(b, u, hcol, last):
                    for e in range(2):
                        if last and e == 1:
                            block_transposes(b + (B0 + 1))
                            after(pe, pxT_out, b + (B0 + 1))
                            route(u + (e + 1 + R0), 0)
                        else:
                            route(u + (e + 1 + R0), hcol + (e + 1))
                        for k in range(TOPK):
                            after(pe, diag_ready, u * TOPK + (e * TOPK + k + S0))
                            for j in range(2):
                                i = t.matmul(PS[:, j, :], diag[:, k % NBUF, :],
                                             gath[:, k % NBUF, D_MODEL + j * 512:D_MODEL + (j + 1) * 512],
                                             start=False, stop=False)
                            i.then_inc(slot_done.sem, 1)

                w = (w_out_sb, wo_odd)[layer]
                pe.wait_ge(wout_in, 16 * (layer + 1))
                if layer == 0:
                    after(pe, oT_out, 3)
                else:
                    after(pe, ogT_out, C_HEADS - 1)
                project_out(layer, w, 0, (0, 1))
                project_out(layer, w, 1, (0, 1))
                block_transposes(B0)
                after(pe, wo_out, layer * TB)
                project_out(layer, w, 2, (0,))
                pe.wait_ge(wq_in, 32 * (layer + 1))
                after(pe, pxT_out, B0)
                after(pe, wo_out, layer * TB + 1)
                route(R0, 0)
                project_out(layer, w, 2, (1,))
                project_out(layer, w, 3, (0, 1))
                after(pe, wo_out, layer * TB + 3)
                with pe.Fori(0, TB) as b:
                    after(pe, acc_out, b + (layer * TB - 1))
                    zero_products(True, False)
                    with pe.Fori(0, P_HEADS // 2 - 1) as hp:
                        pair(b, b * P_HEADS + hp * 2, hp * 2, False)
                    pair(b, b * P_HEADS + (P_HEADS - 2), P_HEADS - 2, True)
                    zero_products(False, True).then_inc(acc_done.sem, 1)

            peer(0)

            after(pe, acc_out, TB - 1)
            transposes(1)
            after(pe, hT_ready, 2 * TB - 1)

            def projections(W, part, parts):
                todo = [(j, None, c) for c in range(KC) for j in range(2)]
                todo += [(None, tb, c) for tb in range(TB) for c in range(KC)]
                cost = [2 if tb is None else 1 for _, tb, _ in todo]
                last, done = None, 0
                for (j, tb, c), w_ in zip(todo, cost):
                    mine = done * parts // sum(cost) == part
                    done += w_
                    if not mine:
                        continue
                    if tb is None:
                        last = t.matmul(PS[:, j, :], W[:, c, j * P:(j + 1) * P], hT[:, c, :],
                                        start=c == 0, stop=c == KC - 1)
                    else:
                        last = t.matmul(PS[:, 2 + tb // 2, (tb % 2) * 256:(tb % 2 + 1) * 256],
                                        hT[:, c, tb * P:(tb + 1) * P], W[:, c, 256:512],
                                        start=c == 0, stop=c == KC - 1)
                if part == parts - 1:
                    last.then_inc(pr_done.sem, 1)

            FIRST = 3
            SHARES = FIRST + LEVELS + 1 + 4

            def head_pair(hp, final):
                for e in range(2):
                    h = hp * 2 + e
                    W = slab[:, 1 - e, :].rearrange("p (c n) -> p c n", c=KC)
                    more = not (final and e == 1)

                    def share(n):
                        if more:
                            if n == SHARES // 2:
                                after(pe, ig_free, h)
                            projections(W, n, SHARES)

                    if more:
                        reached(pe, slab_in[1 - e], hp * 16 + 16 * (1 + e))
                        after(pe, qk_ready, h)
                    for n in range(FIRST):
                        share(n)
                    for lev in range(LEVELS + 1):
                        after(pe, lv_out, h * (LEVELS + 1) + (lev - 2))
                        if lev < LEVELS:
                            after(pe, qe_ready, h * LEVELS + lev)
                            after(pe, ke_ready, h * LEVELS + lev)
                            q_, k_ = qE[:, lev % 2, :], kE[:, lev % 2, :]
                        else:
                            q_, k_ = qs, kk
                        for tb in range(TB):
                            i = t.matmul(PS[:, 4 + lev % 2, tb * P:(tb + 1) * P], k_[:, tb * P:(tb + 1) * P],
                                         q_[:, tb * P:(tb + 1) * P], start=True, stop=True)
                        i.then_inc(lv_done.sem, 1)
                        share(FIRST + lev)
                    after(pe, kd_ready, h)
                    after(pe, og_ready, h - 1)
                    for tb in range(TB):
                        i = t.transpose(PS[:, 6, tb * P:(tb + 1) * P], kd[:, tb * P:(tb + 1) * P], ident)
                    i.then_inc(kdT_done.sem, 1)
                    share(FIRST + LEVELS + 1)
                    after(pe, kdT_out, h)
                    after(pe, ogT_out, h - 1)
                    for tb in range(TB):
                        i = t.matmul(PS[:, 7, tb * P:(tb + 1) * P], kdT[:, tb * P:(tb + 1) * P],
                                     iS[:, tb * P:(tb + 1) * P], start=True, stop=True)
                    i.then_inc(kv_done.sem, 1)
                    share(FIRST + LEVELS + 2)
                    after(pe, s_ready, h)
                    after(pe, lv_out, h * (LEVELS + 1) + LEVELS)
                    for tb in range(TB):
                        o = PS[:, 6, tb * P:(tb + 1) * P]
                        if tb:
                            t.matmul(o, qd[:, tb * P:(tb + 1) * P], Sst[:, tb - 1, :], start=True, stop=False)
                        i = t.matmul(o, attn[:, tb * P:(tb + 1) * P], iS[:, tb * P:(tb + 1) * P],
                                     start=tb == 0, stop=True)
                    i.then_inc(oi_done.sem, 1)
                    share(FIRST + LEVELS + 3)
                    share(FIRST + LEVELS + 4)
                    after(pe, og_ready, h)
                    for tb in range(TB):
                        i = t.transpose(PS[:, 7, tb * P:(tb + 1) * P], ob[:, tb * P:(tb + 1) * P], ident)
                    i.then_inc(ogT_done.sem, 1)

            reached(pe, slab_in[0], 16)
            projections(slab[:, 0, :].rearrange("p (c n) -> p c n", c=KC), 0, 1)
            with pe.Fori(0, C_HEADS // 2 - 1) as hp:
                head_pair(hp, False)
            head_pair(C_HEADS // 2 - 1, True)
            peer(1)


def kernel(**inputs):
    import numpy as np
    import concourse.bacc as bacc
    from concourse import mybir as mb
    from concourse.bass_utils import run_bass_kernel_spmd as run

    def arr(name):
        return np.asarray(inputs[name])

    def chunks(w):
        return w.reshape(-1, 128, w.shape[-1]).transpose(1, 0, 2)

    we = arr("even_w_in")[0]
    q = we[:, 1024:1536].reshape(1024, 8, 64)
    qpairs = np.stack([q[:, 0:4], q[:, 4:8]], axis=2).reshape(1024, 512)
    kc, vc, ks, vs, kw, vw = (we[:, 1536 + 128 * i:1664 + 128 * i] for i in range(6))
    we = np.concatenate([we[:, 0:1024], vs, vw, we[:, 2304:2328], qpairs, kc, vc, ks, kw], axis=1)

    wo = arr("even_w_out")[0]
    heads = wo[512:].reshape(8, 64, 1024)
    wo = np.concatenate([wo[:512], np.stack([heads[0:4], heads[4:8]], axis=1).reshape(512, 1024)], axis=0)

    def two_positions(w):
        return w.reshape(16, 2, 64, -1).transpose(1, 2, 0, 3).reshape(128, 16, -1)

    odd = arr("odd_w_in")[0].reshape(8, 128, 4, 8, 128)
    odd = odd.transpose(3, 1, 0, 2, 4).reshape(8, 128, 4096)
    data = {
        "x": arr("x")[0],
        "wcol_mix": arr("norm_mix").reshape(2, 8, 128).transpose(2, 0, 1),
        "w_ffn": arr("norm_ffn"),
        "w_fin": arr("final_norm").reshape(1, 1024),
        "w_even": chunks(we),
        "ln_w": arr("gmlp_ln_w"),
        "ws_t": arr("gmlp_w_s")[0].transpose(2, 0, 1),
        "b_s": arr("gmlp_b_s")[0].T,
        "pos": two_positions(arr("nsa_cmp_pos")[0].reshape(2048, 1)).reshape(128, 16),
        "ck1": two_positions(arr("nsa_ck_w1")[0]).reshape(128, 2048),
        "ck2": arr("nsa_ck_w2")[0],
        "cv1": two_positions(arr("nsa_cv_w1")[0]).reshape(128, 2048),
        "cv2": arr("nsa_cv_w2")[0],
        "w_out_e": chunks(wo),
        "w_odd": odd,
        "lbs": arr("hgrn_lower_bounds").reshape(2, 8, 128).transpose(2, 0, 1),
        "hg_w": arr("hgrn_norm_w"),
        "w_out_o": chunks(arr("odd_w_out")[0]),
        "w_q": arr("peer_w_q").reshape(2, 8, 128, 2048).transpose(0, 2, 1, 3),
        "keys": arr("peer_keys").reshape(2, 16, 128, 128).transpose(0, 3, 1, 2),
    }
    for layer in range(2):
        data[f"uv{layer}"] = np.concatenate([arr("peer_u")[layer], arr("peer_v")[layer]], axis=1)

    nc = bacc.Bacc("TRN2", target_bir_lowering=False, num_devices=1)
    arrays, args = {}, {}
    for name, a in data.items():
        a = np.ascontiguousarray(a)
        arrays[f"in_{name}_dram"] = a
        args[name] = nc.dram_tensor(f"in_{name}_dram", a.shape, mb.dt.from_np(a.dtype), kind="ExternalInput").ap()
    args["out"] = nc.dram_tensor("out_0_dram", (512, 1024), mb.dt.float32, kind="ExternalOutput").ap()
    args["uv"] = [args.pop("uv0"), args.pop("uv1")]
    build(nc, **args)
    r = run(nc, [arrays], core_ids=[0])
    return r.results[0]["out_0_dram"].reshape(1, 512, 1024)
```

```python
import concourse.bass as bass
from concourse import mybir
from contextlib import ExitStack

D_MODEL = 1024
SEQ = 512
DEPTH = 2
P = 128
TB = SEQ // P
KC = D_MODEL // P
EPS = 1e-6
NEG = -1e30
A_GROUPS = 4
B_HEADS = 8
HD = 64
CMP_BLOCK = 32
CMP_STRIDE = 16
N_CMP = (SEQ - CMP_BLOCK) // CMP_STRIDE + 1
W_EVEN = 2328
TM_UV = 1024
TM_ALL = 1304
C_HEADS = 8
LEVELS = 7
P_HEADS = 8
TOPK = 16
NKEYS = 128
ROW = 2 * D_MODEL
NBUF = 8
GRP = 4


class Event:

    def __init__(self, sem, prime=2):
        self.sem, self.prime = sem, prime

    def at(self, n):
        return n + self.prime + 1


class Chain:

    def __init__(self, eng, sem):
        self.eng, self.sem, self.n = eng, sem, 0

    def __call__(self, ins):
        self.n += 1
        ins.then_inc(self.sem, 1)
        self.eng.wait_ge(self.sem, self.n)

    def reset(self):
        self.eng.sem_clear(self.sem)
        self.n = 0


def build(nc, x, wcol_mix, w_ffn, w_fin, w_even, ln_w, ws_t, b_s, pos, ck1, ck2, cv1, cv2, w_out_e,
          w_odd, lbs, hg_w, w_out_o, w_q, keys, uv, out):
    fp32 = mybir.dt.float32
    u32 = mybir.dt.uint32
    i32 = mybir.dt.int32
    ALU = mybir.AluOpType
    ACT = mybir.ActivationFunctionType
    AXX = mybir.AxisListType.X
    ds = bass.ds

    with ExitStack() as ctx:
        def sb(name, shape, dt=fp32):
            return ctx.enter_context(nc.sbuf_tensor(name, shape, dt))

        def sem(name):
            return ctx.enter_context(nc.semaphore(name))

        events = []

        def event(name, prime=2):
            e = Event(sem(name), prime)
            events.append(e)
            return e

        RA = sb("region_a", [P, KC * W_EVEN])
        RG = sb("region_g", [P, NBUF * ROW])
        RH = sb("region_h", [P, KC * SEQ])
        RC = sb("region_c", [P, 5632])
        X = sb("x_res", [P, TB + 1, D_MODEL])
        ident_z = sb("ident_z", [P, 2 * P])
        ident = ident_z[:, 0:P]
        alibi = sb("alibi", [P, SEQ])
        level_mask = sb("level_mask", [P, LEVELS + 1, P], i32)
        iota16 = sb("iota16", [P, TOPK])
        scan_keep = alibi
        half = sb("half", [P, 8])
        final_rstd = sb("final_rstd", [P, TB])
        wcol = sb("wcol", [P, DEPTH, KC])
        stat = sb("stat", [P, 8])
        rstd = sb("rstd", [P, 8])
        PS = ctx.enter_context(nc.psum_tensor("ps", [P, 8, 512], fp32))

        def carve(region, at, *shape):
            n = 1
            for s in shape:
                n *= s
            v = region[:, at:at + n]
            if len(shape) == 2:
                v = v.rearrange("p (a b) -> p a b", a=shape[0])
            if len(shape) == 3:
                v = v.rearrange("p (a b c) -> p a b c", a=shape[0], b=shape[1])
            return v

        def taker(region, start=0):
            at = [start]

            def take(*shape):
                n = 1
                for s in shape:
                    n *= s
                v = carve(region, at[0], *shape)
                at[0] += n
                assert at[0] <= region.shape[1], (at[0], region.shape)
                return v
            return take

        hT = carve(RH, 0, KC, SEQ)

        We = carve(RA, 0, KC, W_EVEN)
        tg = taker(RG)
        w_out_sb = tg(KC, D_MODEL)
        mixT = tg(KC, SEQ)
        qT = tg(4, SEQ)
        kcd = tg(2, SEQ)
        vcd = tg(2, SEQ)
        tc = taker(RC)
        xnS = tc(2, D_MODEL)
        kT = tc(2, SEQ)
        vsw = tc(TB, 2, P)
        gates = tc(TB, 24)
        gu = tc(SEQ)
        gv = tc(SEQ)
        kvc = X[:, TB, :].rearrange("p (a b) -> p a b", a=2)
        alibi_c = tc(TB, N_CMP)
        valid_c = tc(TB, N_CMP)
        bs_sb = sb("bs_sb", [P, A_GROUPS])
        mean = sb("mean", [P, 4])
        w2s = sb("w2s", [P, 2, HD])
        pos_sb = sb("pos_sb", [P, CMP_BLOCK // 2])
        posb = sb("posb", [P, 2])
        hid = sb("hid", [P, 2, 2 * N_CMP])
        kcmp = sb("kcmp", [P, N_CMP])
        vcmp = sb("vcmp", [N_CMP, 2 * HD])
        slope = sb("slope", [P, 2])
        gst = sb("gst", [P, TB, 2, 3])
        nmax = sb("nmax", [P, 2, 2])
        sums = sb("sums", [P, 2, 2])
        coef = sb("coef", [P, 2])
        cmax = sb("cmax", [P, 2, TB])
        csum = sb("csum", [P, 2, TB])
        ws_sb = carve(RG, 8192 + 4 * SEQ, 4, P)
        lnw = carve(RG, 8192 + 5 * SEQ, SEQ)
        gsq = carve(RG, 8192 + 6 * SEQ, SEQ)
        gvn = carve(RG, 8192 + 7 * SEQ, SEQ)
        w1 = carve(RG, 0, 2, CMP_BLOCK // 2 * P)
        zs = carve(RH, 0, 2, 2 * SEQ)
        ps_ = carve(RH, 4 * SEQ, 2, 2 * SEQ)
        pTs = carve(RC, 0, 2, 2 * SEQ)
        pcT = X[0:N_CMP, TB, :].rearrange("p (a b c) -> p a b c", a=2, b=TB)
        pc = carve(RG, 8192 + KC * SEQ + 4 * SEQ, 2, TB, N_CMP)
        qst = gu
        ot = gv

        slab = carve(RG, 0, 2, KC * 512)
        wo_odd = carve(RG, 0, KC, D_MODEL)
        og = taker(RG, 8192 + KC * SEQ)
        qs, kk, bb, fg, gs, iS, sigm, ob = (og(SEQ) for _ in range(8))
        oc2 = taker(RC)
        dE = oc2(2, SEQ)
        qE = oc2(2, SEQ)
        kE = oc2(2, SEQ)
        attn = oc2(SEQ)
        kdT = oc2(SEQ)
        qd = oc2(SEQ)
        kd = oc2(SEQ)
        eb = oc2(SEQ)
        Sst = sb("state", [P, TB - 1, P])
        hgw = X[:, TB, :]
        lb = sb("lb", [P, 2, 8])
        lbst = sb("lbst", [P, 2, 2])
        lbraw = sb("lbraw", [P, 2, 8])

        wq = carve(RA, 0, KC, 2 * D_MODEL)
        keysT = carve(RA, KC * 2 * D_MODEL, 2 * P_HEADS, NKEYS)
        gath = carve(RG, 0, NBUF, ROW)
        th = taker(RH)
        XN = th(D_MODEL)
        XN2 = th(D_MODEL)
        hTb = th(KC, P)
        wrow = th(D_MODEL)
        tp = taker(RC)
        diag = tp(NBUF, P)
        q_sb = tp(2, P)
        qT_sb = tp(2, P)
        s1 = tp(2, P)
        s2 = tp(2, P)
        cand = tp(2 * P)
        cand2 = tp(2 * P)
        oneh = tp(2, TOPK, TOPK)
        vtop = tp(2, TOPK)
        itop = tp(2, TOPK).bitcast(u32)
        itopf = tp(2, TOPK)
        best = tp(TOPK)
        bpos = tp(TOPK).bitcast(u32)
        bij = tp(2, TOPK).bitcast(u32)
        bijf = tp(2, TOPK)
        esel = tp(2, TOPK)
        experts = sb("experts", [P, 2 * TOPK], u32)
        gexp = tp(TOPK)
        gate = sb("gate", [P, 2, TOPK])
        gstat = sb("gstat", [P, 4])
        dots = tp(2 * TOPK)
        gact = tp(2 * TOPK)
        wts = tp(2 * TOPK)
        rsb = sb("rsb", [P, 1])
        wfin = level_mask[:].rearrange("p a b -> p (a b)").bitcast(fp32)

        primed = sem("primed")
        consts = sem("consts")
        pool_chain, dve_chain, act_chain = sem("pool_chain"), sem("dve_chain"), sem("act_chain")
        half_set = sem("half_set")
        x_in = [sem(f"x_in{tb}") for tb in range(TB)]
        fm_in, tm_in, wcol_in = sem("fm_in"), sem("tm_in"), sem("wcol_in")
        small_in, w1_in, wout_in = sem("small_in"), sem("w1_in"), sem("wout_in")
        dup_in = sem("dup_in")
        wq_in, ffn_in, lb_in = sem("wq_in"), sem("ffn_in"), sem("lb_in")
        slab_in = [sem("slab_in0"), sem("slab_in1")]
        fin_in, stored = sem("fin_in"), sem("stored")
        xss_ready, xrs_ready = event("xss_ready"), event("xrs_ready")
        ss_ready, rs_ready = event("ss_ready"), event("rs_ready")
        xn_ready, xT_done, hT_ready = event("xn_ready"), event("xT_done"), event("hT_ready")
        fm_done, fm_out = event("fm_done"), event("fm_out")
        tv_done, v_out = event("tv_done"), event("v_out")
        tm_done, uv_out, vsw_out = event("tm_done"), event("uv_out"), event("vsw_out")
        ln_ss, ln_rs, ln_done = event("ln_ss"), event("ln_rs"), event("ln_done")
        mix_done, a_ready, aT_done, aT_out = event("mix_done"), event("a_ready"), event("aT_done"), event("aT_out")
        posb_done, posb_out, hid_done, hid_out, cmp_done, cmp_out = (
            event(n) for n in ("posb_done", "posb_out", "hid_done", "hid_out", "cmp_done", "cmp_out"))
        q_staged, gate_sig = event("q_staged"), event("gate_sig")
        sc_done, z_ready, ec_ready, pc_ready, p_ready, pT_done, pT_out, pv_done, o_ready = (
            event(n) for n in ("sc_done", "z_ready", "ec_ready", "pc_ready", "p_ready", "pT_done", "pT_out",
                               "pv_done", "o_ready"))
        oT_done, oT_out = event("oT_done"), event("oT_out")
        cs_done, pcT_done, pcT_out = event("cs_done"), event("pcT_done"), event("pcT_out")
        wo_done, wo_out = event("wo_done"), event("wo_out")
        pr_done = event("pr_done")
        sig_ready, fg_ready, lf_ready, dd_ready, e_ready, qe_ready, ke_ready, lv_out = (
            event(n) for n in ("sig_ready", "fg_ready", "lf_ready", "dd_ready", "e_ready", "qe_ready",
                               "ke_ready", "lv_out"))
        lv_done = event("lv_done", 4)
        og_final = event("og_final")
        i_out, kds_ready, ebe_ready, kd_ready, kdT_done, kdT_out, kv_done, s_ready, oi_done, osq_ready = (
            event(n) for n in ("i_out", "kds_ready", "ebe_ready", "kd_ready", "kdT_done", "kdT_out", "kv_done",
                               "s_ready", "oi_done", "osq_ready"))
        oss_ready, ors_ready, og_ready, ogT_done, ogT_out = (
            event(n) for n in ("oss_ready", "ors_ready", "og_ready", "ogT_done", "ogT_out"))
        qk_ready, ig_free = event("qk_ready"), event("ig_free")
        pxn_ready, pxT_done, pxT_out = event("pxn_ready"), event("pxT_done"), event("pxT_out")
        rq_done, rq_out, rqT_done, rqT_out, rs_done, rs_out = (
            event(n) for n in ("rq_done", "rq_out", "rqT_done", "rqT_out", "rs_done", "rs_out"))
        routed, gexp_in, gexp_out = event("routed"), event("gexp_in"), event("gexp_out")
        dots_ready, gelu_ready, w_ready, diag_ready = (
            event(n) for n in ("dots_ready", "gelu_ready", "w_ready", "diag_ready"))
        slot_done = event("slot_done", NBUF)
        acc_done, acc_out = event("acc_done"), event("acc_out")
        gathered = [sem(f"gathered{i}") for i in range(NBUF)]

        block = ctx.enter_context(nc.Block())

        def after(eng, ev, n):
            v = ev.at(n)
            if isinstance(v, int):
                eng.wait_ge(ev.sem, v)
            else:
                r = eng.to_reg(v)
                eng.wait_ge(primed, 1)
                eng.wait_ge(ev.sem, r)

        def reached(eng, s, v):
            if isinstance(v, int):
                eng.wait_ge(s, v)
            else:
                r = eng.to_reg(v)
                eng.wait_ge(primed, 1)
                eng.wait_ge(s, r)

        def bc(ap, n):
            shape = list(ap.shape)
            return ap.unsqueeze(len(shape)).broadcast_to(shape + [n])

        def bmid(ap, n):
            return ap.unsqueeze(1).broadcast_to([ap.shape[0], n, ap.shape[1]])

        def v3(ap, a):
            return ap.rearrange("p (a b) -> p a b", a=a)

        UNITS = 8

        def unit(i):
            return i // 2, i % 2

        OUT_BANKS = (0, 6, 0, 2)
        LAYER_SLOTS = TB * P_HEADS * TOPK
        LAYER_UNITS = TB * P_HEADS

        @block.sync
        def _(sp):
            for e in events:
                sp.sem_inc(e.sem, e.prime)
            sp.sem_inc(primed, 1)
            for tb in range(TB):
                sp.dma_start(X[:, tb, :], x[tb * P:(tb + 1) * P, :]).then_inc(x_in[tb], 16)
            sp.dma_start(wcol[:], wcol_mix).then_inc(wcol_in, 16)
            sp.dma_start(We[:, :, TM_ALL:W_EVEN], w_even[:, :, TM_ALL:W_EVEN]).then_inc(fm_in, 16)
            sp.dma_start(bs_sb[:], b_s).then_inc(small_in, 16)
            sp.dma_start(lnw, ln_w.partition_broadcast(P)).then_inc(small_in, 16)
            sp.dma_start(ws_sb, ws_t).then_inc(small_in, 16)
            sp.dma_start(pos_sb[:], pos).then_inc(small_in, 16)
            sp.dma_start(w2s[:, 0, :], ck2).then_inc(small_in, 16)
            sp.dma_start(w2s[:, 1, :], cv2).then_inc(small_in, 16)
            sp.dma_start(lbraw[:], lbs).then_inc(small_in, 16)
            sp.dma_start(We[:, :, 0:TM_ALL], w_even[:, :, 0:TM_ALL]).then_inc(tm_in, 16)
            sp.dma_start(w1[:, 0, :], ck1).then_inc(w1_in, 16)
            sp.dma_start(w1[:, 1, :], cv1).then_inc(w1_in, 16)
            sp.wait_ge(fm_out.sem, fm_out.at(7))
            for kv, dst in ((0, kcd), (1, vcd)):
                for g in range(2):
                    src = kvc[g * HD:(g + 1) * HD, kv, :]
                    sp.dma_start(dst[0:HD, g, :], src).then_inc(dup_in, 16)
                    sp.dma_start(dst[HD:P, g, 0:SEQ - 1], src[:, 1:SEQ]).then_inc(dup_in, 16)
            sp.wait_ge(hid_done.sem, hid_done.at(0))
            sp.dma_start(w_out_sb, w_out_e).then_inc(wout_in, 16)
            sp.wait_ge(tm_done.sem, tm_done.at(TB - 1))
            sp.dma_start(wq, w_q[0]).then_inc(wq_in, 16)
            sp.dma_start(keysT, keys[0]).then_inc(wq_in, 16)
            sp.wait_ge(oT_out.sem, oT_out.at(3))
            sp.dma_start(wrow, w_ffn[0:1, :].partition_broadcast(P)).then_inc(ffn_in, 16)
            sp.wait_ge(acc_out.sem, acc_out.at(TB - 1))
            sp.dma_start(slab[:, 0, :], w_odd[0]).then_inc(slab_in[0], 16)
            sp.dma_start(hgw, hg_w.partition_broadcast(P)).then_inc(lb_in, 16)
            sp.dma_start(slab[:, 1, :], w_odd[1]).then_inc(slab_in[1], 16)
            sp.dma_start(wq, w_q[1]).then_inc(wq_in, 16)
            sp.dma_start(keysT, keys[1]).then_inc(wq_in, 16)
            with sp.Fori(0, C_HEADS // 2 - 1) as hp:
                for e in range(2):
                    after(sp, pr_done, hp * 2 + e)
                    sp.dma_start(slab[:, e, :], w_odd[ds(hp * 2 + (e + 2), 1)].rearrange("o p n -> (o p) n")
                                 ).then_inc(slab_in[e], 16)
            sp.wait_ge(pr_done.sem, pr_done.at(C_HEADS - 1))
            sp.dma_start(wo_odd, w_out_o).then_inc(wout_in, 16)
            sp.dma_start(wrow, w_ffn[1:2, :].partition_broadcast(P)).then_inc(ffn_in, 16)
            sp.wait_ge(ogT_out.sem, ogT_out.at(C_HEADS - 1))
            sp.dma_start(wfin, w_fin.partition_broadcast(P)).then_inc(fin_in, 16)
            for b in range(TB):
                sp.wait_ge(og_final.sem, og_final.at(b))
                sp.dma_start(out[b * P:(b + 1) * P, :], X[:, b, :]).then_inc(stored, 16)
            sp.wait_ge(stored, 16 * TB)

        @block.gpsimd
        def _(pool):
            g = nc.gpsimd
            link = Chain(pool, pool_chain)
            pool.wait_ge(primed, 1)
            link(g.memset(half[:], -0.5))
            link(g.memset(ident_z[:], 0.0))
            link(g.affine_select(out=ident, in_=ident, compare_op=ALU.not_equal, fill=1.0, base=0,
                                 pattern=[[-1, P]], channel_multiplier=1))
            pool.sem_inc(half_set, 1)

            def inverse_root(src, dst, n, count):
                link(g.tensor_scalar(dst, src, 1.0 / count, EPS, ALU.mult, ALU.add))
                link(g.tensor_tensor(dst, dst, half[:, 0:n], ALU.pow))

            for tb in range(TB):
                pool.wait_ge(xss_ready.sem, xss_ready.at(tb))
                inverse_root(stat[:, tb:tb + 1], rstd[:, tb:tb + 1], 1, D_MODEL)
                pool.sem_inc(xrs_ready.sem, 1)
            link(g.iota(alibi[:], [[1, SEQ]], base=-(SEQ - P), channel_multiplier=-1,
                        allow_small_or_imprecise_dtypes=True))
            link(g.affine_select(out=alibi[:], in_=alibi[:], compare_op=ALU.is_ge, fill=NEG, base=SEQ - P,
                                 pattern=[[-1, SEQ]], channel_multiplier=1))
            link(g.iota(alibi_c, [[-P, TB], [CMP_STRIDE, N_CMP]], base=CMP_BLOCK - 1, channel_multiplier=-1,
                        allow_small_or_imprecise_dtypes=True))
            link(g.affine_select(out=alibi_c, in_=alibi_c, compare_op=ALU.is_ge, fill=NEG,
                                 base=-(CMP_BLOCK - 1), pattern=[[P, TB], [-CMP_STRIDE, N_CMP]],
                                 channel_multiplier=1))
            link(g.memset(valid_c, 1.0))
            link(g.affine_select(out=valid_c, in_=valid_c, compare_op=ALU.is_ge, fill=0.0,
                                 base=-(CMP_BLOCK - 1), pattern=[[P, TB], [-CMP_STRIDE, N_CMP]],
                                 channel_multiplier=1))
            link(g.iota(iota16[:], [[1, TOPK]], base=0, channel_multiplier=0,
                        allow_small_or_imprecise_dtypes=True))
            link(g.memset(level_mask[:], 1))
            for lev in range(LEVELS):
                n = 1 << lev
                m = level_mask[:, lev, :].rearrange("p (b h l) -> p b h l", h=2, l=n)
                link(g.affine_select(out=m, in_=m, compare_op=ALU.is_ge, fill=0.0, base=0,
                                     pattern=[[-2 * n, P // (2 * n)], [0, 2], [0, n]], channel_multiplier=1))
                link(g.affine_select(out=m, in_=m, compare_op=ALU.is_ge, fill=0.0, base=n - 1,
                                     pattern=[[2 * n, P // (2 * n)], [0, 2], [0, n]], channel_multiplier=-1))
                link(g.memset(m[:, :, 0, :], 0))
            d = level_mask[:, LEVELS, :]
            link(g.affine_select(out=d, in_=d, compare_op=ALU.is_equal, fill=0.0, base=0,
                                 pattern=[[-1, P]], channel_multiplier=1))
            pool.wait_ge(small_in, 16 * 7)
            link(g.affine_select(out=ws_sb, in_=ws_sb, compare_op=ALU.is_ge, fill=0.0, base=0,
                                 pattern=[[0, A_GROUPS], [1, P]], channel_multiplier=-1))
            pool.sem_inc(consts, 1)

            for tb in range(TB):
                pool.wait_ge(ln_ss.sem, ln_ss.at(tb))
                inverse_root(mean[:], rstd[:, 4:8], 4, P)
                pool.sem_inc(ln_rs.sem, 1)

            def peer(layer):
                pool.wait_ge(ss_ready.sem, ss_ready.at(4 * layer))
                inverse_root(stat[:, 0:1], rstd[:, 0:1], 1, D_MODEL)
                pool.sem_inc(rs_ready.sem, 1)
                tab = uv[layer]

                def gathers(up):
                    for e in range(2):
                        after(pool, routed, up * 2 + (e + layer * (LAYER_UNITS + 1)))
                        for k in range(TOPK):
                            after(pool, slot_done, up * (2 * TOPK) + (e * TOPK + k - NBUF + layer * LAYER_SLOTS))
                            g.indirect_dma_start(
                                out=gath[:, k % NBUF, :], out_offset=None, in_=tab,
                                in_offset=bass.IndirectOffsetOnAxis(
                                    ap=experts[:, e * TOPK + k:e * TOPK + k + 1], axis=0),
                            ).then_inc(gathered[k % NBUF], 16)

                pool.wait_ge(wo_done.sem, wo_done.at(layer * TB + TB - 1))
                gathers(0)
                pool.wait_ge(ss_ready.sem, ss_ready.at(4 * layer + 1))
                inverse_root(stat[:, 1:TB], rstd[:, 1:TB], TB - 1, D_MODEL)
                pool.sem_inc(rs_ready.sem, 1)
                with pool.Fori(1, LAYER_UNITS // 2) as up:
                    gathers(up)

            peer(0)

            pool.wait_ge(ss_ready.sem, ss_ready.at(3))
            inverse_root(stat[:, 0:TB], rstd[:, 0:TB], TB, D_MODEL)
            pool.sem_inc(rs_ready.sem, 1)
            link.reset()
            with pool.Fori(0, C_HEADS) as h:
                for lev in range(LEVELS):
                    n = 1 << lev
                    after(pool, e_ready, h * LEVELS + lev)
                    after(pool, lv_done, h * (LEVELS + 1) + (-2, -3)[lev] if lev < 2 else h * (LEVELS + 1) + (lev - 2))
                    left = "p (b h l) -> p b h l"
                    o_ = kE[:, lev % 2, :].rearrange(left, h=2, l=n)[:, :, 0, :]
                    k_ = kk.rearrange(left, h=2, l=n)[:, :, 0, :]
                    e_ = dE[:, lev % 2, :].rearrange(left, h=2, l=n)[:, :, 0, :]
                    g.tensor_tensor(o_, k_, e_, ALU.mult).then_inc(ke_ready.sem, 1)
                after(pool, oss_ready, h)
                inverse_root(mean[:], rstd[:, 4:8], 4, P)
                pool.sem_inc(ors_ready.sem, 1)
                link.reset()

            peer(1)
            for mark, (b0, b1) in enumerate(((0, TB - 1), (TB - 1, TB))):
                pool.wait_ge(ss_ready.sem, ss_ready.at(6 + mark))
                inverse_root(stat[:, b0:b1], final_rstd[:, b0:b1], b1 - b0, D_MODEL)
                pool.sem_inc(rs_ready.sem, 1)

        @block.scalar
        def _(act):
            a = nc.scalar
            link = Chain(act, act_chain)
            act.wait_ge(primed, 1)
            act.wait_ge(small_in, 16 * 7)
            for ch in range(8):
                act.wait_ge(fm_done.sem, fm_done.at(ch))
                dst = qT[:, ch, :] if ch < 4 else (kvc[:, ch - 4, :] if ch < 6 else kT[:, ch - 6, :])
                a.activation(dst, PS[:, 6 + ch % 2, :], ACT.Copy).then_inc(fm_out.sem, 1)
            def gmlp_out(tb):
                act.wait_ge(aT_done.sem, aT_done.at(tb))
                a.activation(mixT[:, 0:4, tb * P:(tb + 1) * P], v3(PS[:, 7, :], 4), ACT.Copy).then_inc(aT_out.sem, 1)

            for tb in range(TB):
                act.wait_ge(tv_done.sem, tv_done.at(tb))
                act.wait_ge(ln_done.sem, ln_done.at(tb - 1))
                a.activation(gv, PS[:, 3 * (tb % 2) + 1, :], ACT.Gelu_apprx_tanh).then_inc(v_out.sem, 1)
                if tb:
                    gmlp_out(tb - 1)
                act.wait_ge(tm_done.sem, tm_done.at(tb))
                act.wait_ge(a_ready.sem, a_ready.at(tb - 1))
                a.activation(gu, PS[:, 3 * (tb % 2), :], ACT.Gelu_apprx_tanh).then_inc(uv_out.sem, 1)
                a.activation(vsw[:, tb, :, :], PS[:, 3 * (tb % 2) + 2, 0:256].rearrange("p (a b) -> p a b", a=2),
                             ACT.Copy)
                a.activation(gates[:, tb, :], PS[:, 3 * (tb % 2) + 2, 256:280], ACT.Copy).then_inc(vsw_out.sem, 1)
                if tb == 0:
                    act.wait_ge(posb_done.sem, posb_done.at(0))
                    link(a.activation(posb[:], PS[:, 6, 0:2], ACT.Copy))
                    act.wait_ge(hid_done.sem, hid_done.at(0))
                    for kv in range(2):
                        i = a.activation(hid[:, kv, :], PS[:, 7, kv * 64:kv * 64 + 2 * N_CMP], ACT.Gelu_apprx_tanh,
                                         bias=posb[:, kv:kv + 1])
                    i.then_inc(hid_out.sem, 1)
                    act.wait_ge(cmp_done.sem, cmp_done.at(0))
                    a.activation(kcmp[:], PS[:, 3, 0:N_CMP], ACT.Copy)
                    a.activation(vcmp[:], PS[0:N_CMP, 4, 0:2 * HD], ACT.Copy).then_inc(cmp_out.sem, 1)
            act.wait_ge(vsw_out.sem, vsw_out.at(TB - 1))
            link(a.activation(gates.rearrange("p a b -> p (a b)"), gates.rearrange("p a b -> p (a b)"), ACT.Sigmoid))
            act.sem_inc(gate_sig.sem, 1)
            gmlp_out(TB - 1)
            with act.Fori(0, 4) as c:
                after(act, sc_done, c * UNITS - 1)
                i = a.activation(qst, qT[:, ds(c, 1), :].rearrange("p a b -> p (a b)"), ACT.Copy)
                i.then_inc(q_staged.sem, 1)

                after(act, z_ready, c * (UNITS + 1))
                a.activation(pc.rearrange("p a b c -> p (a b c)"), pc.rearrange("p a b c -> p (a b c)"), ACT.Exp,
                             scale=0.125).then_inc(ec_ready.sem, 1)

                def exps(i):
                    qb, e = unit(i)
                    par, nk = i % 2, (qb + 1) * P
                    after(act, z_ready, c * (UNITS + 1) + (i + 1))
                    after(act, pT_done, c * UNITS + (i - 2))
                    for br in range(2):
                        last = a.activation(ps_[:, par, br * SEQ:br * SEQ + nk], zs[:, par, br * SEQ:br * SEQ + nk],
                                            ACT.Exp, bias=nmax[:, par, br:br + 1], scale=0.125,
                                            accum_out=sums[:, par, br:br + 1])
                    last.then_inc(p_ready.sem, 1)

                exps(0)
                after(act, pcT_done, c)
                a.activation(pcT[:, :, :, :].rearrange("p a b c -> p a (b c)"),
                             PS[0:N_CMP, 6:8, :], ACT.Copy).then_inc(pcT_out.sem, 1)
                for i in range(UNITS):
                    qb, e = unit(i)
                    par, nk = i % 2, (qb + 1) * P
                    after(act, pT_done, c * UNITS + i)
                    after(act, pv_done, c * UNITS + (i - 2))
                    a.activation(pTs[:, par, :].rearrange("p (a b) -> p a b", a=2)[:, :, 0:nk], PS[:, 4:6, 0:nk],
                                 ACT.Copy).then_inc(pT_out.sem, 1)
                    if i + 1 < UNITS:
                        exps(i + 1)
                after(act, oT_done, c)
                a.activation(mixT[:, ds(c + 4, 1), :].rearrange("p a b -> p (a b)"), PS[:, 4, :],
                             ACT.Copy).then_inc(oT_out.sem, 1)

            def peer(layer):
                U0, S0, B0 = layer * LAYER_UNITS, layer * LAYER_SLOTS, layer * (TB + 1)
                Q0, R0 = layer * (LAYER_UNITS + 2), layer * (LAYER_UNITS + 1)
                G0 = S0 // GRP

                def route(r):
                    after(act, rq_done, r)
                    a.activation(q_sb, v3(PS[:, 4, 0:256], 2), ACT.Copy).then_inc(rq_out.sem, 1)
                    after(act, rqT_done, r)
                    a.activation(qT_sb, v3(PS[:, 5, 0:256], 2), ACT.Copy).then_inc(rqT_out.sem, 1)

                def soft(r):
                    after(act, gexp_in, r)
                    a.activation(gexp, best, ACT.Exp, bias=gstat[:, 0:1],
                                 accum_out=gstat[:, 1:2]).then_inc(gexp_out.sem, 1)

                def diags(e, grp_index, slot_index, grp):
                    after(act, w_ready, grp_index)
                    for k in range(grp * GRP, grp * GRP + GRP):
                        after(act, slot_done, slot_index + (k - NBUF))
                        a.activation(diag[:, k % NBUF, :], ident, ACT.Copy,
                                     scale=wts[:, e * TOPK + k:e * TOPK + k + 1]).then_inc(diag_ready.sem, 1)

                act.wait_ge(pxT_done.sem, pxT_done.at(B0))
                for j in range(2):
                    i = a.activation(hTb[:, 4 * j:4 * j + 4, :], v3(PS[:, 2 + j, :], 4), ACT.Copy)
                i.then_inc(pxT_out.sem, 1)
                route(Q0)
                soft(R0)
                route(Q0 + 1)

                def pair(b, u, first, last):
                    for e in range(2):
                        if last and e == 1:
                            after(act, pxT_done, b + (B0 + 1))
                            after(act, rq_done, u + (Q0 + 1))
                            for j in range(2):
                                i = a.activation(hTb[:, 4 * j:4 * j + 4, :], v3(PS[:, 2 + j, :], 4), ACT.Copy)
                            i.then_inc(pxT_out.sem, 1)
                        if not (first and e == 0):
                            route(u + (e + 1 + Q0))
                        for grp in range(TOPK // GRP):
                            gi = u * (TOPK // GRP) + (e * (TOPK // GRP) + grp + G0)
                            after(act, dots_ready, gi)
                            q0 = e * TOPK + grp * GRP
                            a.activation(gact[:, q0:q0 + GRP], dots[:, q0:q0 + GRP], ACT.Gelu_apprx_tanh
                                         ).then_inc(gelu_ready.sem, 1)
                            diags(e, gi, u * TOPK + (e * TOPK + S0), grp)
                            if grp == 1:
                                soft(u + (e + 1 + R0))
                            if last and e == 1 and grp == 1:
                                route(u + (3 + Q0))

                with act.Fori(0, TB) as b:
                    pair(b, b * P_HEADS, True, False)
                    with act.Fori(1, P_HEADS // 2 - 1) as hp:
                        pair(b, b * P_HEADS + hp * 2, False, False)
                    pair(b, b * P_HEADS + (P_HEADS - 2), False, True)

            peer(0)

            link.reset()
            link(a.activation(lb[:, 0, :], lb[:, 1, :], ACT.Sigmoid))
            act.sem_inc(lf_ready.sem, 1)
            def sigmoids(h):
                after(act, pr_done, h)
                a.activation(sigm, PS[:, 1, :], ACT.Sigmoid)
                a.activation(dE[:, 0, :], PS[:, 0, :], ACT.Sigmoid).then_inc(sig_ready.sem, 1)
                gi = PS[:, 2:4, :].rearrange("p a (b c) -> p (a b) c", b=2)
                a.activation(v3(iS, 4), gi[:, :, 0:P], ACT.Copy)
                a.activation(v3(dE[:, 1, :], 4), gi[:, :, P:2 * P], ACT.Sigmoid).then_inc(i_out.sem, 1)

            def head_pair(hp, final):
                for e in range(2):
                    h = hp * 2 + e
                    after(act, fg_ready, h)
                    a.activation(bb, fg, ACT.Ln).then_inc(lf_ready.sem, 1)
                    for lev in range(LEVELS):
                        after(act, dd_ready, h * LEVELS + lev)
                        a.activation(dE[:, lev % 2, :], dE[:, lev % 2, :], ACT.Exp).then_inc(e_ready.sem, 1)
                    after(act, kds_ready, h)
                    a.activation(eb, bb, ACT.Exp)
                    a.activation(kd, kd, ACT.Exp).then_inc(ebe_ready.sem, 1)
                    after(act, kdT_done, h)
                    a.activation(kdT, PS[:, 6, :], ACT.Copy).then_inc(kdT_out.sem, 1)
                    after(act, oi_done, h)
                    a.activation(v3(eb, 4), v3(PS[:, 6, :], 4), ACT.Square).then_inc(osq_ready.sem, 1)
                    if not (final and e == 1):
                        sigmoids(h + 1)
                    after(act, ogT_done, h)
                    a.activation(mixT[:, ds(h, 1), :].rearrange("p a b -> p (a b)"), PS[:, 7, :],
                                 ACT.Copy).then_inc(ogT_out.sem, 1)

            sigmoids(0)
            with act.Fori(0, C_HEADS // 2 - 1) as hp:
                head_pair(hp, False)
            head_pair(C_HEADS // 2 - 1, True)

            peer(1)

        @block.vector
        def _(dve):
            v = nc.vector
            link = Chain(dve, dve_chain)
            dve.wait_ge(primed, 1)
            link(v.memset(slope[:, 0:1], 4.0))
            link(v.memset(slope[:, 1:2], 0.25))

            def normed_transposed(layer):
                dve.wait_ge(half_set, 1)
                for tb in range(TB):
                    n = layer * TB + tb
                    if layer == 0:
                        dve.wait_ge(xrs_ready.sem, xrs_ready.at(tb))
                    dve.wait_ge(xT_done.sem, xT_done.at(n - 2))
                    v.tensor_scalar(xnS[:, tb % 2, :], X[:, tb, :], rstd[:, tb:tb + 1], None, ALU.mult
                                    ).then_inc(xn_ready.sem, 1)
                    dve.wait_ge(xT_done.sem, xT_done.at(n))
                    v.tensor_tensor(hT[:, :, tb * P:(tb + 1) * P],
                                    PS[:, 0:2, :].rearrange("p a (b c) -> p (a b) c", b=4),
                                    bc(wcol[:, layer, :], P), ALU.mult).then_inc(hT_ready.sem, 1)

            for tb in range(TB):
                dve.wait_ge(x_in[tb], 16)
                link(v.tensor_tensor_reduce(out=xnS[:, tb % 2, :], in0=X[:, tb, :], in1=X[:, tb, :], scale=1.0,
                                            scalar=0.0, op0=ALU.mult, op1=ALU.add, accum_out=stat[:, tb:tb + 1]))
                dve.sem_inc(xss_ready.sem, 1)
            dve.wait_ge(wcol_in, 16)
            normed_transposed(0)
            dve.wait_ge(small_in, 16 * 7)
            link(v.tensor_tensor(lb[:, 1, :], lbraw[:, 1, :], lbraw[:, 0, :], ALU.subtract))
            dve.wait_ge(consts, 1)
            for tb in range(TB):
                dve.wait_ge(v_out.sem, v_out.at(tb))
                dve.wait_ge(mix_done.sem, mix_done.at(tb - 1))
                link(v.tensor_reduce(mean[:], v3(gv, 4), AXX, ALU.add))
                link(v.tensor_scalar(mean[:], mean[:], 1.0 / P, None, ALU.mult))
                link(v.tensor_tensor(v3(gvn, 4), v3(gv, 4), bc(mean[:], P), ALU.subtract))
                link(v.tensor_tensor(gsq, gvn, gvn, ALU.mult))
                link(v.tensor_reduce(mean[:], v3(gsq, 4), AXX, ALU.add))
                dve.sem_inc(ln_ss.sem, 1)
                link(v.tensor_tensor(gvn, gvn, lnw, ALU.mult))
                dve.wait_ge(ln_rs.sem, ln_rs.at(tb))
                v.tensor_tensor(v3(gvn, 4), v3(gvn, 4), bc(rstd[:, 4:8], P), ALU.mult).then_inc(ln_done.sem, 1)
                dve.wait_ge(mix_done.sem, mix_done.at(tb))
                dve.wait_ge(uv_out.sem, uv_out.at(tb))
                for gr in range(A_GROUPS):
                    last = v.scalar_tensor_tensor(gsq[:, gr * P:(gr + 1) * P], PS[:, 6, gr * P:(gr + 1) * P],
                                                  bs_sb[:, gr:gr + 1], gu[:, gr * P:(gr + 1) * P], ALU.add, ALU.mult)
                last.then_inc(a_ready.sem, 1)
                dve.wait_ge(aT_done.sem, aT_done.at(tb))
            link.reset()
            dve.wait_ge(gate_sig.sem, gate_sig.at(0))
            gview = gates.rearrange("p b (e c r) -> p b e c r", e=2, c=4)
            with dve.Fori(0, 4) as c:
                for e in range(2):
                    link(v.tensor_copy(gst[:, :, e, :], gates[:, :, ds(c * 3 + 12 * e, 3)]))
                after(dve, cs_done, c)
                for e in range(2):
                    link(v.scalar_tensor_tensor(pc[:, e, :, :], alibi_c, slope[:, e:e + 1],
                                                PS[:, 4 + e, 0:TB * N_CMP].rearrange("p (a b) -> p a b", a=TB),
                                                ALU.mult, ALU.add))
                pc3 = pc.rearrange("p a b c -> p (a b) c")
                cm, cs = cmax[:].rearrange("p a b -> p (a b)"), csum[:].rearrange("p a b -> p (a b)")
                link(v.tensor_reduce(cm, pc3, AXX, ALU.max))
                link(v.tensor_tensor(pc3, pc3, bc(cm, N_CMP), ALU.subtract))
                dve.sem_inc(z_ready.sem, 1)

                def biased(i):
                    qb, e = unit(i)
                    par, nk = i % 2, (qb + 1) * P
                    after(dve, sc_done, c * UNITS + i)
                    after(dve, p_ready, c * UNITS + (i - 2))
                    z = zs[:, par, :].rearrange("p (a b) -> p a b", a=2)[:, :, 0:nk]
                    link(v.scalar_tensor_tensor(z, bmid(alibi[:, SEQ - nk:SEQ], 2), slope[:, e:e + 1],
                                                PS[:, 2 * par:2 * par + 2, 0:nk], ALU.mult, ALU.add))
                    link(v.tensor_reduce(nmax[:, par, :], z, AXX, ALU.max))
                    link(v.tensor_scalar(nmax[:, par, :], nmax[:, par, :], -0.125, None, ALU.mult))
                    dve.sem_inc(z_ready.sem, 1)

                def combine(i):
                    qb, e = unit(i)
                    par = i % 2
                    after(dve, p_ready, c * UNITS + i)
                    link(v.reciprocal(coef[:], sums[:, par, :]))
                    link(v.tensor_tensor(coef[:], coef[:], gst[:, qb, e, 1:3], ALU.mult))
                    after(dve, pv_done, c * UNITS + i)
                    o = v3(ot, 4)[:, qb, e * HD:(e + 1) * HD]
                    pv = PS[:, 6 + par, 0:192].rearrange("p (a b) -> p a b", a=3)
                    link(v.tensor_scalar(o, pv[:, 0, :], coef[:, 0:1], None, ALU.mult))
                    link(v.scalar_tensor_tensor(o, pv[:, 1, :], coef[:, 1:2], o, ALU.mult, ALU.add))
                    link(v.scalar_tensor_tensor(o, pv[:, 2, :], csum[:, e, qb:qb + 1], o, ALU.mult, ALU.add))
                    dve.sem_inc(o_ready.sem, 1)

                after(dve, oT_done, c - 1)
                biased(0)
                after(dve, ec_ready, c)
                vb = valid_c.rearrange("p b n -> p (b n)")
                for e in range(2):
                    pe_ = pc[:, e, :, :].rearrange("p b n -> p (b n)")
                    link(v.tensor_tensor(pe_, pe_, vb, ALU.mult))
                dve.sem_inc(pc_ready.sem, 1)
                link(v.tensor_reduce(cs, pc3, AXX, ALU.add))
                link(v.tensor_scalar(cs, cs, 1e-30, None, ALU.max))
                link(v.reciprocal(cs, cs))
                link(v.tensor_tensor(csum[:], csum[:], gst[:, :, :, 0].rearrange("p b e -> p e b"), ALU.mult))
                for i in range(UNITS):
                    if i + 1 < UNITS:
                        biased(i + 1)
                    combine(i)
                link(v.tensor_scalar(slope[:], slope[:], 0.5, None, ALU.mult))
                link.reset()

            def final_norm(b):
                v.scalar_tensor_tensor(X[:, b, :], X[:, b, :], final_rstd[:, b:b + 1], wfin, ALU.mult, ALU.mult
                                       ).then_inc(og_final.sem, 1)

            def residual(layer, tb, mark):
                dve.wait_ge(wo_done.sem, wo_done.at(layer * TB + tb))
                p = OUT_BANKS[tb]
                link(v.tensor_tensor(X[:, tb, :].rearrange("p (a b) -> p a b", a=2),
                                     X[:, tb, :].rearrange("p (a b) -> p a b", a=2), PS[:, p:p + 2, :], ALU.add))
                dve.sem_inc(wo_out.sem, 1)
                link(v.tensor_tensor_reduce(out=XN, in0=X[:, tb, :], in1=X[:, tb, :], scale=1.0,
                                            scalar=0.0, op0=ALU.mult, op1=ALU.add, accum_out=stat[:, tb:tb + 1]))
                if mark:
                    dve.sem_inc(ss_ready.sem, 1)

            def peer(layer):
                U0, S0, B0 = layer * LAYER_UNITS, layer * LAYER_SLOTS, layer * (TB + 1)
                Q0, R0 = layer * (LAYER_UNITS + 2), layer * (LAYER_UNITS + 1)
                G0 = S0 // GRP
                residual(layer, 0, True)
                dve.wait_ge(ffn_in, 16 * (layer + 1))
                dve.wait_ge(rs_ready.sem, rs_ready.at(3 * layer))

                def prologue(b):
                    link(v.tensor_copy(rsb[:], rstd[:, ds(b, 1)]))
                    link(v.scalar_tensor_tensor(XN2, X[:, ds(b, 1), :].rearrange("p a d -> p (a d)"), rsb[:], wrow,
                                                ALU.mult, ALU.mult))
                    dve.sem_inc(pxn_ready.sem, 1)

                def top16(vals, idx, src, spare):
                    link(v.max(vals[:, 0:8], src))
                    link(v.max_index(idx[:, 0:8], vals[:, 0:8], src))
                    link(v.match_replace(spare, vals[:, 0:8], src, -3e38))
                    link(v.max(vals[:, 8:16], spare))
                    link(v.max_index(idx[:, 8:16], vals[:, 8:16], spare))

                def scores_in(r):
                    after(dve, rs_done, r)
                    link(v.tensor_copy(s1, v3(PS[:, 6, 0:256], 2)))
                    dve.sem_inc(rs_out.sem, 1)
                    top16(vtop[:, 0, :], itop[:, 0, :], s1[:, 0, :], s2[:, 0, :])

                def second_half():
                    top16(vtop[:, 1, :], itop[:, 1, :], s1[:, 1, :], s2[:, 1, :])
                    link(v.tensor_copy(itopf, itop))

                def candidates(r):
                    link(v.tensor_tensor(v3(cand, TOPK), bc(vtop[:, 0, :], TOPK), bmid(vtop[:, 1, :], TOPK), ALU.add))
                    top16(best, bpos, cand, cand2)
                    link(v.tensor_scalar(gstat[:, 0:1], best[:, 0:1], -1.0, None, ALU.mult))
                    dve.sem_inc(gexp_in.sem, 1)

                def chosen(e):
                    link(v.tensor_scalar(bij[:, 0, :], bpos, 4, None, ALU.logical_shift_right))
                    link(v.tensor_scalar(bij[:, 1, :], bpos, 15, None, ALU.bitwise_and))
                    link(v.tensor_copy(bijf, bij))
                    for p in range(2):
                        oh = oneh[:, p, :, :]
                        link(v.tensor_tensor(oh, bc(bijf[:, p, :], TOPK), bmid(iota16[:], TOPK), ALU.is_equal))
                        link(v.tensor_tensor(oh, oh, bmid(itopf[:, p, :], TOPK), ALU.mult))
                        link(v.tensor_reduce(esel[:, p, :], oh, AXX, ALU.add))
                    link(v.scalar_tensor_tensor(experts[:, e * TOPK:(e + 1) * TOPK], esel[:, 0, :], float(NKEYS),
                                                esel[:, 1, :], ALU.mult, ALU.add))

                def gates_of(e, r):
                    after(dve, gexp_out, r)
                    link(v.reciprocal(gstat[:, 2:3], gstat[:, 1:2]))
                    link(v.tensor_scalar(gate[:, e, :], gexp, gstat[:, 2:3], None, ALU.mult))
                    dve.sem_inc(routed.sem, 1)

                link(v.tensor_copy(rsb[:], rstd[:, 0:1]))
                link(v.scalar_tensor_tensor(XN2, X[:, 0, :], rsb[:], wrow, ALU.mult, ALU.mult))
                dve.sem_inc(pxn_ready.sem, 1)
                residual(layer, 1, False)
                scores_in(Q0)
                second_half()
                candidates(R0)
                chosen(0)
                gates_of(0, R0)
                residual(layer, 2, False)
                residual(layer, 3, True)
                link.reset()

                def dot_products(u, e, grp):
                    for k in range(grp * GRP, grp * GRP + GRP):
                        buf = k % NBUF
                        rounds = TOPK // NBUF
                        reached(dve, gathered[buf],
                                u * (16 * rounds) + 16 * (rounds * (U0 + e) + k // NBUF + 1))
                        q = e * TOPK + k
                        i = v.tensor_tensor_reduce(out=gath[:, buf, 0:D_MODEL], in0=gath[:, buf, 0:D_MODEL],
                                                   in1=XN, scale=1.0, scalar=0.0, op0=ALU.mult, op1=ALU.add,
                                                   accum_out=dots[:, q:q + 1])
                    link(i)
                    dve.sem_inc(dots_ready.sem, 1)

                def pair(b, u, first, last):
                    for e in range(2):
                        r, rq = u + (e + 1 + R0), u + (e + 1 + Q0)
                        if last and e == 1:
                            dve.wait_ge(rs_ready.sem, rs_ready.at(1 + 3 * layer))
                            prologue(b + 1)
                        for grp in range(TOPK // GRP):
                            gi = u * (TOPK // GRP) + (e * (TOPK // GRP) + grp + G0)
                            if not (first and e == 0 and grp == 0):
                                dot_products(u, e, grp)
                            after(dve, gelu_ready, gi)
                            q0 = e * TOPK + grp * GRP
                            v.tensor_tensor(wts[:, q0:q0 + GRP], gact[:, q0:q0 + GRP],
                                            gate[:, e, grp * GRP:grp * GRP + GRP], ALU.mult).then_inc(w_ready.sem, 1)
                            if grp == 0:
                                scores_in(rq)
                                second_half()
                            if grp == 1:
                                candidates(r)
                                chosen(1 - e)
                                gates_of(1 - e, r)
                        link.reset()

                def one_block(b, final):
                    pair(b, b * P_HEADS, True, False)
                    with dve.Fori(1, P_HEADS // 2 - 1) as hp:
                        pair(b, b * P_HEADS + hp * 2, False, False)
                    pair(b, b * P_HEADS + (P_HEADS - 2), False, True)
                    if not final:
                        link(v.tensor_copy(XN, XN2))
                        dot_products(b * P_HEADS + P_HEADS, 0, 0)
                    if final and layer == DEPTH - 1:
                        dve.wait_ge(fin_in, 16)
                        dve.wait_ge(rs_ready.sem, rs_ready.at(5))
                        for done in range(TB - 1):
                            final_norm(done)
                    after(dve, acc_done, b + layer * TB)
                    xb = X[:, ds(b, 1), :].rearrange("p a (c d) -> p (a c) d", c=2)
                    link(v.tensor_tensor(v3(XN2, 2), xb, PS[:, 0:2, :], ALU.add))
                    dve.sem_inc(acc_out.sem, 1)
                    link(v.tensor_copy(xb, v3(XN2, 2)))
                    link(v.tensor_tensor_reduce(out=XN2, in0=XN2, in1=XN2, scale=1.0, scalar=0.0, op0=ALU.mult,
                                                op1=ALU.add, accum_out=rsb[:]))
                    link(v.tensor_copy(stat[:, ds(b, 1)], rsb[:]))
                    link.reset()

                link(v.tensor_copy(XN, XN2))
                dot_products(0, 0, 0)
                link.reset()
                with dve.Fori(0, TB - 1) as b:
                    one_block(b, False)
                dve.sem_inc(ss_ready.sem, 1)
                one_block(TB - 1, True)
                dve.sem_inc(ss_ready.sem, 1)
                dve.wait_ge(rs_done.sem, rs_done.at(Q0 + LAYER_UNITS + 1))
                dve.sem_inc(rs_out.sem, 1)

            peer(0)

            dve.wait_ge(rs_ready.sem, rs_ready.at(2))
            normed_transposed(1)
            link(v.memset(scan_keep[:], 1.0))
            link(v.memset(v3(scan_keep[:], TB)[:, :, 0:1], 0.0))
            link(v.memset(attn, 0.0))
            link(v.memset(qE, 0.0))
            link(v.memset(kE, 0.0))
            dve.wait_ge(lf_ready.sem, lf_ready.at(0))
            dve.wait_ge(lb_in, 16)
            link(v.tensor_scalar(lb[:, 1, :], lb[:, 0, :], -1.0, 1.0, ALU.mult, ALU.add))
            link.reset()
            with dve.Fori(0, C_HEADS // 2) as hp:
                for e in range(2):
                    h = hp * 2 + e
                    for j in range(2):
                        link(v.tensor_copy(lbst[:, j, 0:1], lb[:, j, ds(h, 1)]))
                    after(dve, sig_ready, h)
                    link(v.tensor_scalar(fg, sigm, lbst[:, 1, 0:1], lbst[:, 0, 0:1], ALU.mult, ALU.add))
                    link(v.tensor_scalar(kk, fg, -1.0, 1.0, ALU.mult, ALU.add))
                    link(v.tensor_scalar(fg, fg, 2.0 ** -63, None, ALU.max))
                    dve.sem_inc(fg_ready.sem, 1)
                    link(v.tensor_tensor(qs, PS[:, 0, :], dE[:, 0, :], ALU.mult))
                    dve.sem_inc(qk_ready.sem, 1)
                    after(dve, lf_ready, h + 1)
                    link(v.tensor_tensor_scan(bb, scan_keep[:], bb, 0.0, ALU.mult, ALU.add))
                    halves = "p (b h l) -> p b h l"

                    def distance(lev):
                        n = 1 << lev
                        b_ = bb.rearrange(halves, h=2, l=n)
                        d_ = dE[:, lev % 2, :].rearrange(halves, h=2, l=n)
                        ref = b_[:, :, 0, n - 1:n].broadcast_to([P, SEQ // (2 * n), n])
                        if lev >= 2:
                            after(dve, ke_ready, h * LEVELS + (lev - 2))
                            after(dve, qe_ready, h * LEVELS + (lev - 2))
                        link(v.tensor_tensor(d_[:, :, 0, :], ref, b_[:, :, 0, :], ALU.subtract))
                        v.tensor_tensor(d_[:, :, 1, :], b_[:, :, 1, :], ref, ALU.subtract).then_inc(dd_ready.sem, 1)

                    def evacuate(lev):
                        after(dve, lv_done, h * (LEVELS + 1) + lev)
                        link(v.copy_predicated(v3(attn, 4), bmid(level_mask[:, lev, :], 4),
                                               v3(PS[:, 4 + lev % 2, :], 4)))
                        dve.sem_inc(lv_out.sem, 1)

                    distance(0)
                    gi = PS[:, 2:4, :].rearrange("p a (b c) -> p (a b) c", b=2)
                    after(dve, i_out, h)
                    link(v.tensor_tensor(v3(gs, 4), gi[:, :, P:2 * P], v3(dE[:, 1, :], 4), ALU.mult))
                    dve.sem_inc(ig_free.sem, 1)
                    link(v.tensor_tensor(v3(gs, 4), v3(gs, 4), bmid(hgw[:, ds(h * P, P)], 4), ALU.mult))
                    for lev in range(LEVELS):
                        n = 1 << lev
                        if lev + 1 < LEVELS:
                            distance(lev + 1)
                        after(dve, e_ready, h * LEVELS + lev)
                        if lev >= 2:
                            after(dve, lv_done, h * (LEVELS + 1) + (lev - 2))
                        v.tensor_tensor(qE[:, lev % 2, :].rearrange(halves, h=2, l=n)[:, :, 1, :],
                                        qs.rearrange(halves, h=2, l=n)[:, :, 1, :],
                                        dE[:, lev % 2, :].rearrange(halves, h=2, l=n)[:, :, 1, :], ALU.mult
                                        ).then_inc(qe_ready.sem, 1)
                        if lev:
                            evacuate(lev - 1)
                    link(v.tensor_tensor(v3(kd, 4), bc(v3(bb, 4)[:, :, P - 1], P), v3(bb, 4), ALU.subtract))
                    dve.sem_inc(kds_ready.sem, 1)
                    evacuate(LEVELS - 1)
                    evacuate(LEVELS)
                    after(dve, ebe_ready, h)
                    link(v.tensor_tensor(kd, kk, kd, ALU.mult))
                    link(v.tensor_tensor(qd, qs, eb, ALU.mult))
                    dve.sem_inc(kd_ready.sem, 1)
                    after(dve, kv_done, h)
                    link(v.tensor_copy(Sst[:, 0, :], PS[:, 7, 0:P]))
                    for b in (1, 2):
                        link(v.scalar_tensor_tensor(Sst[:, b, :], Sst[:, b - 1, :], v3(eb, 4)[:, b, P - 1:P],
                                                    PS[:, 7, b * P:(b + 1) * P], ALU.mult, ALU.add))
                    dve.sem_inc(s_ready.sem, 1)
                    after(dve, osq_ready, h)
                    link(v.tensor_reduce(mean[:], v3(eb, 4), AXX, ALU.add))
                    dve.sem_inc(oss_ready.sem, 1)
                    link(v.tensor_tensor(v3(ob, 4), v3(PS[:, 6, :], 4), v3(gs, 4), ALU.mult))
                    after(dve, ors_ready, h)
                    v.tensor_tensor(v3(ob, 4), v3(ob, 4), bc(rstd[:, 4:8], P), ALU.mult).then_inc(og_ready.sem, 1)
                    after(dve, ogT_done, h)
                    link.reset()
            peer(1)
            dve.wait_ge(rs_ready.sem, rs_ready.at(6))
            final_norm(TB - 1)

        @block.tensor
        def _(pe):
            t = nc.tensor
            pe.wait_ge(primed, 1)

            def transposes(layer):
                for tb in range(TB):
                    n = layer * TB + tb
                    pe.wait_ge(xn_ready.sem, xn_ready.at(n))
                    pe.wait_ge(hT_ready.sem, hT_ready.at(n - 1))
                    for c in range(KC):
                        i = t.transpose(PS[:, c // 4, (c % 4) * P:(c % 4 + 1) * P], xnS[:, tb % 2, c * P:(c + 1) * P],
                                        ident)
                    i.then_inc(xT_done.sem, 1)

            pe.wait_ge(half_set, 1)
            transposes(0)
            pe.wait_ge(hT_ready.sem, hT_ready.at(TB - 1))
            pe.wait_ge(fm_in, 16)
            for ch in range(8):
                pe.wait_ge(fm_out.sem, fm_out.at(ch - 2))
                for c in range(KC):
                    i = t.matmul(PS[:, 6 + ch % 2, :], We[:, c, TM_ALL + ch * P:TM_ALL + (ch + 1) * P], hT[:, c, :],
                                 start=c == 0, stop=c == KC - 1)
                i.then_inc(fm_done.sem, 1)
            pe.wait_ge(consts, 1)
            pe.wait_ge(tm_in, 16)

            def token_major(tb, j):
                if j == 1:
                    pe.wait_ge(uv_out.sem, uv_out.at(tb - 2))
                    pe.wait_ge(vsw_out.sem, vsw_out.at(tb - 2))
                c0, c1 = ((0, 512), (512, 1024), (1024, TM_ALL))[j]
                for c in range(KC):
                    i = t.matmul(PS[:, 3 * (tb % 2) + j, 0:c1 - c0], hT[:, c, tb * P:(tb + 1) * P], We[:, c, c0:c1],
                                 start=c == 0, stop=c == KC - 1)
                if j != 2:
                    i.then_inc((tm_done if j == 0 else tv_done).sem, 1)

            pe.wait_ge(fm_out.sem, fm_out.at(7))
            for j in (1, 2, 0):
                token_major(0, j)
            pe.wait_ge(w1_in, 32)
            pe.wait_ge(dup_in, 16 * 8)
            J = CMP_BLOCK // 2
            for kv in range(2):
                for j in range(J):
                    i = t.matmul(PS[:, 6, kv:kv + 1], w1[:, kv, j * P:(j + 1) * P], pos_sb[:, j:j + 1],
                                 start=j == 0, stop=j == J - 1)
            i.then_inc(posb_done.sem, 1)
            for kv, src in ((0, kcd), (1, vcd)):
                for j in range(J):
                    sv = src[:, :, 2 * j:2 * j + CMP_STRIDE * (N_CMP - 1) + 1:CMP_STRIDE]
                    i = t.matmul(PS[:, 7, kv * 64:kv * 64 + 2 * N_CMP].rearrange("p (a b) -> p a b", a=2),
                                 w1[:, kv, j * P:(j + 1) * P], sv, start=j == 0, stop=j == J - 1)
            i.then_inc(hid_done.sem, 1)
            pe.wait_ge(hid_out.sem, hid_out.at(0))
            for g_ in range(2):
                t.matmul(PS[g_ * HD:(g_ + 1) * HD, 3, 0:N_CMP], w2s[:, 0, :], hid[:, 0, g_ * N_CMP:(g_ + 1) * N_CMP],
                         start=True, stop=True)
                i = t.matmul(PS[0:N_CMP, 4, g_ * HD:(g_ + 1) * HD], hid[:, 1, g_ * N_CMP:(g_ + 1) * N_CMP],
                             w2s[:, 1, :], start=True, stop=True)
            i.then_inc(cmp_done.sem, 1)
            pe.wait_ge(cmp_out.sem, cmp_out.at(0))
            for tb in range(TB):
                if tb + 1 < TB:
                    token_major(tb + 1, 1)
                pe.wait_ge(ln_done.sem, ln_done.at(tb))
                pe.wait_ge(a_ready.sem, a_ready.at(tb - 1))
                for gr in range(A_GROUPS):
                    i = t.matmul(PS[:, 6, gr * P:(gr + 1) * P], ws_sb[:, gr, :], gvn[:, gr * P:(gr + 1) * P],
                                 start=True, stop=True)
                i.then_inc(mix_done.sem, 1)
                if tb + 1 < TB:
                    token_major(tb + 1, 2)
                pe.wait_ge(a_ready.sem, a_ready.at(tb))
                pe.wait_ge(aT_out.sem, aT_out.at(tb - 1))
                for gr in range(A_GROUPS):
                    i = t.transpose(PS[:, 7, gr * P:(gr + 1) * P], gsq[:, gr * P:(gr + 1) * P], ident)
                i.then_inc(aT_done.sem, 1)
                if tb + 1 < TB:
                    token_major(tb + 1, 0)
            with pe.Fori(0, 4) as c:
                after(pe, q_staged, c)

                def scores(i):
                    qb, e = unit(i)
                    par, nk = i % 2, (qb + 1) * P
                    after(pe, z_ready, c * (UNITS + 1) + (i - 1) if i >= 2 else c * (UNITS + 1) + (i - 2))
                    r = slice(e * HD, (e + 1) * HD)
                    for br in range(2):
                        k_ = t.matmul(PS[:, 2 * par + br, 0:nk], qst[r, qb * P:(qb + 1) * P], kT[r, br, 0:nk],
                                      start=True, stop=True)
                    k_.then_inc(sc_done.sem, 1)

                after(pe, oT_out, c - 1)
                after(pe, o_ready, c * UNITS - 1)
                for i in range(UNITS):
                    qb, e = unit(i)
                    r = slice(e * HD, (e + 1) * HD)
                    k_ = t.matmul(PS[:, 4 + e, qb * N_CMP:(qb + 1) * N_CMP], qst[r, qb * P:(qb + 1) * P],
                                  kcmp[r, :], start=True, stop=True)
                k_.then_inc(cs_done.sem, 1)
                scores(0)
                scores(1)
                after(pe, pc_ready, c)
                pe.wait_ge(aT_out.sem, aT_out.at(TB - 1))
                for i in range(UNITS):
                    qb, e = unit(i)
                    k_ = t.transpose(PS[0:N_CMP, 6 + e, qb * P:(qb + 1) * P], pc[:, e, qb, :], ident)
                k_.then_inc(pcT_done.sem, 1)
                after(pe, pcT_out, c)
                for i in range(UNITS):
                    qb, e = unit(i)
                    par = i % 2
                    after(pe, p_ready, c * UNITS + i)
                    after(pe, pT_out, c * UNITS + (i - 1))
                    for br in range(2):
                        for kt in range(qb + 1):
                            k_ = t.transpose(PS[:, 4 + br, kt * P:(kt + 1) * P],
                                             ps_[:, par, br * SEQ + kt * P:br * SEQ + (kt + 1) * P], ident)
                    k_.then_inc(pT_done.sem, 1)
                    if i + 2 < UNITS:
                        scores(i + 2)
                    after(pe, pT_out, c * UNITS + i)
                    after(pe, o_ready, c * UNITS + (i - 2))
                    for br in range(2):
                        for kt in range(qb + 1):
                            t.matmul(PS[:, 6 + par, br * HD:(br + 1) * HD],
                                     pTs[:, par, br * SEQ + kt * P:br * SEQ + (kt + 1) * P],
                                     vsw[:, kt, br, e * HD:(e + 1) * HD], start=kt == 0, stop=kt == qb)
                    t.matmul(PS[:, 6 + par, 2 * HD:3 * HD], pcT[:, e, qb, :], vcmp[:, e * HD:(e + 1) * HD],
                             start=True, stop=True).then_inc(pv_done.sem, 1)
                after(pe, o_ready, c * UNITS + (UNITS - 1))
                for qb in range(TB):
                    i = t.transpose(PS[:, 4, qb * P:(qb + 1) * P], ot[:, qb * P:(qb + 1) * P], ident)
                i.then_inc(oT_done.sem, 1)

            def project_out(layer, w, tb, js):
                for j in js:
                    for c in range(KC):
                        i = t.matmul(PS[:, OUT_BANKS[tb] + j, :], mixT[:, c, tb * P:(tb + 1) * P],
                                     w[:, c, j * 512:(j + 1) * 512], start=c == 0, stop=c == KC - 1)
                if 1 in js:
                    i.then_inc(wo_done.sem, 1)

            def peer(layer):
                U0, S0, B0 = layer * LAYER_UNITS, layer * LAYER_SLOTS, layer * (TB + 1)
                Q0, R0 = layer * (LAYER_UNITS + 2), layer * (LAYER_UNITS + 1)

                def block_transposes(n):
                    after(pe, pxn_ready, n)
                    for c in range(KC):
                        i = t.transpose(PS[:, 2 + c // 4, (c % 4) * P:(c % 4 + 1) * P], XN2[:, c * P:(c + 1) * P],
                                        ident)
                    i.then_inc(pxT_done.sem, 1)

                def route(r, hcol):
                    for c in range(KC):
                        i = t.matmul(PS[:, 4, 0:256], hTb[:, c, :], wq[:, c, ds(hcol * 256, 256)],
                                     start=c == 0, stop=c == KC - 1)
                    i.then_inc(rq_done.sem, 1)
                    after(pe, rq_out, r)
                    for p in range(2):
                        i = t.transpose(PS[:, 5, p * P:(p + 1) * P], q_sb[:, p, :], ident)
                    i.then_inc(rqT_done.sem, 1)
                    after(pe, rqT_out, r)
                    after(pe, rs_out, r - 1)
                    for p in range(2):
                        i = t.matmul(PS[:, 6, p * P:(p + 1) * P], qT_sb[:, p, :],
                                     keysT[:, ds(hcol * 2 + p, 1), :].rearrange("p a b -> p (a b)"),
                                     start=True, stop=True)
                    i.then_inc(rs_done.sem, 1)

                def zero_products(start, stop):
                    for j in range(2):
                        i = t.matmul(PS[:, j, :], ident_z[0:1, P:2 * P], alibi[0:1, :], start=start, stop=stop)
                    return i

                def pair(b, u, hcol, first, last):
                    for e in range(2):
                        if first and e == 0:
                            after(pe, acc_out, b + (layer * TB - 1))
                            zero_products(True, False)
                        elif last and e == 1:
                            block_transposes(b + (B0 + 1))
                            after(pe, pxT_out, b + (B0 + 1))
                            route(u + (e + 1 + Q0), 0)
                        else:
                            route(u + (e + 1 + Q0), hcol + (e + 1))
                        for k in range(TOPK):
                            if last and e == 1 and k == 2 * GRP:
                                route(u + (3 + Q0), 1)
                            after(pe, diag_ready, u * TOPK + (e * TOPK + k + S0))
                            for j in range(2):
                                i = t.matmul(PS[:, j, :], diag[:, k % NBUF, :],
                                             gath[:, k % NBUF, D_MODEL + j * 512:D_MODEL + (j + 1) * 512],
                                             start=False, stop=False)
                            i.then_inc(slot_done.sem, 1)

                w = (w_out_sb, wo_odd)[layer]
                pe.wait_ge(wout_in, 16 * (layer + 1))
                if layer == 0:
                    pe.wait_ge(oT_out.sem, oT_out.at(3))
                else:
                    pe.wait_ge(ogT_out.sem, ogT_out.at(C_HEADS - 1))
                project_out(layer, w, 0, (0, 1))
                project_out(layer, w, 1, (0, 1))
                block_transposes(B0)
                pe.wait_ge(wo_out.sem, wo_out.at(layer * TB))
                project_out(layer, w, 2, (0,))
                pe.wait_ge(wq_in, 32 * (layer + 1))
                pe.wait_ge(pxT_out.sem, pxT_out.at(B0))
                pe.wait_ge(wo_out.sem, wo_out.at(layer * TB + 1))
                route(Q0, 0)
                project_out(layer, w, 2, (1,))
                project_out(layer, w, 3, (0, 1))
                route(Q0 + 1, 1)
                pe.wait_ge(wo_out.sem, wo_out.at(layer * TB + 3))
                with pe.Fori(0, TB) as b:
                    pair(b, b * P_HEADS, 0, True, False)
                    with pe.Fori(1, P_HEADS // 2 - 1) as hp:
                        pair(b, b * P_HEADS + hp * 2, hp * 2, False, False)
                    pair(b, b * P_HEADS + (P_HEADS - 2), P_HEADS - 2, False, True)
                    zero_products(False, True).then_inc(acc_done.sem, 1)

            peer(0)

            pe.wait_ge(acc_out.sem, acc_out.at(TB - 1))
            transposes(1)
            pe.wait_ge(hT_ready.sem, hT_ready.at(2 * TB - 1))

            def projections(W, part, parts):
                todo = [(j, None, c) for c in range(KC) for j in range(2)]
                todo += [(None, tb, c) for tb in range(TB) for c in range(KC)]
                cost = [2 if tb is None else 1 for _, tb, _ in todo]
                last, done = None, 0
                for (j, tb, c), w_ in zip(todo, cost):
                    mine = done * parts // sum(cost) == part
                    done += w_
                    if not mine:
                        continue
                    if tb is None:
                        last = t.matmul(PS[:, j, :], W[:, c, j * P:(j + 1) * P], hT[:, c, :],
                                        start=c == 0, stop=c == KC - 1)
                    else:
                        last = t.matmul(PS[:, 2 + tb // 2, (tb % 2) * 256:(tb % 2 + 1) * 256],
                                        hT[:, c, tb * P:(tb + 1) * P], W[:, c, 256:512],
                                        start=c == 0, stop=c == KC - 1)
                if part == parts - 1:
                    last.then_inc(pr_done.sem, 1)

            FIRST = 3
            SHARES = FIRST + LEVELS + 1 + 4

            def head_pair(hp, final):
                for e in range(2):
                    h = hp * 2 + e
                    W = slab[:, 1 - e, :].rearrange("p (c n) -> p c n", c=KC)
                    more = not (final and e == 1)

                    def share(n):
                        if more:
                            if n == SHARES // 2:
                                after(pe, ig_free, h)
                            projections(W, n, SHARES)

                    if more:
                        reached(pe, slab_in[1 - e], hp * 16 + 16 * (1 + e))
                        after(pe, qk_ready, h)
                    for n in range(FIRST):
                        share(n)
                    for lev in range(LEVELS + 1):
                        after(pe, lv_out, h * (LEVELS + 1) + (lev - 2))
                        if lev < LEVELS:
                            after(pe, qe_ready, h * LEVELS + lev)
                            after(pe, ke_ready, h * LEVELS + lev)
                            q_, k_ = qE[:, lev % 2, :], kE[:, lev % 2, :]
                        else:
                            q_, k_ = qs, kk
                        for tb in range(TB):
                            i = t.matmul(PS[:, 4 + lev % 2, tb * P:(tb + 1) * P], k_[:, tb * P:(tb + 1) * P],
                                         q_[:, tb * P:(tb + 1) * P], start=True, stop=True)
                        i.then_inc(lv_done.sem, 1)
                        share(FIRST + lev)
                    after(pe, kd_ready, h)
                    after(pe, og_ready, h - 1)
                    for tb in range(TB):
                        i = t.transpose(PS[:, 6, tb * P:(tb + 1) * P], kd[:, tb * P:(tb + 1) * P], ident)
                    i.then_inc(kdT_done.sem, 1)
                    share(FIRST + LEVELS + 1)
                    after(pe, kdT_out, h)
                    after(pe, ogT_out, h - 1)
                    for tb in range(TB):
                        i = t.matmul(PS[:, 7, tb * P:(tb + 1) * P], kdT[:, tb * P:(tb + 1) * P],
                                     iS[:, tb * P:(tb + 1) * P], start=True, stop=True)
                    i.then_inc(kv_done.sem, 1)
                    share(FIRST + LEVELS + 2)
                    share(FIRST + LEVELS + 3)
                    after(pe, s_ready, h)
                    after(pe, lv_out, h * (LEVELS + 1) + LEVELS)
                    for tb in range(TB):
                        o = PS[:, 6, tb * P:(tb + 1) * P]
                        if tb:
                            t.matmul(o, qd[:, tb * P:(tb + 1) * P], Sst[:, tb - 1, :], start=True, stop=False)
                        i = t.matmul(o, attn[:, tb * P:(tb + 1) * P], iS[:, tb * P:(tb + 1) * P],
                                     start=tb == 0, stop=True)
                    i.then_inc(oi_done.sem, 1)
                    share(FIRST + LEVELS + 4)
                    after(pe, og_ready, h)
                    for tb in range(TB):
                        i = t.transpose(PS[:, 7, tb * P:(tb + 1) * P], ob[:, tb * P:(tb + 1) * P], ident)
                    i.then_inc(ogT_done.sem, 1)

            reached(pe, slab_in[0], 16)
            projections(slab[:, 0, :].rearrange("p (c n) -> p c n", c=KC), 0, 1)
            with pe.Fori(0, C_HEADS // 2 - 1) as hp:
                head_pair(hp, False)
            head_pair(C_HEADS // 2 - 1, True)
            peer(1)


def kernel(**inputs):
    import numpy as np
    import concourse.bacc as bacc
    from concourse import mybir as mb
    from concourse.bass_utils import run_bass_kernel_spmd as run

    def arr(name):
        return np.asarray(inputs[name])

    def chunks(w):
        return w.reshape(-1, 128, w.shape[-1]).transpose(1, 0, 2)

    we = arr("even_w_in")[0]
    q = we[:, 1024:1536].reshape(1024, 8, 64)
    qpairs = np.stack([q[:, 0:4], q[:, 4:8]], axis=2).reshape(1024, 512)
    kc, vc, ks, vs, kw, vw = (we[:, 1536 + 128 * i:1664 + 128 * i] for i in range(6))
    we = np.concatenate([we[:, 0:1024], vs, vw, we[:, 2304:2328], qpairs, kc, vc, ks, kw], axis=1)

    wo = arr("even_w_out")[0]
    heads = wo[512:].reshape(8, 64, 1024)
    wo = np.concatenate([wo[:512], np.stack([heads[0:4], heads[4:8]], axis=1).reshape(512, 1024)], axis=0)

    def two_positions(w):
        return w.reshape(16, 2, 64, -1).transpose(1, 2, 0, 3).reshape(128, 16, -1)

    odd = arr("odd_w_in")[0].reshape(8, 128, 4, 8, 128)
    odd = odd.transpose(3, 1, 0, 2, 4).reshape(8, 128, 4096)
    data = {
        "x": arr("x")[0],
        "wcol_mix": arr("norm_mix").reshape(2, 8, 128).transpose(2, 0, 1),
        "w_ffn": arr("norm_ffn"),
        "w_fin": arr("final_norm").reshape(1, 1024),
        "w_even": chunks(we),
        "ln_w": arr("gmlp_ln_w"),
        "ws_t": arr("gmlp_w_s")[0].transpose(2, 0, 1),
        "b_s": arr("gmlp_b_s")[0].T,
        "pos": two_positions(arr("nsa_cmp_pos")[0].reshape(2048, 1)).reshape(128, 16),
        "ck1": two_positions(arr("nsa_ck_w1")[0]).reshape(128, 2048),
        "ck2": arr("nsa_ck_w2")[0],
        "cv1": two_positions(arr("nsa_cv_w1")[0]).reshape(128, 2048),
        "cv2": arr("nsa_cv_w2")[0],
        "w_out_e": chunks(wo),
        "w_odd": odd,
        "lbs": arr("hgrn_lower_bounds").reshape(2, 8, 128).transpose(2, 0, 1),
        "hg_w": arr("hgrn_norm_w"),
        "w_out_o": chunks(arr("odd_w_out")[0]),
        "w_q": arr("peer_w_q").reshape(2, 8, 128, 2048).transpose(0, 2, 1, 3),
        "keys": arr("peer_keys").reshape(2, 16, 128, 128).transpose(0, 3, 1, 2),
    }
    for layer in range(2):
        data[f"uv{layer}"] = np.concatenate([arr("peer_u")[layer], arr("peer_v")[layer]], axis=1)

    nc = bacc.Bacc("TRN2", target_bir_lowering=False, num_devices=1)
    arrays, args = {}, {}
    for name, a in data.items():
        a = np.ascontiguousarray(a)
        arrays[f"in_{name}_dram"] = a
        args[name] = nc.dram_tensor(f"in_{name}_dram", a.shape, mb.dt.from_np(a.dtype), kind="ExternalInput").ap()
    args["out"] = nc.dram_tensor("out_0_dram", (512, 1024), mb.dt.float32, kind="ExternalOutput").ap()
    args["uv"] = [args.pop("uv0"), args.pop("uv1")]
    build(nc, **args)
    r = run(nc, [arrays], core_ids=[0])
    return r.results[0]["out_0_dram"].reshape(1, 512, 1024)
```
